# Optimizing a Trainium2 kernel written in Bass

```python
import math
import jax, jax.numpy as jnp
from jax import lax
import numpy as np

D_MODEL = 1024
BATCH = 1
SEQ = 256
DEPTH = 2

PLE_DIM = 256
Q_BLOCK = 128
RNN_WIDTH = 512
RNN_BLOCKS = 8
CONV_WIDTH = 4
LRU_C = 8.0
DSA_HEADS = 8
DSA_HEAD_DIM = 64
IDX_HEADS = 4
IDX_DIM = 64
DSA_TOPK_MAX = 256
MLA_HEADS = 16
MLA_Q_LORA = 512
MLA_KV_LORA = 256
MLA_NOPE = 64
MLA_ROPE = 32
MLA_V = 64
ROPE_BASE = 10000.0
D_FF = 4 * D_MODEL
DN_ALPHA = (2 * DEPTH) ** 0.25
DN_BETA = (8 * DEPTH) ** -0.25
LN_EPS = 1e-5
RMS_EPS = 1e-6
N_EVEN = (DEPTH + 1) // 2
N_ODD = DEPTH // 2
EVEN_SPLITS = (RNN_WIDTH, RNN_WIDTH, DSA_HEADS * DSA_HEAD_DIM, DSA_HEAD_DIM, DSA_HEAD_DIM,
               IDX_HEADS * IDX_DIM, IDX_DIM, IDX_HEADS)
EVEN_IN = sum(EVEN_SPLITS)
EVEN_MIX = RNN_WIDTH + DSA_HEADS * DSA_HEAD_DIM
MLA_DOWN = MLA_Q_LORA + MLA_KV_LORA + MLA_ROPE
MLA_MIX = MLA_HEADS * MLA_V


def layer_norm(x, g, b):
    xf = x.astype(jnp.float32)
    mu = jnp.mean(xf, axis=-1, keepdims=True)
    var = jnp.mean(jnp.square(xf - mu), axis=-1, keepdims=True)
    y = (xf - mu) * lax.rsqrt(var + LN_EPS) * g.astype(jnp.float32) + b.astype(jnp.float32)
    return y.astype(x.dtype)

def rms_norm(x, g):
    xf = x.astype(jnp.float32)
    y = xf * lax.rsqrt(jnp.mean(jnp.square(xf), axis=-1, keepdims=True) + RMS_EPS)
    return (y * g.astype(jnp.float32)).astype(x.dtype)

def causal_depthwise_conv(x, w, b):
    c = x.shape[-1]
    y = lax.conv_general_dilated(x, w[:, None, :], window_strides=(1,), padding=[(CONV_WIDTH - 1, 0)],
                                 dimension_numbers=("NWC", "WIO", "NWC"), feature_group_count=c)
    return y + b

def rg_lru(x, w_a, b_a, w_x, b_x, lam):
    bsz, s, c = x.shape
    xb = x.reshape(bsz, s, RNN_BLOCKS, c // RNN_BLOCKS)
    r = jax.nn.sigmoid(jnp.einsum("bsnc,ncd->bsnd", xb, w_a).reshape(bsz, s, c) + b_a)
    i = jax.nn.sigmoid(jnp.einsum("bsnc,ncd->bsnd", xb, w_x).reshape(bsz, s, c) + b_x)
    log_a = -LRU_C * r.astype(jnp.float32) * jax.nn.softplus(-lam.astype(jnp.float32))
    a = jnp.exp(log_a)
    u = jnp.sqrt(-jnp.expm1(2.0 * log_a)) * (i * x).astype(jnp.float32)

    def combine(left, right):
        a1, b1 = left
        a2, b2 = right
        return a1 * a2, a2 * b1 + b2

    _, h = lax.associative_scan(combine, (a, u), axis=1)
    return h.astype(x.dtype)

def alibi_slopes(n):
    return jnp.exp2(-8.0 * (jnp.arange(n, dtype=jnp.float32) + 1.0) / n)

def rope(x, cos, sin):
    half = x.shape[-1] // 2
    x1, x2 = x[..., :half], x[..., half:]
    return jnp.concatenate([x1 * cos - x2 * sin, x2 * cos + x1 * sin], axis=-1)

def to_blocks(a, nb):
    a = a.reshape((a.shape[0], nb, Q_BLOCK) + a.shape[2:])
    return jnp.moveaxis(a, 1, 0)

def from_blocks(o):
    o = jnp.moveaxis(o, 0, 1)
    return o.reshape((o.shape[0], o.shape[1] * o.shape[2]) + o.shape[3:])

def gather_rows(src, idx):
    return jax.vmap(lambda sb, ib: sb[ib])(src, idx)

def dsa_attention(q, k, v, iq, ik, iw):
    bsz, s = q.shape[:2]
    nb = s // Q_BLOCK
    topk = min(DSA_TOPK_MAX, s // 4)
    slopes = alibi_slopes(DSA_HEADS)
    key_pos = jnp.arange(s, dtype=jnp.int32)
    iw = iw.astype(jnp.float32) * (IDX_HEADS ** -0.5 * IDX_DIM ** -0.5)

    def block(args):
        qb, iqb, iwb, t0 = args
        qpos = t0 + jnp.arange(Q_BLOCK, dtype=jnp.int32)
        dots = jnp.einsum("bthd,bsd->bths", iqb, ik).astype(jnp.float32)
        isc = jnp.einsum("bths,bth->bts", jax.nn.relu(dots), iwb)
        causal = key_pos[None, :] <= qpos[:, None]
        isc = jnp.where(causal[None], isc, -jnp.inf)
        _, idx = lax.top_k(isc, topk)
        ksel = gather_rows(k, idx)
        vsel = gather_rows(v, idx)
        logits = jnp.einsum("bthd,btkd->bthk", qb, ksel).astype(jnp.float32) * (DSA_HEAD_DIM ** -0.5)
        dist = qpos[None, :, None] - idx
        logits = logits - slopes[None, None, :, None] * dist.astype(jnp.float32)[:, :, None, :]
        logits = jnp.where((dist >= 0)[:, :, None, :], logits, -jnp.inf)
        probs = jax.nn.softmax(logits, axis=-1).astype(v.dtype)
        return jnp.einsum("bthk,btkd->bthd", probs, vsel)

    starts = jnp.arange(nb, dtype=jnp.int32) * Q_BLOCK
    out = lax.map(block, (to_blocks(q, nb), to_blocks(iq, nb), to_blocks(iw, nb), starts))
    return from_blocks(out)

def mla_attention(q, k, v):
    bsz, s = q.shape[:2]
    nb = s // Q_BLOCK
    scale = q.shape[-1] ** -0.5
    key_pos = jnp.arange(s, dtype=jnp.int32)

    def block(args):
        qb, t0 = args
        qpos = t0 + jnp.arange(Q_BLOCK, dtype=jnp.int32)
        logits = jnp.einsum("bthd,bshd->bhts", qb, k).astype(jnp.float32) * scale
        causal = key_pos[None, :] <= qpos[:, None]
        logits = jnp.where(causal[None, None], logits, -jnp.inf)
        probs = jax.nn.softmax(logits, axis=-1).astype(v.dtype)
        return jnp.einsum("bhts,bshd->bthd", probs, v)

    starts = jnp.arange(nb, dtype=jnp.int32) * Q_BLOCK
    out = lax.map(block, (to_blocks(q, nb), starts))
    return from_blocks(out)

def hybrid_mixer(x, w_in, conv_w, conv_b, ga_w, ga_b, gx_w, gx_b, lam, w_out):
    bsz, s, _ = x.shape
    proj = x @ w_in
    split_points = np.cumsum(EVEN_SPLITS)[:-1].tolist()
    xr, yr, q, k, v, iq, ik, iw = jnp.split(proj, split_points, axis=-1)
    xr = causal_depthwise_conv(xr, conv_w, conv_b)
    rec = rg_lru(xr, ga_w, ga_b, gx_w, gx_b, lam) * jax.nn.gelu(yr)
    att = dsa_attention(q.reshape(bsz, s, DSA_HEADS, DSA_HEAD_DIM), k, v,
                        iq.reshape(bsz, s, IDX_HEADS, IDX_DIM), ik, iw)
    mixed = jnp.concatenate([rec, att.reshape(bsz, s, DSA_HEADS * DSA_HEAD_DIM)], axis=-1)
    return mixed @ w_out

def mla_mixer(x, w_down, q_norm, kv_norm, w_uq, w_ukv, w_out):
    bsz, s, _ = x.shape
    down = x @ w_down
    cq, ckv, kr = jnp.split(down, [MLA_Q_LORA, MLA_Q_LORA + MLA_KV_LORA], axis=-1)
    q = (rms_norm(cq, q_norm) @ w_uq).reshape(bsz, s, MLA_HEADS, MLA_NOPE + MLA_ROPE)
    kv = (rms_norm(ckv, kv_norm) @ w_ukv).reshape(bsz, s, MLA_HEADS, MLA_NOPE + MLA_V)
    q_nope, q_rope = q[..., :MLA_NOPE], q[..., MLA_NOPE:]
    k_nope, v = kv[..., :MLA_NOPE], kv[..., MLA_NOPE:]
    pos = jnp.arange(s, dtype=jnp.float32)
    freq = ROPE_BASE ** (-jnp.arange(0, MLA_ROPE, 2, dtype=jnp.float32) / MLA_ROPE)
    ang = pos[:, None] * freq[None, :]
    cos = jnp.cos(ang).astype(x.dtype)
    sin = jnp.sin(ang).astype(x.dtype)
    q_rope = rope(q_rope, cos[:, None, :], sin[:, None, :])
    k_rope = rope(kr, cos, sin)
    qf = jnp.concatenate([q_nope, q_rope], axis=-1)
    kf = jnp.concatenate([k_nope, jnp.broadcast_to(k_rope[:, :, None, :], (bsz, s, MLA_HEADS, MLA_ROPE))], axis=-1)
    o = mla_attention(qf, kf, v)
    return o.reshape(bsz, s, MLA_MIX) @ w_out

def first_inputs(seed: int = 0) -> dict:
    key = jax.random.key(seed)
    ks = jax.random.split(key, 32)

    def nrm(k, shape, scale):
        return jax.random.normal(k, shape, jnp.float32) * scale

    u = jax.random.uniform(ks[12], (N_EVEN, RNN_WIDTH), jnp.float32, 0.9, 0.999)
    sig = u ** (1.0 / LRU_C)
    lam = jnp.log(sig) - jnp.log1p(-sig)
    bw = RNN_WIDTH // RNN_BLOCKS
    return {
        "x": nrm(ks[0], (BATCH, SEQ, D_MODEL), 1.0),
        "p": nrm(ks[1], (DEPTH, BATCH, SEQ, PLE_DIM), 1.0),
        "ln1_g": 1.0 + nrm(ks[2], (DEPTH, D_MODEL), 0.02),
        "ln1_b": nrm(ks[3], (DEPTH, D_MODEL), 0.02),
        "ln2_g": 1.0 + nrm(ks[4], (DEPTH, D_MODEL), 0.02),
        "ln2_b": nrm(ks[5], (DEPTH, D_MODEL), 0.02),
        "mlp_w1": nrm(ks[6], (DEPTH, D_MODEL, D_FF), D_MODEL ** -0.5),
        "mlp_w2": nrm(ks[7], (DEPTH, D_FF, D_MODEL), DN_BETA * D_FF ** -0.5),
        "ple_w_proj": nrm(ks[8], (DEPTH, PLE_DIM, D_MODEL), DN_BETA * PLE_DIM ** -0.5),
        "ple_w_gate": nrm(ks[9], (DEPTH, D_MODEL, D_MODEL), D_MODEL ** -0.5),
        "hy_w_in": nrm(ks[10], (N_EVEN, D_MODEL, EVEN_IN), D_MODEL ** -0.5),
        "hy_conv_w": nrm(ks[11], (N_EVEN, CONV_WIDTH, RNN_WIDTH), CONV_WIDTH ** -0.5),
        "hy_conv_b": nrm(ks[13], (N_EVEN, RNN_WIDTH), 0.01),
        "hy_ga_w": nrm(ks[14], (N_EVEN, RNN_BLOCKS, bw, bw), bw ** -0.5),
        "hy_ga_b": nrm(ks[15], (N_EVEN, RNN_WIDTH), 0.01),
        "hy_gx_w": nrm(ks[16], (N_EVEN, RNN_BLOCKS, bw, bw), bw ** -0.5),
        "hy_gx_b": nrm(ks[17], (N_EVEN, RNN_WIDTH), 0.01),
        "hy_lambda": lam,
        "hy_w_out": nrm(ks[18], (N_EVEN, EVEN_MIX, D_MODEL), DN_BETA * EVEN_MIX ** -0.5),
        "mla_w_down": nrm(ks[19], (N_ODD, D_MODEL, MLA_DOWN), D_MODEL ** -0.5),
        "mla_q_norm": 1.0 + nrm(ks[20], (N_ODD, MLA_Q_LORA), 0.02),
        "mla_kv_norm": 1.0 + nrm(ks[21], (N_ODD, MLA_KV_LORA), 0.02),
        "mla_w_uq": nrm(ks[22], (N_ODD, MLA_Q_LORA, MLA_HEADS * (MLA_NOPE + MLA_ROPE)), MLA_Q_LORA ** -0.5),
        "mla_w_ukv": nrm(ks[23], (N_ODD, MLA_KV_LORA, MLA_HEADS * (MLA_NOPE + MLA_V)), MLA_KV_LORA ** -0.5),
        "mla_w_out": nrm(ks[24], (N_ODD, MLA_MIX, D_MODEL), DN_BETA * MLA_MIX ** -0.5),
    }

def first_block(x, p, ln1_g, ln1_b, ln2_g, ln2_b, mlp_w1, mlp_w2, ple_w_proj, ple_w_gate,
              hy_w_in, hy_conv_w, hy_conv_b, hy_ga_w, hy_ga_b, hy_gx_w, hy_gx_b, hy_lambda, hy_w_out,
              mla_w_down, mla_q_norm, mla_kv_norm, mla_w_uq, mla_w_ukv, mla_w_out):
    for i in range(DEPTH):
        j = i // 2
        if i % 2 == 0:
            m = hybrid_mixer(x, hy_w_in[j], hy_conv_w[j], hy_conv_b[j], hy_ga_w[j], hy_ga_b[j],
                             hy_gx_w[j], hy_gx_b[j], hy_lambda[j], hy_w_out[j])
        else:
            m = mla_mixer(x, mla_w_down[j], mla_q_norm[j], mla_kv_norm[j], mla_w_uq[j],
                          mla_w_ukv[j], mla_w_out[j])
        h = layer_norm(DN_ALPHA * x + m, ln1_g[i], ln1_b[i])
        f = jnp.square(jax.nn.relu(h @ mlp_w1[i])) @ mlp_w2[i]
        e = jax.nn.sigmoid(h @ ple_w_gate[i]) * (p[i] @ ple_w_proj[i])
        x = layer_norm(DN_ALPHA * h + f + e, ln2_g[i], ln2_b[i])
    return x


MIX_WIDTH = D_MODEL // 2
RET_HEAD_DIM = 128
RET_HEADS = MIX_WIDTH // RET_HEAD_DIM
RET_CHUNK = 128
RWKV_HEAD_DIM = 64
RWKV_HEADS = MIX_WIDTH // RWKV_HEAD_DIM
DECAY_LORA = 64
AAA_LORA = 64
GATE_LORA = 128
CONV_WIDTH_2 = 3
N_BRANCHES = 3
RET_COLS = 4 * MIX_WIDTH
RWKV_COLS = 3 * MIX_WIDTH + DECAY_LORA + AAA_LORA + GATE_LORA
CONV_COLS = 3 * MIX_WIDTH
IN_COLS = RET_COLS + RWKV_COLS + CONV_COLS
N_GROUPS = 4
EXPERTS_PER_GROUP = 8
N_EXPERTS = N_GROUPS * EXPERTS_PER_GROUP
EXPERT_FF = D_MODEL // 2
TOP_K = 2
MOE_BLOCK = 128
NORM_EPS = 1e-6
HEAD_NORM_EPS = 1e-5
RWKV_NORM_EPS = 64e-5


F32 = jnp.float32

def rms_norm_2(x, g):
    xf = x.astype(F32)
    y = xf * lax.rsqrt(jnp.mean(xf * xf, axis=-1, keepdims=True) + NORM_EPS)
    return (y * g.astype(F32)).astype(x.dtype)

def modulate(h, shift, scale):
    return (h.astype(F32) * (1.0 + scale[:, None, :]) + shift[:, None, :]).astype(h.dtype)

def head_norm(y, g, eps):
    yf = y.astype(F32)
    mu = jnp.mean(yf, axis=-1, keepdims=True)
    var = jnp.mean(jnp.square(yf - mu), axis=-1, keepdims=True)
    return (yf - mu) * lax.rsqrt(var + eps) * g.astype(F32).reshape(y.shape[-2:])

def rotary(t, positions):
    half = t.shape[-1] // 2
    inv_freq = ROPE_BASE ** (-jnp.arange(half, dtype=F32) / half)
    ang = positions.astype(F32)[..., None] * inv_freq
    cos = jnp.cos(ang)[:, :, None, :]
    sin = jnp.sin(ang)[:, :, None, :]
    t1 = t[..., :half].astype(F32)
    t2 = t[..., half:].astype(F32)
    return jnp.concatenate([t1 * cos - t2 * sin, t1 * sin + t2 * cos], axis=-1)

def retention(q, k, v, g, positions, gn_g):
    bsz, seq, _ = q.shape
    split = lambda t: t.reshape(bsz, seq, RET_HEADS, RET_HEAD_DIM)
    qh = rotary(split(q), positions)
    kh = rotary(split(k), positions) * (RET_HEAD_DIM ** -0.5)
    vh = split(v).astype(F32)
    n_chunks = seq // RET_CHUNK

    def to_chunks(t):
        return t.reshape(bsz, n_chunks, RET_CHUNK, RET_HEADS, RET_HEAD_DIM).transpose(1, 0, 3, 2, 4)

    log_gamma = jnp.log1p(-jnp.exp2(-5.0 - jnp.arange(RET_HEADS, dtype=F32)))
    pos = jnp.arange(RET_CHUNK, dtype=F32)
    rel = pos[:, None] - pos[None, :]
    decay_in = jnp.where(rel >= 0, jnp.exp(log_gamma[:, None, None] * jnp.maximum(rel, 0.0)), 0.0)
    decay_k = jnp.exp(log_gamma[:, None] * (RET_CHUNK - 1 - pos))
    decay_q = jnp.exp(log_gamma[:, None] * (pos + 1.0))
    decay_chunk = jnp.exp(log_gamma * RET_CHUNK)

    def chunk_step(state, qkv):
        qc, kc, vc = qkv
        scores = jnp.einsum('bhid,bhjd->bhij', qc, kc) * decay_in
        inner = jnp.einsum('bhij,bhjv->bhiv', scores, vc)
        cross = jnp.einsum('bhid,bhdv->bhiv', qc, state) * decay_q[None, :, :, None]
        state = state * decay_chunk[None, :, None, None] + jnp.einsum(
            'bhjd,bhjv->bhdv', kc * decay_k[None, :, :, None], vc)
        return state, inner + cross

    state0 = jnp.zeros((bsz, RET_HEADS, RET_HEAD_DIM, RET_HEAD_DIM), F32)
    _, out = lax.scan(chunk_step, state0, (to_chunks(qh), to_chunks(kh), to_chunks(vh)))
    out = out.transpose(1, 0, 3, 2, 4).reshape(bsz, seq, RET_HEADS, RET_HEAD_DIM)
    out = head_norm(out, gn_g, HEAD_NORM_EPS).reshape(bsz, seq, MIX_WIDTH)
    return (jax.nn.silu(g.astype(F32)) * out).astype(q.dtype)

def rwkv7_time_mix(p, mu, w0, w_lora, a0, a_lora, g_lora, k_k, k_a, r_k, gn_g):
    bsz, seq, _ = p.shape
    mw = MIX_WIDTH
    pf = p.astype(F32)
    prev = jnp.pad(pf, ((0, 0), (1, 0), (0, 0)))[:, :-1]
    pf = pf + mu * (prev - pf)
    o_w = 3 * mw
    o_a = o_w + DECAY_LORA
    o_g = o_a + AAA_LORA
    r = pf[..., 0:mw]
    k = pf[..., mw:2 * mw]
    v = pf[..., 2 * mw:3 * mw]
    wd = pf[..., o_w:o_a]
    ad = pf[..., o_a:o_g]
    gd = pf[..., o_g:o_g + GATE_LORA]
    w = jnp.exp(-math.exp(-0.5) * jax.nn.sigmoid(w0 + jnp.tanh(wd) @ w_lora))
    a = jax.nn.sigmoid(a0 + ad @ a_lora)
    g = jax.nn.sigmoid(gd) @ g_lora
    heads = lambda t: t.reshape(bsz, seq, RWKV_HEADS, RWKV_HEAD_DIM)
    r, w, k, v, a = heads(r), heads(w), heads(k), heads(v), heads(a)
    kk = k * k_k.reshape(RWKV_HEADS, RWKV_HEAD_DIM)
    kh = kk * lax.rsqrt(jnp.maximum(jnp.sum(kk * kk, axis=-1, keepdims=True), 1e-12))
    kt = k * (1.0 + (a - 1.0) * k_a.reshape(RWKV_HEADS, RWKV_HEAD_DIM))

    def time_step(state, inp):
        rt, wt, ktt, vt, kht, at = inp
        sk = jnp.einsum('bhvk,bhk->bhv', state, kht)
        state = (state * wt[:, :, None, :]
                 - sk[..., None] * (at * kht)[:, :, None, :]
                 + vt[..., None] * ktt[:, :, None, :])
        return state, jnp.einsum('bhvk,bhk->bhv', state, rt)

    tm = lambda t: jnp.moveaxis(t, 1, 0)
    state0 = jnp.zeros((bsz, RWKV_HEADS, RWKV_HEAD_DIM, RWKV_HEAD_DIM), F32)
    _, y = lax.scan(time_step, state0, (tm(r), tm(w), tm(kt), tm(v), tm(kh), tm(a)))
    y = jnp.moveaxis(y, 0, 1)
    y = head_norm(y, gn_g, RWKV_NORM_EPS)
    y = y + jnp.sum(r * kt * r_k.astype(F32), axis=-1, keepdims=True) * v
    return (y.reshape(bsz, seq, mw) * g).astype(p.dtype)

def short_conv(p, conv_w):
    h, bgate, cgate = jnp.split(p, 3, axis=-1)
    u = cgate * h
    seq = u.shape[1]
    up = jnp.pad(u, ((0, 0), (CONV_WIDTH_2 - 1, 0), (0, 0)))
    conv = conv_w[0] * up[:, 0:seq]
    for i in range(1, CONV_WIDTH_2):
        conv = conv + conv_w[i] * up[:, i:i + seq]
    return bgate * conv

def hier_moe(h, w_router_group, b_router_group, w_router_expert, b_router_expert,
             w_exp_gate, w_exp_up, w_exp_down):
    bsz, seq, d = h.shape
    n_tok = bsz * seq
    xf = h.reshape(n_tok, d)
    g_logits = (xf @ w_router_group + b_router_group).astype(F32)
    g_prob = jax.nn.softmax(g_logits, axis=-1)
    g_sel = jnp.argmax(g_logits, axis=-1).astype(jnp.int32)
    p_group = jnp.take_along_axis(g_prob, g_sel[:, None], axis=-1)
    e_logits = (xf @ w_router_expert + b_router_expert).astype(F32).reshape(n_tok, N_GROUPS, EXPERTS_PER_GROUP)
    e_logits = jnp.take_along_axis(e_logits, g_sel[:, None, None], axis=1)[:, 0]
    top_v, top_i = lax.top_k(e_logits, TOP_K)
    weights = (jax.nn.softmax(top_v, axis=-1) * p_group).reshape(-1)
    eid = (g_sel[:, None] * EXPERTS_PER_GROUP + top_i).reshape(-1).astype(jnp.int32)
    tok = jnp.repeat(jnp.arange(n_tok, dtype=jnp.int32), TOP_K)
    n_assign = n_tok * TOP_K
    order = jnp.argsort(eid)
    eid_s, tok_s, w_s = eid[order], tok[order], weights[order]
    counts = jnp.bincount(eid, length=N_EXPERTS).astype(jnp.int32)
    starts = jnp.cumsum(counts) - counts
    padded = (counts + MOE_BLOCK - 1) // MOE_BLOCK * MOE_BLOCK
    pends = jnp.cumsum(padded)
    pstarts = pends - padded
    dest = pstarts[eid_s] + jnp.arange(n_assign, dtype=jnp.int32) - starts[eid_s]
    n_rows = n_assign + N_EXPERTS * MOE_BLOCK
    n_blocks = n_rows // MOE_BLOCK
    row_tok = jnp.full((n_rows,), n_tok, jnp.int32).at[dest].set(tok_s)
    row_w = jnp.zeros((n_rows,), F32).at[dest].set(w_s)
    block_e = jnp.minimum(
        jnp.searchsorted(pends, jnp.arange(n_blocks, dtype=jnp.int32) * MOE_BLOCK, side='right'),
        N_EXPERTS - 1)
    x_rows = jnp.concatenate([xf, jnp.zeros((1, d), xf.dtype)], axis=0)[row_tok]
    x_rows = x_rows.reshape(n_blocks, MOE_BLOCK, d)

    def expert_block(args):
        xb, e = args
        return (jax.nn.silu(xb @ w_exp_gate[e]) * (xb @ w_exp_up[e])) @ w_exp_down[e]

    y_rows = lax.map(expert_block, (x_rows, block_e)).reshape(n_rows, d)
    y_rows = y_rows.astype(F32) * row_w[:, None]
    out = jax.ops.segment_sum(y_rows, row_tok, num_segments=n_tok + 1)[:n_tok]
    return out.reshape(bsz, seq, d).astype(h.dtype)

def decoder_layer(x, c, positions, norm1_g, norm2_g, w_ada, b_ada, w_in, w_gate, b_gate,
                  ret_gn_g, rwkv_mu, rwkv_w0, rwkv_w_lora, rwkv_a0, rwkv_a_lora, rwkv_g_lora,
                  rwkv_k_k, rwkv_k_a, rwkv_r_k, rwkv_gn_g, conv_w, w_branch, w_o,
                  w_router_group, b_router_group, w_router_expert, b_router_expert,
                  w_exp_gate, w_exp_up, w_exp_down):
    d = D_MODEL
    mod = jax.nn.silu(c.astype(F32)) @ w_ada + b_ada
    shift1, scale1, gate1, shift2, scale2, gate2 = jnp.split(mod, 6, axis=-1)

    h = modulate(rms_norm_2(x, norm1_g), shift1, scale1)
    p = h @ w_in
    p_ret = p[..., :RET_COLS]
    p_rwkv = p[..., RET_COLS:RET_COLS + RWKV_COLS]
    p_conv = p[..., RET_COLS + RWKV_COLS:]
    q, k, v, g = jnp.split(p_ret, 4, axis=-1)
    y_ret = retention(q, k, v, g, positions, ret_gn_g)
    y_rwkv = rwkv7_time_mix(p_rwkv, rwkv_mu, rwkv_w0, rwkv_w_lora, rwkv_a0, rwkv_a_lora,
                            rwkv_g_lora, rwkv_k_k, rwkv_k_a, rwkv_r_k, rwkv_gn_g)
    y_conv = short_conv(p_conv, conv_w)
    gates = jax.nn.sigmoid((h @ w_gate + b_gate).astype(F32))
    merged = jnp.zeros(x.shape, F32)
    for i, y in enumerate((y_ret, y_rwkv, y_conv)):
        merged = merged + gates[..., i * d:(i + 1) * d] * (y @ w_branch[i])
    x = x + (gate1[:, None, :] * (merged.astype(x.dtype) @ w_o)).astype(x.dtype)

    h2 = modulate(rms_norm_2(x, norm2_g), shift2, scale2)
    y_moe = hier_moe(h2, w_router_group, b_router_group, w_router_expert, b_router_expert,
                     w_exp_gate, w_exp_up, w_exp_down)
    x = x + (gate2[:, None, :] * y_moe).astype(x.dtype)
    return x

def second_inputs(seed: int = 0) -> dict:
    key = jax.random.key(seed)
    k = jax.random.split(key, 32)
    L, D, MW = DEPTH, D_MODEL, MIX_WIDTH

    def nrm(kk, shape, scale):
        return scale * jax.random.normal(kk, shape, jnp.float32)

    return {
        'x': nrm(k[0], (BATCH, SEQ, D), 1.0),
        'c': nrm(k[1], (BATCH, D), 1.0),
        'positions': jnp.tile(jnp.arange(SEQ, dtype=jnp.int32)[None, :], (BATCH, 1)),
        'norm1_g': 1.0 + nrm(k[2], (L, D), 0.02),
        'norm2_g': 1.0 + nrm(k[3], (L, D), 0.02),
        'final_norm_g': 1.0 + nrm(k[4], (D,), 0.02),
        'w_ada': nrm(k[5], (L, D, 6 * D), 0.5 * D ** -0.5),
        'b_ada': nrm(k[6], (L, 6 * D), 0.01),
        'w_in': nrm(k[7], (L, D, IN_COLS), D ** -0.5),
        'w_gate': nrm(k[8], (L, D, N_BRANCHES * D), D ** -0.5),
        'b_gate': nrm(k[9], (L, N_BRANCHES * D), 0.01),
        'ret_gn_g': 1.0 + nrm(k[10], (L, MW), 0.02),
        'rwkv_mu': jax.random.uniform(k[11], (L, RWKV_COLS), jnp.float32),
        'rwkv_w0': nrm(k[12], (L, MW), 0.5),
        'rwkv_w_lora': nrm(k[13], (L, DECAY_LORA, MW), DECAY_LORA ** -0.5),
        'rwkv_a0': nrm(k[14], (L, MW), 0.5),
        'rwkv_a_lora': nrm(k[15], (L, AAA_LORA, MW), AAA_LORA ** -0.5),
        'rwkv_g_lora': nrm(k[16], (L, GATE_LORA, MW), GATE_LORA ** -0.5),
        'rwkv_k_k': 0.85 + nrm(k[17], (L, MW), 0.05),
        'rwkv_k_a': 1.0 + nrm(k[18], (L, MW), 0.05),
        'rwkv_r_k': nrm(k[19], (L, RWKV_HEADS, RWKV_HEAD_DIM), 0.1),
        'rwkv_gn_g': 1.0 + nrm(k[20], (L, MW), 0.02),
        'conv_w': nrm(k[21], (L, CONV_WIDTH_2, MW), CONV_WIDTH_2 ** -0.5),
        'w_branch': nrm(k[22], (L, N_BRANCHES, MW, D), MW ** -0.5),
        'w_o': nrm(k[23], (L, D, D), D ** -0.5),
        'w_router_group': nrm(k[24], (L, D, N_GROUPS), D ** -0.5),
        'b_router_group': nrm(k[25], (L, N_GROUPS), 0.01),
        'w_router_expert': nrm(k[26], (L, D, N_EXPERTS), D ** -0.5),
        'b_router_expert': nrm(k[27], (L, N_EXPERTS), 0.01),
        'w_exp_gate': nrm(k[28], (L, N_EXPERTS, D, EXPERT_FF), D ** -0.5),
        'w_exp_up': nrm(k[29], (L, N_EXPERTS, D, EXPERT_FF), D ** -0.5),
        'w_exp_down': nrm(k[30], (L, N_EXPERTS, EXPERT_FF, D), EXPERT_FF ** -0.5),
    }

def second_block(x, c, positions, norm1_g, norm2_g, final_norm_g, w_ada, b_ada, w_in, w_gate, b_gate,
              ret_gn_g, rwkv_mu, rwkv_w0, rwkv_w_lora, rwkv_a0, rwkv_a_lora, rwkv_g_lora,
              rwkv_k_k, rwkv_k_a, rwkv_r_k, rwkv_gn_g, conv_w, w_branch, w_o,
              w_router_group, b_router_group, w_router_expert, b_router_expert,
              w_exp_gate, w_exp_up, w_exp_down):
    for l in range(DEPTH):
        x = decoder_layer(
            x, c, positions, norm1_g[l], norm2_g[l], w_ada[l], b_ada[l], w_in[l], w_gate[l], b_gate[l],
            ret_gn_g[l], rwkv_mu[l], rwkv_w0[l], rwkv_w_lora[l], rwkv_a0[l], rwkv_a_lora[l],
            rwkv_g_lora[l], rwkv_k_k[l], rwkv_k_a[l], rwkv_r_k[l], rwkv_gn_g[l], conv_w[l],
            w_branch[l], w_o[l], w_router_group[l], b_router_group[l], w_router_expert[l],
            b_router_expert[l], w_exp_gate[l], w_exp_up[l], w_exp_down[l])
    return rms_norm_2(x, final_norm_g)


def setup_inputs(seed=0):
    out = dict(first_inputs(seed))
    for name, value in second_inputs(seed + 1).items():
        if name != "x":
            out[name + "_2"] = value
    return out


def reference(
    x, p, ln1_g, ln1_b, ln2_g, ln2_b, mlp_w1, mlp_w2, ple_w_proj, ple_w_gate, hy_w_in,
    hy_conv_w, hy_conv_b, hy_ga_w, hy_ga_b, hy_gx_w, hy_gx_b, hy_lambda, hy_w_out, mla_w_down,
    mla_q_norm, mla_kv_norm, mla_w_uq, mla_w_ukv, mla_w_out, c_2, positions_2, norm1_g_2,
    norm2_g_2, final_norm_g_2, w_ada_2, b_ada_2, w_in_2, w_gate_2, b_gate_2, ret_gn_g_2,
    rwkv_mu_2, rwkv_w0_2, rwkv_w_lora_2, rwkv_a0_2, rwkv_a_lora_2, rwkv_g_lora_2, rwkv_k_k_2,
    rwkv_k_a_2, rwkv_r_k_2, rwkv_gn_g_2, conv_w_2, w_branch_2, w_o_2, w_router_group_2,
    b_router_group_2, w_router_expert_2, b_router_expert_2, w_exp_gate_2, w_exp_up_2,
    w_exp_down_2,
):
    x = first_block(
        x, p, ln1_g, ln1_b, ln2_g, ln2_b, mlp_w1, mlp_w2, ple_w_proj, ple_w_gate, hy_w_in,
        hy_conv_w, hy_conv_b, hy_ga_w, hy_ga_b, hy_gx_w, hy_gx_b, hy_lambda, hy_w_out,
        mla_w_down, mla_q_norm, mla_kv_norm, mla_w_uq, mla_w_ukv, mla_w_out,
    )
    return second_block(
        x, c_2, positions_2, norm1_g_2, norm2_g_2, final_norm_g_2, w_ada_2, b_ada_2, w_in_2,
        w_gate_2, b_gate_2, ret_gn_g_2, rwkv_mu_2, rwkv_w0_2, rwkv_w_lora_2, rwkv_a0_2,
        rwkv_a_lora_2, rwkv_g_lora_2, rwkv_k_k_2, rwkv_k_a_2, rwkv_r_k_2, rwkv_gn_g_2, conv_w_2,
        w_branch_2, w_o_2, w_router_group_2, b_router_group_2, w_router_expert_2,
        b_router_expert_2, w_exp_gate_2, w_exp_up_2, w_exp_down_2,
    )


_drawn_inputs = setup_inputs


def setup_inputs(seed=0):
    import zlib

    import numpy as np

    out = dict(_drawn_inputs(seed))
    spreads = {}
    factors = {'hy_conv_b': 5.038,
     'hy_ga_b': 8.0,
     'hy_gx_b': 8.0,
     'mla_q_norm': 8.0,
     'mla_kv_norm': 8.0,
     'norm1_g_2': 3.151,
     'norm2_g_2': 3.28,
     'final_norm_g_2': 8.563,
     'b_gate_2': 8.0,
     'ret_gn_g_2': 8.0,
     'rwkv_k_k_2': 32.28,
     'rwkv_k_a_2': 4.115,
     'rwkv_gn_g_2': 31.327,
     'b_router_group_2': 7.672,
     'b_router_expert_2': 14.646}
    for name, (base, spread) in spreads.items():
        noise = np.random.default_rng([zlib.crc32(name.encode()), seed]).standard_normal(out[name].shape)
        drawn = base * np.exp(spread * noise) if base else spread * noise
        out[name] = __import__('jax').numpy.asarray(drawn.astype(out[name].dtype))
    for name, factor in factors.items():
        out[name] = (out[name] * factor).astype(out[name].dtype)
    return out
```

```python
import math
from contextlib import ExitStack

import numpy as np
import concourse.bass as bass
from concourse import mybir
from concourse.alu_op_type import AluOpType as ALU

ACT = mybir.ActivationFunctionType
AX = mybir.AxisListType
F32 = mybir.dt.float32
I32 = mybir.dt.int32

P = 128
D = 1024
KT = D // P
S = 256
TT = S // P
DEPTH = 2
FFN = 4 * D
RNN = 512
DSA_H, DSA_D = 8, 64
IDX_H = 4
TOPK = min(256, S // 4)
MLA_H, NOPE, ROPE, VD = 16, 64, 32, 64
QL, KVL = 512, 256
RET_H = 4
RW_H, RW_D = 8, 64
N_GROUP, PER_GROUP = 4, 8
N_EXP = N_GROUP * PER_GROUP
IN_TILES = 5376 // P
ALPHA = (2 * DEPTH) ** 0.25
BIG = 1e30
TAKEN = -3e38
SLOTS = 4
SLOT = 4096
BANKS = 4


def constant_table():
    cols, at, n = [], {}, 0

    def put(name, a):
        nonlocal n
        full = np.zeros((P, a.shape[1]), np.float32)
        full[:a.shape[0]] = a
        cols.append(full)
        at[name] = (n, a.shape[1])
        n += a.shape[1]

    p = np.arange(P)
    put("ident", np.eye(P))
    put("ones", np.ones((P, P)))
    put("head_ones", (p[:, None] // 64 == p[None, :] // 64).astype(np.float32))
    put("swap", (p[:, None] == (p[None, :] + 64) % P).astype(np.float32))
    swap96 = np.zeros((96, 96), np.float32)
    for m in range(ROPE):
        swap96[NOPE + (m + ROPE // 2) % ROPE, NOPE + m] = 1.0
    put("swap_rope", swap96)
    t = np.arange(S)
    q = p[:, None] + P * np.arange(TT)[None, :]
    dist = q[:, :, None] - t[None, None, :]
    put("dist", dist.reshape(P, TT * S))
    put("causal", (dist >= 0).astype(np.float32).reshape(P, TT * S))
    put("noncausal", np.where(dist >= 0, 0.0, -BIG).reshape(P, TT * S))
    freq = (np.float32(10000.0) ** (-np.arange(0, ROPE, 2, dtype=np.float32) / ROPE)).astype(np.float32)
    ang = (t.astype(np.float32)[None, :] * freq[:, None]).astype(np.float32)
    cos, sin = np.ones((96, S)), np.zeros((96, S))
    cos[NOPE:] = np.concatenate([np.cos(ang)] * 2)
    sin[NOPE:] = np.concatenate([-np.sin(ang), np.sin(ang)])
    put("rope_cos", cos)
    put("rope_sin", sin)
    inv = (np.float32(10000.0) ** (-np.arange(64, dtype=np.float32) / np.float32(64))).astype(np.float32)
    put("inv_freq", np.concatenate([inv, inv])[:, None])
    put("sin_sign", np.where(p < 64, -1.0, 1.0)[:, None])
    lg = np.log1p(-np.exp2(-5.0 - np.arange(RET_H)))
    rel = p[None, :] - p[:, None]
    put("ret_decay_in", np.stack([np.where(rel >= 0, np.exp(g * np.maximum(rel, 0)), 0.0) for g in lg], 1)
        .reshape(P, -1) * P ** -0.5)
    put("ret_decay_k", np.stack([np.exp(g * (P - 1 - p)) for g in lg], 1) * P ** -0.5)
    put("ret_decay_q", np.stack([np.broadcast_to(np.exp(g * (p + 1.0))[None, :], (P, P)) for g in lg], 1)
        .reshape(P, -1))
    put("zeros", np.zeros((P, P)))
    put("before", (p[:, None] < p[None, :]).astype(np.float32))
    put("upto", (p[:, None] <= p[None, :]).astype(np.float32))
    levels = []
    for lev in range(7):
        b = 1 << lev
        s_, t_ = p[:, None], p[None, :]
        levels.append(((s_ // (2 * b) == t_ // (2 * b)) & ((t_ // b) % 2 == 1) & ((s_ // b) % 2 == 0)))
    put("levels", np.concatenate(levels, 1).astype(np.float32))
    put("first4", np.broadcast_to(np.arange(4, 0, -1.0), (P, 4)))
    put("first32", np.broadcast_to(np.arange(32, 0, -1.0), (P, 32)))
    return np.ascontiguousarray(np.concatenate(cols, 1), dtype=np.float32), at


CONST, CONST_AT = constant_table()
TWO_PI = (6.28125, 0.0019350051879882812, 3.019915981956753e-07)


def h8(ap):
    return ap.rearrange("p (h d) -> p h d", h=8)

VECTORS = []
for _l in range(DEPTH):
    for _n in ("ln1_g", "ln1_b", "ln2_g", "ln2_b"):
        VECTORS.append((f"{_n}{_l}", KT, _n, _l))
VECTORS += [(f"conv_w{i}", 4, "hy_conv_w", (0, i)) for i in range(4)]
VECTORS += [("conv_b", 4, "hy_conv_b", 0), ("ga_b", 4, "hy_ga_b", 0), ("gx_b", 4, "hy_gx_b", 0),
            ("lam", 4, "hy_lambda", 0), ("q_norm", 4, "mla_q_norm", 0), ("kv_norm", 2, "mla_kv_norm", 0),
            ("c", KT, "c_2", 0), ("final_g", KT, "final_norm_g_2", None)]
for _l in range(DEPTH):
    VECTORS += [(f"norm1_g{_l}", KT, "norm1_g_2", _l), (f"norm2_g{_l}", KT, "norm2_g_2", _l),
                (f"b_ada{_l}", 48, "b_ada_2", _l), (f"b_gate{_l}", 24, "b_gate_2", _l),
                (f"ret_gn{_l}", 4, "ret_gn_g_2", _l), (f"mu{_l}", 14, "rwkv_mu_2", _l),
                (f"w0{_l}", 4, "rwkv_w0_2", _l), (f"a0{_l}", 4, "rwkv_a0_2", _l),
                (f"k_k{_l}", 4, "rwkv_k_k_2", _l), (f"k_a{_l}", 4, "rwkv_k_a_2", _l),
                (f"r_k{_l}", 4, "rwkv_r_k_2", _l), (f"rw_gn{_l}", 4, "rwkv_gn_g_2", _l)]
    VECTORS += [(f"cw{_l}{i}", 4, "conv_w_2", (_l, i)) for i in range(3)]
VEC_AT, _n = {}, 0
for _v in VECTORS:
    VEC_AT[_v[0]] = (_n, _v[1])
    _n += _v[1]
N_VEC = _n

STREAM = [("hy_in", (0, 1), 2), ("hy_out", (2, 3), 1)]
for _l in range(DEPTH):
    if _l == 1:
        STREAM += [("mla_down", (0, 1), 1), ("mla_uq", (2, 3), 1), ("mla_ukv", (0,), 1), ("mla_out", (2, 3), 1)]
    STREAM += [(f"mlp{_l}", (0, 1, 2, 3), 4), (f"ple_gate{_l}", (0, 1), 1), (f"ple_proj{_l}", (2,), 1)]
for _l in range(DEPTH):
    STREAM += [(f"ada{_l}", (0, 1), 6), (f"w_in{_l}", (2, 3), 5), (f"w_in_last{_l}", (0,), 1),
               (f"w_gate{_l}", (2, 3), 3), (f"w_branch{_l}", (0, 1, 2), 1), (f"w_o{_l}", (0, 1), 1),
               (f"moe{_l}", (1, 2, 3), N_EXP)]
SLOT_AT, _uses = {}, [0] * SLOTS
for _name, _slots, _times in STREAM:
    SLOT_AT[_name] = [(s, _uses[s]) for s in _slots]
    for s in _slots:
        _uses[s] += _times

BANK_USES = [("x_in", 4), ("hy_in", 8), ("dsa_v", 1), ("rg_gates", 4), ("idx", 4), ("dsa", 4 * 5), ("hy_out", 4)]
for _l in range(DEPTH):
    if _l == 1:
        BANK_USES += [("mla_down", 4), ("mla_uq", 8), ("mla_rope", 9), ("mla_k", 8), ("mla_v", 4),
                      ("mla", 8 * 5), ("mla_out", 4)]
    BANK_USES += [(f"p_in{_l}", 1), (f"mlp{_l}", 16), (f"ple_gate{_l}", 4), (f"ple_proj{_l}", 4)]
for _l in range(DEPTH):
    BANK_USES += [(f"ada{_l}", 24), (f"w_in{_l}", 21), (f"rot{_l}", 4), (f"ret_t{_l}", 3), (f"ret{_l}", 7),
                  (f"lora{_l}", 6), (f"head_sum{_l}", 4), (f"rw_t{_l}", 4), (f"rwkv{_l}", 2 * (8 + 7 * 6 + 4) + 1),
                  (f"w_gate{_l}", 12), (f"w_branch{_l}", 12), (f"w_o{_l}", 4),
                  (f"route{_l}", 2), (f"moe{_l}", 4 * N_EXP)]
BANK_USES += [("x_out", 4)]
BANK_AT, _n = {}, 0
for _name, _k in BANK_USES:
    BANK_AT[_name] = _n
    _n += _k


class Count:

    def __init__(self):
        self.own, self.seen = 0, {}

    def up(self):
        self.own += 1
        return self.own

    def nxt(self, name, k=1):
        self.seen[name] = self.seen.get(name, 0) + k
        return self.seen[name]


def filled(n, i=0):
    return i + (n // BANKS + 1)


def emptied(n, i=0):
    return i + n // BANKS


def loaded(u, i=0):
    return i * 16 + 16 * (u + 1)


def attention_order(n0, pairs):
    order = {}
    for hp in range(pairs + 1):
        if hp < pairs:
            for tt in range(TT):
                order["l", hp, tt] = n0 + len(order)
        if hp:
            for h in range(2):
                order["t", hp - 1, h] = n0 + len(order)
            order["o", hp - 1, 0] = n0 + len(order)
    return order


def build(nc, a, out):
    with ExitStack() as ctx:
        def sb(name, shape, dt=F32):
            return ctx.enter_context(nc.sbuf_tensor(name, shape, dt))

        ring = [sb(f"ring{s}", [P, SLOT]) for s in range(SLOTS)]
        const = sb("const", [P, CONST.shape[1]])
        vec = sb("vec", [P, N_VEC])
        xT = sb("xT", [P, KT, S])
        hT = sb("hT", [P, KT, S])
        R = sb("R", [P, KT, S])
        SQ = sb("SQ", [P, KT, S])
        PR = sb("PR", [P, IN_TILES, S])
        GT = sb("GT", [P, 24, S])
        YB = sb("YB", [P, 12, S])
        stat = sb("stat", [P, 2, S])
        pin = sb("pin", [P, 2, S])
        pT = sb("pT", [P, 2, S])
        sm = sb("sm", [P, 512])
        mod = sb("mod", [P, DEPTH * 48])
        small_w = sb("small_w", [P, 1024])
        cosT, sinT = pin[:, 0, :], pin[:, 1, :]
        posi = pT[:, 1, :].bitcast(I32)
        S1 = pT[:, 0, :]
        bank = [ctx.enter_context(nc.psum_tensor(f"bank{b}", [P, 512], F32)) for b in range(8)]
        acc = bank[4:8]
        cw_dram = nc.dram_tensor("expert_weights", (DEPTH, N_EXP, S), F32).ap()

        def C(name):
            o, w = CONST_AT[name]
            return const[:, o:o + w]

        def V_(name):
            o, w = VEC_AT[name]
            return vec[:, o:o + w]

        def bk(n):
            return bank[n % BANKS]

        def two(ap):
            return ap.rearrange("p (a b) -> p a b", a=2)

        def flat(ap):
            return ap.rearrange("p a b -> p (a b)")

        def bcast(ap, n):
            return ap.unsqueeze(1).to_broadcast([ap.shape[0], n, ap.shape[1]])

        names = [
            "inputs_loaded", "x_loaded", "p_loaded", "small_loaded", "kvw_loaded", "tail_loaded", "pos_loaded",
            "lam_abs", "lam_log", "conv_done", "decay_in", "decay_tanh", "decay_den", "decay_sqrt", "gelu_in", "gelu_sig",
            "dsa_max", "dsa_exp", "dsa_probs",
            "norm_in", "norm_sum", "norm_centered", "norm_sq", "norm_var", "norm_std", "norm_scaled", "norm_out",
            "ff_act", "down_done", "kr_rope", "kr_spread", "q_roped",
            "c_sig", "c_silu", "mod_done", "rot_in", "rot_tables",
            "g_sig", "ret_kq", "ret_norm", "y_ret", "head_var", "head_std",
            "mixed", "lora_in", "decay_sum", "decay_exp", "kk_sq", "kk_max", "kk_sqrt", "rw_bonus", "rw_ops",
            "mm_mask", "x_new", "rw_norm", "branch_done", "merged",
            "router_max", "router_exp", "router_w", "cw_stored", "cw_loaded", "moe_sig", "moe_gated", "moe_h",
            "x_new_layer", "out_stored", "vec_chain", "act_chain", "pe_chain", "pool_chain"]
        sems = {n: ctx.enter_context(nc.semaphore(n)) for n in names}
        bank_full = [ctx.enter_context(nc.semaphore(f"bank_full{b}")) for b in range(BANKS)]
        bank_read = [ctx.enter_context(nc.semaphore(f"bank_read{b}")) for b in range(BANKS)]
        slot_full = [ctx.enter_context(nc.semaphore(f"slot_full{s}")) for s in range(SLOTS)]
        block = ctx.enter_context(nc.Block())

        XR, YR, Q0, KD, IQ, IK = 0, 4, 8, 12, 13, 15
        XC, RG, IG = 16, 20, 24
        LG = PR[:, 28:36, :]
        PTB = PR[:, 36:40, :]
        ADM = GT[:, 0:2, :]
        ISC = GT[:, 2:4, :]
        RELU = GT[:, 4:12, :]
        VI = GT[:, 12:13, :]
        MIX = YB[:, 0:8, :]
        QH = PR[:, 0:16, :]
        KH = GT[:, 0:16, :]
        VH = PR[:, 16:24, :]
        CQ = PR[:, 24:30, :]
        KRAW = PR[:, 30, :]
        KROT = PR[:, 31, :]
        FF = PR[:, 32:40, :]

        HI = PR[:, 30:42, :]
        AT_, BT_, KT_, RT_ = SQ[:, 0:4, :], GT[:, 4:8, :], HI[:, 4:8, :], PR[:, 16:20, :]
        KKH, BV, GG, CUM = SQ[:, 4:8, :], HI[:, 8:12, :], GT[:, 8:12, :], GT[:, 12:16, :]
        MMs = (flat(R[:, 0:4, :]), flat(R[:, 4:8, :]))
        MTraw, Xm, XTm, Tm = (flat(PR[:, q:q + 4, :]) for q in (0, 4, 8, 12))
        VT2, NTm, RBm, RKm = (flat(GT[:, q:q + 4, :]) for q in (0, 12, 16, 20))
        BT0, KT0 = flat(PR[:, 20:22, :]), flat(PR[:, 22:24, :])
        Zm, Um = flat(SQ[:, 4:6, :]), flat(SQ[:, 6:8, :])
        YC, YSQ = flat(HI[:, 0:2, :]), flat(HI[:, 2:4, :])

        def vi(tt, c0, c1):
            return flat(VI)[:, tt * 68 + c0:tt * 68 + c1]

        @block.sync
        def _(sp):
            L = Count()
            released = [None] * SLOTS
            down = [0]

            def stream(name, srcs, per_bank):
                slots = SLOT_AT[name]
                times = [t for n_, _, t in STREAM if n_ == name][0]
                for s, _ in slots:
                    if released[s]:
                        sp.wait_ge(*released[s])

                def body(i):
                    for j, (s, u) in enumerate(slots):
                        kind, k, stride = per_bank[j]
                        if not isinstance(i, int):
                            if kind == "bank":
                                n = BANK_AT[name] + k
                                sp.wait_ge(bank_full[n % BANKS], i + n // BANKS)
                            else:
                                sp.wait_ge(sems["down_done"], i * stride + (down[0] + k + 1 - stride))
                        for dst, src in srcs(i, j):
                            sp.dma_start(dst, src).then_inc(slot_full[s], 16)
                body(0)
                if times > 1:
                    with nc.sync.Fori(1, times) as i:
                        body(i)
                for j, (s, _) in enumerate(slots):
                    kind, k, stride = per_bank[j]
                    if kind == "bank":
                        n = BANK_AT[name] + k
                        released[s] = (bank_full[n % BANKS], n // BANKS + 1 + (times - 1))
                    else:
                        released[s] = (sems["down_done"], down[0] + k + 1 + stride * (times - 1))
                if any(p[0] == "down" for p in per_bank):
                    down[0] += {"mlp": 8, "moe": N_EXP}[name[:3]]

            def cols(w, i, j, n=512, kt=KT):
                return w[:, bass.ds(i * (2 * n) + j * n, n)].rearrange("(k p) n -> p k n", p=P)

            def lin8(name, w):
                stream(name, lambda i, j: [(ring[SLOT_AT[name][j][0]][:].rearrange("p (k n) -> p k n", k=KT),
                                            cols(w, i, j))], [("bank", 1, 1), ("bank", 3, 1)])

            sp.dma_start(const[:], a["const"]).then_inc(sems["inputs_loaded"], 16)
            sp.dma_start(vec[:], a["vectors"]).then_inc(sems["inputs_loaded"], 16)
            sp.dma_start(R[:].rearrange("p (t k) s -> p t (k s)", t=TT), a["x"][0].rearrange("(t p) d -> p t d", p=P)).then_inc(sems["x_loaded"], 16)
            sp.dma_start(small_w[:], a["gate_blocks"]).then_inc(sems["small_loaded"], 16)
            w_in = a["hy_w_in"][0]
            tail = w_in[:, 1536:1988].rearrange("(k p) n -> p k n", p=P)
            sp.dma_start(GT[:, 20:24, :].rearrange("p a b -> p (a b)")[:, 0:KT * 68].rearrange("p (k n) -> p k n", k=KT)[:, :, 0:64],
                         tail[:, :, 64:128]).then_inc(sems["kvw_loaded"], 16)
            sp.dma_start(GT[:, 20:24, :].rearrange("p a b -> p (a b)")[:, 0:KT * 68].rearrange("p (k n) -> p k n", k=KT)[:, :, 64:68],
                         tail[:, :, 448:452]).then_inc(sems["kvw_loaded"], 16)

            s0, s1 = 0, 1
            r0 = ring[0][:].rearrange("p (k n) -> p k n", k=KT)
            r1 = ring[1][:].rearrange("p (k n) -> p k n", k=KT)
            sp.dma_start(r0, w_in[:, 0:512].rearrange("(k p) n -> p k n", p=P)).then_inc(slot_full[0], 16)
            sp.dma_start(r1, w_in[:, 512:1024].rearrange("(k p) n -> p k n", p=P)).then_inc(slot_full[1], 16)
            n0 = BANK_AT["hy_in"]
            sp.wait_ge(bank_full[(n0 + 1) % BANKS], filled(n0 + 1))
            sp.dma_start(r0, w_in[:, 1024:1536].rearrange("(k p) n -> p k n", p=P)).then_inc(slot_full[0], 16)
            sp.wait_ge(bank_full[(n0 + 3) % BANKS], filled(n0 + 3))
            for c, (c0, c1) in ((0, (0, 64)), (64, (0, 64)), (128, (128, 384)), (384, (384, 448)), (448, (384, 448))):
                sp.dma_start(r1[:, :, c:c + c1 - c0], tail[:, :, c0:c1]).then_inc(
                    slot_full[1] if c == 448 else sems["tail_loaded"], 16)
            released[0] = (bank_full[(n0 + 5) % BANKS], (n0 + 5) // BANKS + 1)
            released[1] = (bank_full[(n0 + 7) % BANKS], (n0 + 7) // BANKS + 1)
            lin8("hy_out", a["hy_w_out"][0])

            def mlp(l):
                w1, w2 = a["mlp_w1"][l], a["mlp_w2"][l]
                nm = f"mlp{l}"

                def src(i, j):
                    c, is_down = j // 2, j % 2
                    s = SLOT_AT[nm][j][0]
                    if not is_down:
                        return [(ring[s][:].rearrange("p (k n) -> p k n", k=KT), cols(w1, i, c))]
                    return [(ring[s][:].rearrange("p (k n) -> p k n", k=4),
                             w2[bass.ds(i * 1024 + c * 512, 512), :].rearrange("(k p) n -> p k n", p=P))]
                stream(nm, src, [("bank", 1, 1), ("down", 0, 2), ("bank", 3, 1), ("down", 1, 2)])
                lin8(f"ple_gate{l}", a["ple_w_gate"][l])
                stream(f"ple_proj{l}", lambda i, j: [(ring[2][:, 0:2048].rearrange("p (k n) -> p k n", k=2),
                                                      a["ple_w_proj"][l].rearrange("(k p) n -> p k n", p=P))],
                       [("bank", 3, 1)])

            def load_p(l):
                if l:
                    sp.wait_ge(bank_full[(BANK_AT[f"p_in{l - 1}"]) % BANKS], filled(BANK_AT[f"p_in{l - 1}"]))
                sp.dma_start(pin[:], a["p"][l, 0].rearrange("(t p) f -> p t f", p=P)).then_inc(sems["p_loaded"], 16)

            load_p(0)
            mlp(0)
            wd = a["mla_w_down"][0]
            stream("mla_down", lambda i, j: [
                (ring[j][:].rearrange("p (k n) -> p k n", k=KT)[:, :, 0:(512, 288)[j]],
                 wd[:, j * 512:(512, 800)[j]].rearrange("(k p) n -> p k n", p=P))], [("bank", 1, 1), ("bank", 3, 1)])
            uq = a["mla_w_uq"][0]
            stream("mla_uq", lambda i, j: [(ring[2 + j][:, 0:3072].rearrange("p (k n) -> p k n", k=4),
                                            uq[:, j * 768:(j + 1) * 768].rearrange("(k p) n -> p k n", p=P))],
                   [("bank", 3, 1), ("bank", 7, 1)])
            n_v = BANK_AT["mla_v"] + 3
            sp.wait_ge(*released[0])
            sp.dma_start(ring[0][:].rearrange("p (k n) -> p k n", k=2),
                         a["mla_w_ukv"][0].rearrange("(k p) n -> p k n", p=P)).then_inc(slot_full[0], 16)
            released[0] = (bank_full[n_v % BANKS], n_v // BANKS + 1)
            lin8("mla_out", a["mla_w_out"][0])
            load_p(1)
            mlp(1)
            sp.wait_ge(bank_full[(BANK_AT["ple_proj1"] + 3) % BANKS], filled(BANK_AT["ple_proj1"] + 3))
            sp.dma_start(posi, a["positions_2"].to_broadcast([P, S])).then_inc(sems["pos_loaded"], 16)
            for l in range(DEPTH):
                lin8(f"ada{l}", a["w_ada_2"][l])
                lin8(f"w_in{l}", a["w_in_2"][l])
                n_last = BANK_AT[f"w_in{l}"] + 20
                sp.wait_ge(*released[0])
                sp.dma_start(ring[0][:, 0:2048].rearrange("p (k n) -> p k n", k=KT),
                             a["w_in_2"][l][:, 5120:5376].rearrange("(k p) n -> p k n", p=P)).then_inc(slot_full[0], 16)
                released[0] = (bank_full[n_last % BANKS], n_last // BANKS + 1)
                last_small = BANK_AT["rg_gates"] + 3 if l == 0 else BANK_AT["route0"] + 1
                sp.wait_ge(bank_full[last_small % BANKS], filled(last_small))
                sp.dma_start(small_w[0:64, 0:512], a["rwkv_w_lora_2"][l]).then_inc(sems["small_loaded"], 16)
                sp.dma_start(small_w[64:128, 0:512], a["rwkv_a_lora_2"][l]).then_inc(sems["small_loaded"], 16)
                sp.dma_start(small_w[:, 512:1024], a["rwkv_g_lora_2"][l]).then_inc(sems["small_loaded"], 16)
                lin8(f"w_gate{l}", a["w_gate_2"][l])
                stream(f"w_branch{l}", lambda i, j: [(ring[j][:].rearrange("p (k n) -> p k n", k=4),
                                                      a["w_branch_2"][l, j].rearrange("(k p) n -> p k n", p=P))],
                       [("bank", 3, 1), ("bank", 7, 1), ("bank", 11, 1)])
                lin8(f"w_o{l}", a["w_o_2"][l])
                sp.wait_ge(bank_full[(BANK_AT[f"lora{l}"] + 5) % BANKS], filled(BANK_AT[f"lora{l}"] + 5))
                sp.dma_start(small_w[:, 0:288].rearrange("p (k n) -> p k n", k=KT)[:, :, 0:4],
                             a["w_router_group_2"][l].rearrange("(k p) n -> p k n", p=P)).then_inc(sems["small_loaded"], 16)
                sp.dma_start(small_w[:, 0:288].rearrange("p (k n) -> p k n", k=KT)[:, :, 4:36],
                             a["w_router_expert_2"][l].rearrange("(k p) n -> p k n", p=P)).then_inc(sems["small_loaded"], 16)
                sp.dma_start(small_w[0:1, 288:292], a["b_router_group_2"][l:l + 1]).then_inc(sems["small_loaded"], 16)
                sp.dma_start(small_w[0:1, 292:324], a["b_router_expert_2"][l:l + 1]).then_inc(sems["small_loaded"], 16)
                wg, wu, wdn = a["w_exp_gate_2"][l], a["w_exp_up_2"][l], a["w_exp_down_2"][l]

                def moe_src(i, j):
                    s = SLOT_AT[f"moe{l}"][j][0]
                    w = (wg, wu, wdn)[j][bass.ds(i, 1)]
                    k = (KT, KT, 4)[j]
                    return [(ring[s][:].rearrange("p (k n) -> p k n", k=k), w.rearrange("o (k p) n -> p (o k) n", p=P))]
                stream(f"moe{l}", moe_src, [("bank", 3, 1), ("bank", 3, 1), ("down", 0, 1)])
            for m in range(BANK_AT["x_out"], BANK_AT["x_out"] + 4):
                sp.wait_ge(bank_read[m % BANKS], filled(m))
            sp.dma_start(out[0].rearrange("(t p) d -> p t d", p=P), R[:].rearrange("p (t k) s -> p t (k s)", t=TT)).then_inc(sems["out_stored"], 16)
            sp.wait_ge(sems["out_stored"], 16)

        @block.tensor
        def _(pe):
            L = Count()
            mm = nc.tensor.matmul
            used = [0]

            def mul(o, lhsT, rhs, first=True, last=True, **kw):
                return mm(o, lhsT=lhsT, rhs=rhs, start=first, stop=last, **kw)

            def slot(s, k, n=None):
                n = n or SLOT // k
                return ring[s][:, 0:k * n].rearrange("p (k n) -> p k n", k=k)

            def pair(n, lhs, rhs, K, i=0, w=S, rows=slice(0, P)):
                pe.wait_ge(bank_read[n % BANKS], emptied(n, i))
                for h in range(2):
                    for k in range(K):
                        ins = mul(bk(n)[rows, h * w:(h + 1) * w], lhs(h, k), rhs(k), k == 0, k == K - 1)
                ins.then_inc(bank_full[n % BANKS], 1)

            def lin8(name, rhs, w=S):
                n0, slots = BANK_AT[name], SLOT_AT[name]
                times = [t for n_, _, t in STREAM if n_ == name][0]

                def body(i):
                    for b, (s, u) in enumerate(slots):
                        pe.wait_ge(slot_full[s], loaded(u, i))
                        W = slot(s, KT)
                        for j in range(2):
                            pair(n0 + 2 * b + j, lambda h, k: W[:, k, (2 * j + h) * P:(2 * j + h + 1) * P], rhs,
                                 KT, i, w)
                if times > 1:
                    with nc.tensor.Fori(0, times) as i:
                        body(i)
                else:
                    body(0)

            def sums(src, k0, K):
                for k in range(K):
                    ins = mul(acc[3][:, 0:S], C("ones"), src[:, k0 + k, :], k == 0, k == K - 1)
                ins.then_inc(sems["norm_sum"], 1)

            def layer_norm():
                sums(R, 0, KT)
                pe.wait_ge(sems["norm_sq"], L.nxt("norm_sq"))
                sums(SQ, 0, KT)

            def rms_norm(src=SQ, K=KT):
                pe.wait_ge(sems["norm_sq"], L.nxt("norm_sq"))
                sums(src, 0, K)

            def clear_acc():
                for b in range(4):
                    mul(acc[b][:, :], C("zeros")[0:1, :], C("causal")[0:1, 0:512], True, False, skip_group_check=True)

            def down(W, src, last_too):
                for kk in range(4):
                    if kk % last_too == 0:
                        yield kk
                    for m in range(KT):
                        ins = mul(acc[m // 2][:, (m % 2) * S:(m % 2 + 1) * S], W[:, kk, m * P:(m + 1) * P],
                                  src(kk), False, False, skip_group_check=True)
                ins.then_inc(sems["down_done"], 1)

            pe.wait_ge(sems["inputs_loaded"], 32)
            pe.wait_ge(sems["x_loaded"], L.nxt("x_loaded", 16))
            n0 = BANK_AT["x_in"]
            Rtok = R[:].rearrange("p (t k) s -> p t (k s)", t=TT)
            for j in range(4):
                for h in range(2):
                    for tt in range(TT):
                        ins = nc.tensor.transpose(bk(n0 + j)[:, h * S + tt * P:h * S + (tt + 1) * P],
                                                  Rtok[:, tt, (2 * j + h) * P:(2 * j + h + 1) * P], C("ident"))
                ins.then_inc(bank_full[(n0 + j) % BANKS], 1)
            for m in range(n0, n0 + 4):
                pe.wait_ge(bank_read[m % BANKS], filled(m))

            n0 = BANK_AT["hy_in"]
            for b in range(4):
                pe.wait_ge(slot_full[b % 2], loaded(b // 2))
                if b == 3:
                    pe.wait_ge(sems["tail_loaded"], L.nxt("tail_loaded", 64))
                W = slot(b % 2, KT)
                for j in range(2):
                    pair(n0 + 2 * b + j, lambda h, k: W[:, k, (2 * j + h) * P:(2 * j + h + 1) * P],
                         lambda k: xT[:, k, :], KT)
            pe.wait_ge(sems["kvw_loaded"], L.nxt("kvw_loaded", 32))
            n = BANK_AT["dsa_v"]
            pe.wait_ge(bank_read[n % BANKS], emptied(n))
            kvw = flat(GT[:, 20:24, :])[:, 0:KT * 68].rearrange("p (k n) -> p k n", k=KT)
            for tt in range(TT):
                for k in range(KT):
                    ins = mul(bk(n)[:, tt * 68:(tt + 1) * 68], xT[:, k, tt * P:(tt + 1) * P], kvw[:, k, :],
                              k == 0, k == KT - 1)
            ins.then_inc(bank_full[n % BANKS], 1)
            pe.wait_ge(sems["small_loaded"], L.nxt("small_loaded", 16))
            pe.wait_ge(sems["conv_done"], L.nxt("conv_done"))
            n0 = BANK_AT["rg_gates"]
            for g in range(2):
                for j in range(2):
                    n = n0 + 2 * g + j
                    pe.wait_ge(bank_read[n % BANKS], emptied(n))
                    for h in range(2):
                        c = 2 * j + h
                        ins = mul(bk(n)[:, h * S:(h + 1) * S], small_w[:, g * 512 + c * P:g * 512 + (c + 1) * P],
                                  PR[:, XC + c, :])
                    ins.then_inc(bank_full[n % BANKS], 1)
            for m in range(BANK_AT["hy_in"] + 4, BANK_AT["hy_in"] + 8):
                pe.wait_ge(bank_read[m % BANKS], filled(m))
            n0 = BANK_AT["idx"]
            for tt in range(TT):
                for j in range(2):
                    n = n0 + 2 * tt + j
                    pe.wait_ge(bank_read[n % BANKS], emptied(n))
                    for h in range(2):
                        half = slice(64 * h, 64 * h + 64)
                        ins = mul(bk(n)[:, h * S:(h + 1) * S], PR[half, IQ + j, tt * P:(tt + 1) * P], PR[half, IK, :])
                        if h == 0:
                            ins.then_inc(sems["pe_chain"], 1)
                            pe.wait_ge(sems["pe_chain"], L.up())
                    ins.then_inc(bank_full[n % BANKS], 1)

            def attention(name, pairs, q, k, v):
                n0 = BANK_AT[name]

                def logits(hp):
                    for tt in range(TT):
                        n = order[("l", hp, tt)]
                        pe.wait_ge(bank_read[n % BANKS], emptied(n))
                        for h in range(2):
                            ins = mul(bk(n)[:, h * S:(h + 1) * S], q(hp, h, tt), k(hp, h))
                            if h == 0 and name == "dsa":
                                ins.then_inc(sems["pe_chain"], 1)
                                pe.wait_ge(sems["pe_chain"], L.up())
                        ins.then_inc(bank_full[n % BANKS], 1)

                def output(hp):
                    pe.wait_ge(sems["dsa_probs"], L.nxt("dsa_probs"))
                    for h in range(2):
                        n = order[("t", hp, h)]
                        pe.wait_ge(bank_read[n % BANKS], emptied(n))
                        for kt in range(TT):
                            for tt in range(TT):
                                ins = nc.tensor.transpose(
                                    bk(n)[:, kt * S + tt * P:kt * S + (tt + 1) * P],
                                    LG[:, (hp % 2) * 4 + tt * 2 + h, kt * P:(kt + 1) * P], C("ident"))
                        ins.then_inc(bank_full[n % BANKS], 1)
                    n = order[("o", hp, 0)]
                    pe.wait_ge(bank_read[n % BANKS], emptied(n))
                    for h in range(2):
                        pe.wait_ge(bank_read[(order[("t", hp, h)]) % BANKS], filled(order[("t", hp, h)]))
                        for kt in range(TT):
                            ins = mul(bk(n)[64 * h:64 * h + 64, 0:S], v(hp, h, kt), PTB[:, 2 * h + kt, :],
                                      kt == 0, kt == TT - 1)
                    ins.then_inc(bank_full[n % BANKS], 1)
                order = attention_order(n0, pairs)
                for hp in range(pairs + 1):
                    if hp < pairs:
                        logits(hp)
                    if hp:
                        output(hp - 1)

            def lin_out(name, mixer, pairs):
                pe.wait_ge(bank_read[(attention_order(BANK_AT[mixer], pairs)["o", pairs - 1, 0]) % BANKS], filled(attention_order(BANK_AT[mixer], pairs)["o", pairs - 1, 0]))
                lin8(name, lambda k: MIX[:, k, :])
                for m in range(BANK_AT[name], BANK_AT[name] + 4):
                    pe.wait_ge(bank_read[m % BANKS], filled(m))

            def ffn_and_ple(l):
                layer_norm()
                pe.wait_ge(sems["p_loaded"], L.nxt("p_loaded", 16))
                n = BANK_AT[f"p_in{l}"]
                pe.wait_ge(bank_read[n % BANKS], emptied(n))
                for f in range(2):
                    for tt in range(TT):
                        ins = nc.tensor.transpose(bk(n)[:, f * S + tt * P:f * S + (tt + 1) * P],
                                                  pin[:, tt, f * P:(f + 1) * P], C("ident"))
                ins.then_inc(bank_full[n % BANKS], 1)
                pe.wait_ge(sems["norm_out"], L.nxt("norm_out"))
                clear_acc()
                nm = f"mlp{l}"
                n0, slots = BANK_AT[nm], SLOT_AT[nm]
                base = L.seen.get("ff_act", 0)
                with nc.tensor.Fori(0, 4) as i:
                    for c in range(2):
                        s, u = slots[2 * c]
                        pe.wait_ge(slot_full[s], loaded(u, i))
                        for j in range(2):
                            W = slot(s, KT)
                            pair(n0 + 2 * c + j, lambda h, k: W[:, k, (2 * j + h) * P:(2 * j + h + 1) * P],
                                 lambda k: hT[:, k, :], KT, i)
                        s, u = slots[2 * c + 1]
                        pe.wait_ge(slot_full[s], loaded(u, i))
                        for kk in down(slot(s, 4), lambda kk: FF[:, 4 * c + kk, :], 2):
                            pe.wait_ge(sems["ff_act"], i * 4 + (base + 2 * c + kk // 2 + 1))
                L.seen["ff_act"] = base + 16
                lin8(f"ple_gate{l}", lambda k: hT[:, k, :])
                s, u = SLOT_AT[f"ple_proj{l}"][0]
                pe.wait_ge(slot_full[s], loaded(u))
                pe.wait_ge(bank_read[(BANK_AT[f"p_in{l}"]) % BANKS], filled(BANK_AT[f"p_in{l}"]))
                W = slot(s, 2, D)
                for j in range(4):
                    pair(BANK_AT[f"ple_proj{l}"] + j, lambda h, k: W[:, k, (2 * j + h) * P:(2 * j + h + 1) * P],
                         lambda k: pT[:, k, :], 2)
                pe.wait_ge(sems["norm_in"], L.nxt("norm_in"))
                layer_norm()
                pe.wait_ge(sems["norm_out"], L.nxt("norm_out"))

            pe.wait_ge(bank_read[(BANK_AT["dsa_v"]) % BANKS], filled(BANK_AT["dsa_v"]))
            attention("dsa", 4, lambda hp, h, tt: PR[64 * h:64 * h + 64, Q0 + hp, tt * P:(tt + 1) * P],
                      lambda hp, h: PR[64 * h:64 * h + 64, KD, :], lambda hp, h, kt: vi(kt, 0, 64))
            lin_out("hy_out", "dsa", 4)
            ffn_and_ple(0)

            n0 = BANK_AT["mla_down"]
            (s0, u0), (s1, u1) = SLOT_AT["mla_down"]
            pe.wait_ge(slot_full[s0], loaded(u0))
            W0, W1 = slot(s0, KT), slot(s1, KT)
            for j in range(2):
                pair(n0 + j, lambda h, k: W0[:, k, (2 * j + h) * P:(2 * j + h + 1) * P], lambda k: xT[:, k, :], KT)
            pe.wait_ge(slot_full[s1], loaded(u1))
            pair(n0 + 2, lambda h, k: W1[:, k, h * P:(h + 1) * P], lambda k: xT[:, k, :], KT)
            pe.wait_ge(bank_read[(n0 + 3) % BANKS], emptied(n0 + 3))
            for k in range(KT):
                ins = mul(bk(n0 + 3)[64:96, 0:S], W1[:, k, 256:288], xT[:, k, :], k == 0, k == KT - 1)
            ins.then_inc(bank_full[(n0 + 3) % BANKS], 1)
            rms_norm(SQ[:, 0:4, :], 4)
            rms_norm(SQ[:, 4:6, :], 2)
            pe.wait_ge(sems["norm_out"], L.nxt("norm_out"))
            n0 = BANK_AT["mla_uq"]
            for b, (s, u) in enumerate(SLOT_AT["mla_uq"]):
                pe.wait_ge(slot_full[s], loaded(u))
                W = slot(s, 4, 768)
                for j in range(4):
                    pair(n0 + 4 * b + j, lambda h, k: W[:, k, (2 * j + h) * 96:(2 * j + h + 1) * 96],
                         lambda k: CQ[:, k, :], 4, rows=slice(0, 96))
            n0 = BANK_AT["mla_rope"]
            pe.wait_ge(bank_read[(BANK_AT["mla_down"] + 3) % BANKS], filled(BANK_AT["mla_down"] + 3))
            pe.wait_ge(bank_read[n0 % BANKS], emptied(n0))
            mul(bk(n0)[64:96, 0:S], C("swap_rope")[64:96, 64:96], KRAW[64:96, :]).then_inc(bank_full[n0 % BANKS], 1)
            for j in range(8):
                n = n0 + 1 + j
                pe.wait_ge(bank_read[(BANK_AT["mla_uq"] + j) % BANKS], filled(BANK_AT["mla_uq"] + j))
                pe.wait_ge(bank_read[n % BANKS], emptied(n))
                mul(bk(n)[0:96, :], C("swap_rope")[0:96, 0:96], flat(QH[0:96, 2 * j:2 * j + 2, :])).then_inc(bank_full[n % BANKS], 1)
            pe.wait_ge(sems["norm_out"], L.nxt("norm_out"))
            s, u = SLOT_AT["mla_ukv"][0]
            pe.wait_ge(slot_full[s], loaded(u))
            W = slot(s, 2, 2048)
            for j in range(8):
                pair(BANK_AT["mla_k"] + j, lambda h, k: W[:, k, (2 * j + h) * P:(2 * j + h) * P + 64],
                     lambda k: CQ[:, 4 + k, :], 2, rows=slice(0, 64))
            Wv = W.rearrange("p k (h c) -> p k h c", h=MLA_H)
            for tt in range(TT):
                for j in range(2):
                    n = BANK_AT["mla_v"] + 2 * tt + j
                    pe.wait_ge(bank_read[n % BANKS], emptied(n))
                    for k in range(2):
                        ins = mul(bk(n)[:, :], CQ[:, 4 + k, tt * P:(tt + 1) * P], Wv[:, k, 8 * j:8 * j + 8, 64:128],
                                  k == 0, k == 1)
                    ins.then_inc(bank_full[n % BANKS], 1)
            pe.wait_ge(sems["q_roped"], L.nxt("q_roped"))
            pe.wait_ge(sems["kr_spread"], L.nxt("kr_spread"))
            for m in range(BANK_AT["mla_k"] + 4, BANK_AT["mla_k"] + 8):
                pe.wait_ge(bank_read[m % BANKS], filled(m))
            for m in range(BANK_AT["mla_v"], BANK_AT["mla_v"] + 4):
                pe.wait_ge(bank_read[m % BANKS], filled(m))
            vh = flat(VH)
            attention("mla", 8, lambda hp, h, tt: QH[0:96, 2 * hp + h, tt * P:(tt + 1) * P],
                      lambda hp, h: KH[0:96, 2 * hp + h, :],
                      lambda hp, h, kt: vh[:, kt * D + (2 * hp + h) * 64:kt * D + (2 * hp + h + 1) * 64])
            lin_out("mla_out", "mla", 8)
            ffn_and_ple(1)

            for l in range(DEPTH):
                if l == 0:
                    pe.wait_ge(sems["c_silu"], L.nxt("c_silu"))
                lin8(f"ada{l}", lambda k: sm[:, k:k + 1], 1)
                rms_norm()
                pe.wait_ge(sems["norm_out"], L.nxt("norm_out"))
                lin8(f"w_in{l}", lambda k: hT[:, k, :])
                s, u = SLOT_AT[f"w_in_last{l}"][0]
                pe.wait_ge(slot_full[s], loaded(u))
                W = slot(s, KT, 256)
                n0 = BANK_AT[f"w_in{l}"]
                pair(n0 + 20, lambda h, k: W[:, k, h * P:(h + 1) * P], lambda k: hT[:, k, :], KT)
                for m in range(n0 + 17, n0 + 21):
                    pe.wait_ge(bank_read[m % BANKS], filled(m))
                for j in range(4):
                    n = BANK_AT[f"rot{l}"] + j
                    pe.wait_ge(bank_read[n % BANKS], emptied(n))
                    mul(bk(n)[:, :], C("swap"), flat(PR[:, 2 * j:2 * j + 2, :])).then_inc(bank_full[n % BANKS], 1)
                n0 = BANK_AT[f"ret_t{l}"]
                for c in range(TT):
                    pe.wait_ge(bank_read[(n0 + c) % BANKS], emptied(n0 + c))
                    for m in range(4):
                        ins = nc.tensor.transpose(bk(n0 + c)[:, m * P:(m + 1) * P], PR[:, 8 + m, c * P:(c + 1) * P],
                                                  C("ident"))
                    ins.then_inc(bank_full[(n0 + c) % BANKS], 1)
                pe.wait_ge(sems["ret_kq"], L.nxt("ret_kq"))
                pe.wait_ge(bank_read[(n0 + 2) % BANKS], emptied(n0 + 2))
                for m in range(4):
                    ins = nc.tensor.transpose(bk(n0 + 2)[:, m * P:(m + 1) * P], PR[:, 4 + m, 0:P], C("ident"))
                ins.then_inc(bank_full[(n0 + 2) % BANKS], 1)
                n0 = BANK_AT[f"ret{l}"]
                for c in range(TT):
                    pe.wait_ge(bank_read[(n0 + c) % BANKS], emptied(n0 + c))
                    for h in range(RET_H):
                        ins = mul(bk(n0 + c)[:, h * P:(h + 1) * P], PR[:, 4 + h, c * P:(c + 1) * P],
                                  PR[:, h, c * P:(c + 1) * P])
                    ins.then_inc(bank_full[(n0 + c) % BANKS], 1)
                VT, KTD, ST, QD, STATE, RY = (flat(GT[:, x:y, :]) for x, y in
                                              ((4, 8), (8, 10), (10, 14), (14, 16), (16, 18), (18, 22)))
                for m in range(BANK_AT[f"ret_t{l}"], BANK_AT[f"ret_t{l}"] + 3):
                    pe.wait_ge(bank_read[m % BANKS], filled(m))
                pe.wait_ge(bank_read[(n0 + 2) % BANKS], emptied(n0 + 2))
                for h in range(RET_H):
                    ins = mul(bk(n0 + 2)[:, h * P:(h + 1) * P], KTD[:, h * P:(h + 1) * P], VT[:, h * P:(h + 1) * P])
                ins.then_inc(bank_full[(n0 + 2) % BANKS], 1)
                for c in range(TT):
                    pe.wait_ge(bank_read[(n0 + c) % BANKS], filled(n0 + c))
                    if c:
                        pe.wait_ge(bank_read[(n0 + 2) % BANKS], filled(n0 + 2))
                    pe.wait_ge(bank_read[(n0 + 3 + c) % BANKS], emptied(n0 + 3 + c))
                    for h in range(RET_H):
                        hs = slice(h * P, (h + 1) * P)
                        ins = mul(bk(n0 + 3 + c)[:, hs], ST[:, c * 512 + h * P:c * 512 + (h + 1) * P],
                                  VT[:, c * 512 + h * P:c * 512 + (h + 1) * P], True, c == 0)
                        if c:
                            ins = mul(bk(n0 + 3 + c)[:, hs], QD[:, hs], STATE[:, hs], False, True)
                    ins.then_inc(bank_full[(n0 + 3 + c) % BANKS], 1)
                for c in range(TT):
                    pe.wait_ge(sems["ret_norm"], L.nxt("ret_norm"))
                    pe.wait_ge(bank_read[(n0 + 5 + c) % BANKS], emptied(n0 + 5 + c))
                    for h in range(RET_H):
                        ins = nc.tensor.transpose(bk(n0 + 5 + c)[:, h * P:(h + 1) * P],
                                                  RY[:, c * 512 + h * P:c * 512 + (h + 1) * P], C("ident"))
                    ins.then_inc(bank_full[(n0 + 5 + c) % BANKS], 1)

                pe.wait_ge(sems["small_loaded"], L.nxt("small_loaded", 48))
                pe.wait_ge(sems["lora_in"], L.nxt("lora_in", 2))
                n0 = BANK_AT[f"lora{l}"]
                for g in range(3):
                    rows = (slice(0, 64), slice(64, 128), slice(0, 128))[g]
                    w = small_w[rows, 512:1024] if g == 2 else small_w[rows, 0:512]
                    for j in range(2):
                        n = n0 + 2 * g + j
                        pe.wait_ge(bank_read[n % BANKS], emptied(n))
                        for h in range(2):
                            ins = mul(bk(n)[:, h * S:(h + 1) * S], w[:, (2 * j + h) * P:(2 * j + h + 1) * P],
                                      PR[rows, 28 if g < 2 else 29, :])
                        ins.then_inc(bank_full[n % BANKS], 1)
                n0 = BANK_AT[f"head_sum{l}"]
                for g in range(2):
                    pe.wait_ge(sems[("kk_sq", "rw_bonus")[g]], L.nxt(("kk_sq", "rw_bonus")[g]))
                    src = (HI[:, 0:4, :], HI[:, 0:4, :])[g]
                    for j in range(2):
                        n = n0 + 2 * g + j
                        pe.wait_ge(bank_read[n % BANKS], emptied(n))
                        mul(bk(n)[:, :], C("head_ones"), flat(src[:, 2 * j:2 * j + 2, :])).then_inc(bank_full[n % BANKS], 1)
                pe.wait_ge(sems["rw_ops"], L.nxt("rw_ops"))
                n0 = BANK_AT[f"rw_t{l}"]
                for q, (src, c) in enumerate(((PR[:, 24:28, :], 0), (PR[:, 24:28, :], 1), (BT_, 0), (KT_, 0))):
                    pe.wait_ge(bank_read[(n0 + q) % BANKS], emptied(n0 + q))
                    for m in range(4):
                        ins = nc.tensor.transpose(bk(n0 + q)[:, m * P:(m + 1) * P], src[:, m, c * P:(c + 1) * P],
                                                  C("ident"))
                    ins.then_inc(bank_full[(n0 + q) % BANKS], 1)
                n = BANK_AT[f"rwkv{l}"]

                def heads(n, a_, b_, c):
                    for g in range(2):
                        pe.wait_ge(bank_read[(n + g) % BANKS], emptied(n + g))
                        for q in (0, 2, 1, 3):
                            h = 4 * g + q
                            half = slice(64 * (h % 2), 64 * (h % 2) + 64)
                            ins = mul(bk(n + g)[:, q * P:(q + 1) * P], a_[half, h // 2, c * P:(c + 1) * P],
                                      b_[half, h // 2, c * P:(c + 1) * P])
                            if q == 2:
                                ins.then_inc(sems["pe_chain"], 1)
                                pe.wait_ge(sems["pe_chain"], L.up())
                        ins.then_inc(bank_full[(n + g) % BANKS], 1)
                    return n + 2

                def square(n, a_, b_):
                    for g in range(2):
                        pe.wait_ge(bank_read[(n + g) % BANKS], emptied(n + g))
                        for q in range(4):
                            hs = slice((4 * g + q) * P, (4 * g + q + 1) * P)
                            ins = mul(bk(n + g)[:, q * P:(q + 1) * P], a_[:, hs], b_[:, hs])
                        ins.then_inc(bank_full[(n + g) % BANKS], 1)
                    return n + 2

                for c in range(TT):
                    m0 = n
                    n = heads(n, BT_, AT_, c)
                    n = heads(n, KT_, AT_, c)
                    n = heads(n, BT_, RT_, c)
                    n = heads(n, KT_, RT_, c)
                    pe.wait_ge(sems["x_new"], L.nxt("x_new"))
                    for lev in range(7):
                        pe.wait_ge(sems["mm_mask"], L.nxt("mm_mask"))
                        n = square(n, MMs[lev % 2], Xm)
                        pe.wait_ge(bank_read[(n - 2) % BANKS], filled(n - 2))
                        pe.wait_ge(bank_read[(n - 1) % BANKS], filled(n - 1))
                        n = square(n, XTm, Tm)
                        n = square(n, Tm, XTm)
                        pe.wait_ge(bank_read[(n - 4) % BANKS], filled(n - 4))
                        pe.wait_ge(bank_read[(n - 3) % BANKS], filled(n - 3))
                        pe.wait_ge(bank_read[(n - 2) % BANKS], filled(n - 2))
                        pe.wait_ge(bank_read[(n - 1) % BANKS], filled(n - 1))
                    if c == 0:
                        for m in range(BANK_AT[f"rw_t{l}"], BANK_AT[f"rw_t{l}"] + 4):
                            pe.wait_ge(bank_read[m % BANKS], filled(m))
                    def from_state(n, a_, ins):
                        for par in range(2):
                            ins.then_inc(sems["pe_chain"], 1)
                            pe.wait_ge(sems["pe_chain"], L.up())
                            for h in range(par, RW_H, 2):
                                half = slice(64 * par, 64 * par + 64)
                                ins = mul(bk(n)[:, h * 64:h * 64 + 64], a_[half, h // 2, P:2 * P],
                                          S1[half, (h // 2) * 64:(h // 2) * 64 + 64], False, False, skip_group_check=True)
                        return ins

                    pe.wait_ge(bank_read[n % BANKS], emptied(n))
                    for h in range(RW_H):
                        ins = mul(bk(n)[:, h * 64:h * 64 + 64], NTm[:, h * P:(h + 1) * P],
                                  VT2[:, c * 512 + h * 64:c * 512 + h * 64 + 64], h == 0, False, skip_group_check=True)
                    if c:
                        ins = from_state(n, AT_, ins)
                    ins.then_inc(bank_full[n % BANKS], 1)
                    pe.wait_ge(bank_read[n % BANKS], filled(n))
                    n += 1
                    pe.wait_ge(bank_read[n % BANKS], emptied(n))
                    for h in range(RW_H):
                        ins = mul(bk(n)[:, h * 64:h * 64 + 64], XTm[:, h * P:(h + 1) * P], Zm[:, h * 64:h * 64 + 64])
                    ins.then_inc(bank_full[n % BANKS], 1)
                    pe.wait_ge(bank_read[n % BANKS], filled(n))
                    n += 1
                    pe.wait_ge(bank_read[n % BANKS], emptied(n))
                    for h in range(RW_H):
                        o, hp = slice(h * 64, h * 64 + 64), slice(h * P, (h + 1) * P)
                        mul(bk(n)[:, o], RBm[:, hp], Um[:, o], h == 0, False, skip_group_check=True)
                        ins = mul(bk(n)[:, o], RKm[:, hp], VT2[:, c * 512 + h * 64:c * 512 + h * 64 + 64], False, False,
                                  skip_group_check=True)
                    if c:
                        ins = from_state(n, RT_, ins)
                    ins.then_inc(bank_full[n % BANKS], 1)
                    n += 1
                    if c == 0:
                        pe.wait_ge(bank_read[n % BANKS], emptied(n))
                        for h in range(RW_H):
                            half, o = slice(64 * (h % 2), 64 * (h % 2) + 64), slice(h * 64, h * 64 + 64)
                            so = slice((h // 2) * 64, (h // 2) * 64 + 64)
                            mul(bk(n)[half, so], BT0[:, o], Um[:, o], True, False)
                            ins = mul(bk(n)[half, so], KT0[:, o], VT2[:, o], False, True)
                        ins.then_inc(bank_full[n % BANKS], 1)
                        pe.wait_ge(bank_read[n % BANKS], filled(n))
                        n += 1
                    pe.wait_ge(sems["rw_norm"], L.nxt("rw_norm"))
                    pe.wait_ge(bank_read[n % BANKS], emptied(n))
                    for m in range(4):
                        ins = nc.tensor.transpose(bk(n)[:, m * P:(m + 1) * P], YC[:, m * P:(m + 1) * P], C("ident"))
                    ins.then_inc(bank_full[n % BANKS], 1)
                    n += 1
                assert n == BANK_AT[f"rwkv{l}"] + 2 * (8 + 7 * 6 + 4) + 1

                lin8(f"w_gate{l}", lambda k: hT[:, k, :])
                pe.wait_ge(sems["branch_done"], L.nxt("branch_done"))
                for i in range(3):
                    s, u = SLOT_AT[f"w_branch{l}"][i]
                    pe.wait_ge(slot_full[s], loaded(u))
                    W = slot(s, 4)
                    for j in range(4):
                        pair(BANK_AT[f"w_branch{l}"] + 4 * i + j, lambda h, k: W[:, k, (2 * j + h) * P:(2 * j + h + 1) * P],
                             lambda k: YB[:, 4 * i + k, :], 4)
                pe.wait_ge(sems["merged"], L.nxt("merged"))
                lin8(f"w_o{l}", lambda k: R[:, k, :])
                rms_norm()
                pe.wait_ge(sems["norm_out"], L.nxt("norm_out"))
                pe.wait_ge(sems["small_loaded"], L.nxt("small_loaded", 64))
                n0 = BANK_AT[f"route{l}"]
                wr = small_w[:, 0:288].rearrange("p (k n) -> p k n", k=KT)
                pe.wait_ge(bank_read[n0 % BANKS], emptied(n0))
                for tt in range(TT):
                    o = bk(n0)[:, tt * 36:(tt + 1) * 36]
                    mul(o, C("ones")[0:1, :], small_w[0:1, 288:324], True, False)
                    for k in range(KT):
                        ins = mul(o, hT[:, k, tt * P:(tt + 1) * P], wr[:, k, :], False, k == KT - 1)
                ins.then_inc(bank_full[n0 % BANKS], 1)
                pe.wait_ge(sems["router_w"], L.nxt("router_w"))
                pe.wait_ge(bank_read[(n0 + 1) % BANKS], emptied(n0 + 1))
                for tt in range(TT):
                    ins = nc.tensor.transpose(bk(n0 + 1)[0:N_EXP, tt * P:(tt + 1) * P],
                                              sm[:, 256 + tt * 32:256 + (tt + 1) * 32], C("ident"))
                ins.then_inc(bank_full[(n0 + 1) % BANKS], 1)
                clear_acc()
                nm = f"moe{l}"
                n0, slots = BANK_AT[nm], SLOT_AT[nm]
                base = L.seen.get("moe_h", 0)
                with nc.tensor.Fori(0, N_EXP) as e:
                    (sg, ug), (su, uu), (sd, ud) = slots
                    pe.wait_ge(slot_full[sg], loaded(ug, e))
                    pe.wait_ge(slot_full[su], loaded(uu, e))
                    Wg, Wu = slot(sg, KT), slot(su, KT)
                    for f in range(4):
                        pair(n0 + f, lambda h, k: (Wg, Wu)[h][:, k, f * P:(f + 1) * P], lambda k: hT[:, k, :], KT, e)
                    pe.wait_ge(slot_full[sd], loaded(ud, e))
                    for kk in down(slot(sd, 4), lambda kk: FF[:, kk, :], 1):
                        pe.wait_ge(sems["moe_h"], e * 4 + (base + kk + 1))
                L.seen["moe_h"] = base + 4 * N_EXP
            rms_norm()
            pe.wait_ge(sems["norm_out"], L.nxt("norm_out"))
            n0 = BANK_AT["x_out"]
            for j in range(4):
                tt, q = j // 2, j % 2
                pe.wait_ge(bank_read[(n0 + j) % BANKS], emptied(n0 + j))
                for k in range(4):
                    ins = nc.tensor.transpose(bk(n0 + j)[:, k * P:(k + 1) * P], hT[:, 4 * q + k, tt * P:(tt + 1) * P],
                                              C("ident"))
                ins.then_inc(bank_full[(n0 + j) % BANKS], 1)

        CS, GA1, GA2 = 0, 8, 16
        IW, M8, MX, NB, RS = 24, 32, 48, 56, 64
        LAM, LIN = 72, 80
        CMID, CEND, CEXP, OMKA = 84, 92, 96, 100
        HS, HV = 104, 112
        RL, RT, R8 = 128, 200, 250
        CW = 256
        W2, W3 = 320, 384

        def layer_vec(name, k):
            return V_(name)[:, k:k + 1]

        @block.vector
        def _(dve):
            L = Count()
            v = nc.vector

            def copy_out(n, dst, src=None):
                dve.wait_ge(bank_full[n % BANKS], filled(n))
                v.tensor_copy(dst, bk(n)[:, :] if src is None else src).then_inc(bank_read[n % BANKS], 1)

            def stats(width, eps):
                dve.wait_ge(sems["norm_sum"], L.nxt("norm_sum"))
                v.tensor_scalar(stat[:, 1, :], acc[3][:, 0:S], 1.0 / width, eps, ALU.mult, ALU.add).then_inc(sems["norm_var"], 1)
                dve.wait_ge(sems["norm_std"], L.nxt("norm_std"))
                v.reciprocal(stat[:, 1, :], stat[:, 1, :]).then_inc(sems["vec_chain"], 1)
                dve.wait_ge(sems["vec_chain"], L.up())

            def layer_norm():
                dve.wait_ge(sems["norm_sum"], L.nxt("norm_sum"))
                v.tensor_scalar(stat[:, 0, :], acc[3][:, 0:S], 1.0 / D, None, ALU.mult).then_inc(sems["vec_chain"], 1)
                dve.wait_ge(sems["vec_chain"], L.up())
                v.tensor_tensor(R[:, :, :], R[:, :, :], bcast(stat[:, 0, :], KT), ALU.subtract).then_inc(sems["norm_centered"], 1)
                dve.wait_ge(sems["norm_centered"], L.nxt("norm_centered"))
                stats(D, 1e-5)
                v.tensor_tensor(R[:, :, :], R[:, :, :], bcast(stat[:, 1, :], KT), ALU.mult).then_inc(sems["norm_scaled"], 1)
                dve.wait_ge(sems["norm_out"], L.nxt("norm_out"))

            def rms_norm(src, dst, K, width):
                stats(width, 1e-6)
                v.tensor_tensor(dst, src, bcast(stat[:, 1, :], K), ALU.mult).then_inc(sems["norm_scaled"], 1)
                dve.wait_ge(sems["norm_out"], L.nxt("norm_out"))

            n0 = BANK_AT["x_in"]
            for j in range(4):
                copy_out(n0 + j, flat(xT[:, 2 * j:2 * j + 2, :]))
            dve.wait_ge(sems["inputs_loaded"], 32)
            lam = V_("lam")
            v.scalar_tensor_tensor(sm[:, LAM:LAM + 4], lam, -1.0, lam, ALU.mult, ALU.min).then_inc(sems["lam_abs"], 1)
            v.tensor_scalar(sm[:, LIN:LIN + 4], lam, -1.0, 0.0, ALU.mult, ALU.max).then_inc(sems["vec_chain"], 1)
            dve.wait_ge(sems["vec_chain"], L.up())
            dve.wait_ge(sems["lam_log"], L.nxt("lam_log"))
            v.tensor_tensor(sm[:, LIN:LIN + 4], sm[:, LIN:LIN + 4], sm[:, LAM:LAM + 4], ALU.add).then_inc(sems["vec_chain"], 1)
            dve.wait_ge(sems["vec_chain"], L.up())
            v.tensor_scalar(sm[:, LIN:LIN + 4], sm[:, LIN:LIN + 4], 4.0, None, ALU.mult).then_inc(sems["vec_chain"], 1)
            dve.wait_ge(sems["vec_chain"], L.up())

            n0 = BANK_AT["hy_in"]
            for j in range(0, 8, 2):
                copy_out(n0 + j, flat(PR[:, 2 * j:2 * j + 2, :]))
            n = BANK_AT["dsa_v"]
            dve.wait_ge(bank_full[n % BANKS], filled(n))
            v.tensor_copy(flat(VI)[:, 0:136], bk(n)[:, 0:136]).then_inc(bank_read[n % BANKS], 1)
            dve.wait_ge(bank_read[n % BANKS], filled(n))
            for tt in range(TT):
                v.tensor_scalar(sm[:, IW + 4 * tt:IW + 4 * tt + 4], vi(tt, 64, 68), IDX_H ** -0.5 * 64 ** -0.5, None, ALU.mult).then_inc(sems["vec_chain"], 1)
                dve.wait_ge(sems["vec_chain"], L.up())
            dve.wait_ge(bank_read[n0 % BANKS], filled(n0))
            dve.wait_ge(bank_read[(n0 + 1) % BANKS], filled(n0 + 1))
            for c in range(4):
                src, dst = PR[:, XR + c, :], PR[:, XC + c, :]
                v.tensor_scalar(dst, src, layer_vec("conv_w3", c), layer_vec("conv_b", c), ALU.mult, ALU.add).then_inc(sems["vec_chain"], 1)
                dve.wait_ge(sems["vec_chain"], L.up())
                for i in (2, 1, 0):
                    sh = 3 - i
                    ins = v.scalar_tensor_tensor(dst[:, sh:S], src[:, 0:S - sh], layer_vec(f"conv_w{i}", c), dst[:, sh:S],
                                                 ALU.mult, ALU.add)
                    if i == 0 and c == 3:
                        ins.then_inc(sems["conv_done"], 1)
                    else:
                        ins.then_inc(sems["vec_chain"], 1)
                        dve.wait_ge(sems["vec_chain"], L.up())
            dve.wait_ge(sems["conv_done"], L.nxt("conv_done"))
            yr, z = flat(PR[:, YR:YR + 4, :]), flat(R[:, 0:4, :])
            dve.wait_ge(bank_read[(n0 + 2) % BANKS], filled(n0 + 2))
            dve.wait_ge(bank_read[(n0 + 3) % BANKS], filled(n0 + 3))
            v.tensor_tensor(z, yr, yr, ALU.mult).then_inc(sems["vec_chain"], 1)
            dve.wait_ge(sems["vec_chain"], L.up())
            v.tensor_scalar(z, z, 0.044715, 1.0, ALU.mult, ALU.add).then_inc(sems["vec_chain"], 1)
            dve.wait_ge(sems["vec_chain"], L.up())
            v.tensor_tensor(z, z, yr, ALU.mult).then_inc(sems["gelu_in"], 1)
            g0 = BANK_AT["rg_gates"]
            dve.wait_ge(bank_read[g0 % BANKS], filled(g0))
            dve.wait_ge(bank_read[(g0 + 1) % BANKS], filled(g0 + 1))
            dve.wait_ge(bank_read[(g0 + 2) % BANKS], filled(g0 + 2))
            dve.wait_ge(bank_read[(g0 + 3) % BANKS], filled(g0 + 3))
            for c in range(4):
                ins = v.tensor_scalar(PR[:, RG + c, :], PR[:, RG + c, :], sm[:, LIN + c:LIN + c + 1], None, ALU.mult)
                if c < 3:
                    ins.then_inc(sems["vec_chain"], 1)
                    dve.wait_ge(sems["vec_chain"], L.up())
            ins.then_inc(sems["decay_in"], 1)
            xc, th, ig, den = (flat(q) for q in (PR[:, XC:XC + 4, :], PR[:, RG:RG + 4, :], PR[:, IG:IG + 4, :], R[:, 4:8, :]))
            v.tensor_tensor(ig, ig, xc, ALU.mult).then_inc(sems["vec_chain"], 1)
            dve.wait_ge(sems["vec_chain"], L.up())
            dve.wait_ge(sems["decay_tanh"], L.nxt("decay_tanh"))
            v.tensor_scalar(den, th, 1.0, None, ALU.add).then_inc(sems["decay_den"], 1)
            dve.wait_ge(sems["decay_den"], L.nxt("decay_den"))
            v.reciprocal(den, den).then_inc(sems["vec_chain"], 1)
            dve.wait_ge(sems["vec_chain"], L.up())
            v.tensor_tensor(ig, ig, den, ALU.mult).then_inc(sems["vec_chain"], 1)
            dve.wait_ge(sems["vec_chain"], L.up())
            dve.wait_ge(sems["decay_sqrt"], L.nxt("decay_sqrt"))
            v.scalar_tensor_tensor(ig, th, 2.0, ig, ALU.mult, ALU.mult).then_inc(sems["vec_chain"], 1)
            dve.wait_ge(sems["vec_chain"], L.up())
            v.tensor_scalar(den, den, 2.0, -1.0, ALU.mult, ALU.add).then_inc(sems["vec_chain"], 1)
            dve.wait_ge(sems["vec_chain"], L.up())
            for c in range(4):
                v.tensor_tensor_scan(PR[:, XC + c, :], R[:, 4 + c, :], PR[:, IG + c, :], 0.0, ALU.mult, ALU.add).then_inc(sems["vec_chain"], 1)
                dve.wait_ge(sems["vec_chain"], L.up())
            dve.wait_ge(sems["gelu_sig"], L.nxt("gelu_sig"))
            v.tensor_tensor(z, z, yr, ALU.mult).then_inc(sems["vec_chain"], 1)
            dve.wait_ge(sems["vec_chain"], L.up())
            v.tensor_tensor(flat(MIX[:, 0:4, :]), z, xc, ALU.mult).then_inc(sems["vec_chain"], 1)
            dve.wait_ge(sems["vec_chain"], L.up())
            i0 = BANK_AT["idx"]
            for m in range(i0, i0 + 4):
                dve.wait_ge(bank_read[m % BANKS], filled(m))
            for tt in range(TT):
                for h in range(IDX_H):
                    w = sm[:, IW + 4 * tt + h:IW + 4 * tt + h + 1]
                    if h == 0:
                        v.tensor_scalar(ISC[:, tt, :], RELU[:, 4 * tt, :], w, None, ALU.mult).then_inc(sems["vec_chain"], 1)
                        dve.wait_ge(sems["vec_chain"], L.up())
                    else:
                        v.scalar_tensor_tensor(ISC[:, tt, :], RELU[:, 4 * tt + h, :], w, ISC[:, tt, :], ALU.mult, ALU.add).then_inc(sems["vec_chain"], 1)
                        dve.wait_ge(sems["vec_chain"], L.up())
            isc, adm = flat(ISC), flat(ADM)
            v.tensor_tensor(isc, isc, C("causal"), ALU.mult).then_inc(sems["vec_chain"], 1)
            dve.wait_ge(sems["vec_chain"], L.up())
            v.tensor_tensor(isc, isc, C("noncausal"), ALU.add).then_inc(sems["vec_chain"], 1)
            dve.wait_ge(sems["vec_chain"], L.up())
            for _ in range(TOPK // 8):
                for tt in range(TT):
                    m8 = sm[:, M8 + 8 * tt:M8 + 8 * tt + 8]
                    v.max(m8, ISC[:, tt, :]).then_inc(sems["vec_chain"], 1)
                    dve.wait_ge(sems["vec_chain"], L.up())
                    v.match_replace(ISC[:, tt, :], m8, ISC[:, tt, :], TAKEN).then_inc(sems["vec_chain"], 1)
                    dve.wait_ge(sems["vec_chain"], L.up())
            v.tensor_scalar(adm, isc, -2e38, BIG, ALU.is_le, ALU.mult).then_inc(sems["vec_chain"], 1)
            dve.wait_ge(sems["vec_chain"], L.up())
            v.tensor_tensor(adm, adm, C("causal"), ALU.mult).then_inc(sems["vec_chain"], 1)
            dve.wait_ge(sems["vec_chain"], L.up())
            v.tensor_scalar(adm, adm, -BIG, None, ALU.add).then_inc(sems["vec_chain"], 1)
            dve.wait_ge(sems["vec_chain"], L.up())

            def attention(name, pairs, scale, mix0, slopes=None):
                order = attention_order(BANK_AT[name], pairs)

                def softmax(hp):
                    q = 4 * (hp % 2)
                    for tt in range(TT):
                        n = order["l", hp, tt]
                        dve.wait_ge(bank_full[n % BANKS], filled(n))
                        dst = LG[:, q + 2 * tt:q + 2 * tt + 2, :]
                        if slopes:
                            for h in range(2):
                                ins = v.scalar_tensor_tensor(dst[:, h, :], C("dist")[:, tt * S:(tt + 1) * S],
                                                             -slopes[2 * hp + h] / scale, bk(n)[:, h * S:(h + 1) * S],
                                                             ALU.mult, ALU.add)
                                if h:
                                    ins.then_inc(bank_read[n % BANKS], 1)
                                else:
                                    ins.then_inc(sems["vec_chain"], 1)
                                    dve.wait_ge(sems["vec_chain"], L.up())
                            dve.wait_ge(bank_read[n % BANKS], filled(n))
                            v.tensor_tensor(dst, dst, bcast(ADM[:, tt, :], 2), ALU.add).then_inc(sems["vec_chain"], 1)
                            dve.wait_ge(sems["vec_chain"], L.up())
                        else:
                            v.tensor_tensor(dst, two(bk(n)[:, :]), bcast(C("noncausal")[:, tt * S:(tt + 1) * S], 2), ALU.add).then_inc(bank_read[n % BANKS], 1)
                            dve.wait_ge(bank_read[n % BANKS], filled(n))
                    p_ = q
                    v.tensor_reduce(sm[:, MX + p_:MX + p_ + 4], LG[:, q:q + 4, :], AX.X, ALU.max).then_inc(sems["vec_chain"], 1)
                    dve.wait_ge(sems["vec_chain"], L.up())
                    v.tensor_scalar(sm[:, NB + p_:NB + p_ + 4], sm[:, MX + p_:MX + p_ + 4], -scale, None, ALU.mult).then_inc(sems["dsa_max"], 1)
                    dve.wait_ge(sems["dsa_exp"], L.nxt("dsa_exp"))
                    v.reciprocal(sm[:, RS + p_:RS + p_ + 4], sm[:, RS + p_:RS + p_ + 4]).then_inc(sems["vec_chain"], 1)
                    dve.wait_ge(sems["vec_chain"], L.up())
                    v.tensor_tensor(LG[:, q:q + 4, :], LG[:, q:q + 4, :],
                                        sm[:, RS + p_:RS + p_ + 4].unsqueeze(2).to_broadcast([P, 4, S]), ALU.mult).then_inc(sems["dsa_probs"], 1)

                for hp in range(pairs + 1):
                    if hp < pairs:
                        softmax(hp)
                    if hp:
                        n = order["o", hp - 1, 0]
                        dve.wait_ge(bank_full[n % BANKS], filled(n))
                        v.tensor_copy(MIX[:, mix0 + hp - 1, :], bk(n)[:, 0:S]).then_inc(bank_read[n % BANKS], 1)
                        dve.wait_ge(bank_read[n % BANKS], filled(n))

            def out_and_norm(name):
                for j in range(4):
                    n = BANK_AT[name] + j
                    dve.wait_ge(bank_full[n % BANKS], filled(n))
                    v.scalar_tensor_tensor(R[:, 2 * j:2 * j + 2, :], xT[:, 2 * j:2 * j + 2, :], ALPHA, two(bk(n)[:, :]),
                                                ALU.mult, ALU.add).then_inc(bank_read[n % BANKS], 1)
                for m in range(BANK_AT[name], BANK_AT[name] + 4):
                    dve.wait_ge(bank_read[m % BANKS], filled(m))
                layer_norm()

            def ffn_and_ple(l):
                dve.wait_ge(sems["down_done"], L.nxt("down_done", 8))
                for b in range(4):
                    ins = v.scalar_tensor_tensor(R[:, 2 * b:2 * b + 2, :], hT[:, 2 * b:2 * b + 2, :], ALPHA, two(acc[b][:, :]),
                                                 ALU.mult, ALU.add)
                    ins.then_inc(sems["vec_chain"], 1)
                    dve.wait_ge(sems["vec_chain"], L.up())
                g0, n0 = BANK_AT[f"ple_gate{l}"], BANK_AT[f"ple_proj{l}"]
                for j in range(4):
                    dve.wait_ge(bank_read[(g0 + j) % BANKS], filled(g0 + j))
                    dve.wait_ge(bank_full[(n0 + j) % BANKS], filled(n0 + j))
                    q = flat(SQ[:, 2 * j:2 * j + 2, :])
                    v.tensor_tensor(q, q, bk(n0 + j)[:, :], ALU.mult).then_inc(bank_read[(n0 + j) % BANKS], 1)
                for m in range(n0, n0 + 4):
                    dve.wait_ge(bank_read[m % BANKS], filled(m))
                v.tensor_tensor(flat(R[:, :, :]), flat(R[:, :, :]), flat(SQ[:, :, :]), ALU.add).then_inc(sems["norm_in"], 1)
                dve.wait_ge(sems["norm_in"], L.nxt("norm_in"))
                layer_norm()

            attention("dsa", 4, DSA_D ** -0.5, 4, [2.0 ** (-8.0 * (h + 1) / DSA_H) for h in range(DSA_H)])
            out_and_norm("hy_out")
            ffn_and_ple(0)

            n0 = BANK_AT["mla_down"]
            for j in range(3):
                copy_out(n0 + j, flat(CQ[:, 2 * j:2 * j + 2, :]))
            dve.wait_ge(bank_full[(n0 + 3) % BANKS], filled(n0 + 3))
            v.tensor_copy(KRAW[64:96, :], bk(n0 + 3)[64:96, 0:S]).then_inc(bank_read[(n0 + 3) % BANKS], 1)
            for m in range(n0, n0 + 4):
                dve.wait_ge(bank_read[m % BANKS], filled(m))
            rms_norm(CQ[:, 0:4, :], CQ[:, 0:4, :], 4, QL)
            rms_norm(CQ[:, 4:6, :], CQ[:, 4:6, :], 2, KVL)
            n0 = BANK_AT["mla_uq"]
            r0 = BANK_AT["mla_rope"]
            for j in range(0, 8, 2):
                dve.wait_ge(bank_full[(n0 + j) % BANKS], filled(n0 + j))
                v.tensor_copy(flat(QH[0:96, 2 * j:2 * j + 2, :]), bk(n0 + j)[0:96, :]).then_inc(bank_read[(n0 + j) % BANKS], 1)
            dve.wait_ge(bank_full[r0 % BANKS], filled(r0))
            v.tensor_tensor(R[64:96, 7, :], bk(r0)[64:96, 0:S], C("rope_sin")[64:96, :], ALU.mult).then_inc(bank_read[r0 % BANKS], 1)
            v.tensor_tensor(KROT[64:96, :], KRAW[64:96, :], C("rope_cos")[64:96, :], ALU.mult).then_inc(sems["vec_chain"], 1)
            dve.wait_ge(sems["vec_chain"], L.up())
            dve.wait_ge(bank_read[r0 % BANKS], filled(r0))
            v.tensor_tensor(KROT[64:96, :], KROT[64:96, :], R[64:96, 7, :], ALU.add).then_inc(sems["kr_rope"], 1)
            for j in range(8):
                n = r0 + 1 + j
                dve.wait_ge(bank_full[n % BANKS], filled(n))
                dve.wait_ge(bank_read[(n0 + j) % BANKS], filled(n0 + j))
                q, t_ = QH[0:96, 2 * j:2 * j + 2, :], R[0:96, 2 * (j % 2):2 * (j % 2) + 2, :]
                v.tensor_tensor(q, q, bcast(C("rope_cos")[0:96, :], 2), ALU.mult).then_inc(sems["vec_chain"], 1)
                dve.wait_ge(sems["vec_chain"], L.up())
                v.tensor_tensor(t_, two(bk(n)[0:96, :]), bcast(C("rope_sin")[0:96, :], 2), ALU.mult).then_inc(bank_read[n % BANKS], 1)
                dve.wait_ge(bank_read[n % BANKS], filled(n))
                ins = v.tensor_tensor(q, q, t_, ALU.add)
                if j < 7:
                    ins.then_inc(sems["vec_chain"], 1)
                    dve.wait_ge(sems["vec_chain"], L.up())
                else:
                    ins.then_inc(sems["q_roped"], 1)
            attention("mla", 8, (NOPE + ROPE) ** -0.5, 0)
            out_and_norm("mla_out")
            ffn_and_ple(1)

            dve.wait_ge(sems["c_sig"], L.nxt("c_sig"))
            v.tensor_tensor(sm[:, CS:CS + 8], sm[:, CS:CS + 8], V_("c"), ALU.mult).then_inc(sems["c_silu"], 1)
            dve.wait_ge(sems["pos_loaded"], 16)
            ang, red, tmp = R[:, 0, :], R[:, 1, :], R[:, 2, :]
            v.tensor_copy(ang, posi[:, :]).then_inc(sems["vec_chain"], 1)
            dve.wait_ge(sems["vec_chain"], L.up())
            v.tensor_scalar(ang, ang, C("inv_freq"), None, ALU.mult).then_inc(sems["vec_chain"], 1)
            dve.wait_ge(sems["vec_chain"], L.up())
            for q, (dst, shift) in enumerate(((sinT, 0.0), (cosT, 0.25))):
                v.tensor_scalar(tmp, ang, 1.0 / (2 * math.pi), shift, ALU.mult, ALU.add).then_inc(sems["vec_chain"], 1)
                dve.wait_ge(sems["vec_chain"], L.up())
                v.tensor_scalar(tmp, tmp, 12582912.0, None, ALU.add).then_inc(sems["vec_chain"], 1)
                dve.wait_ge(sems["vec_chain"], L.up())
                v.tensor_scalar(tmp, tmp, -12582912.0, None, ALU.add).then_inc(sems["vec_chain"], 1)
                dve.wait_ge(sems["vec_chain"], L.up())
                v.tensor_copy(red, ang).then_inc(sems["vec_chain"], 1)
                dve.wait_ge(sems["vec_chain"], L.up())
                for part in TWO_PI:
                    v.scalar_tensor_tensor(red, tmp, -part, red, ALU.mult, ALU.add).then_inc(sems["vec_chain"], 1)
                    dve.wait_ge(sems["vec_chain"], L.up())
                v.tensor_scalar(red, red, shift * 2 * math.pi, 3.1415925, ALU.add, ALU.min).then_inc(sems["vec_chain"], 1)
                dve.wait_ge(sems["vec_chain"], L.up())
                v.tensor_scalar(dst[:, :], red, -3.1415925, None, ALU.max).then_inc(sems["rot_in"], 1)
                dve.wait_ge(sems["rot_in"], L.nxt("rot_in"))
            dve.wait_ge(sems["rot_tables"], L.nxt("rot_tables", 2))
            v.tensor_scalar(sinT[:, :], sinT[:, :], C("sin_sign"), None, ALU.mult).then_inc(sems["vec_chain"], 1)
            dve.wait_ge(sems["vec_chain"], L.up())

            for l in range(DEPTH):
                m0 = 48 * l
                n0 = BANK_AT[f"ada{l}"]
                with nc.vector.Fori(0, 6) as i:
                    for j in range(4):
                        dve.wait_ge(bank_full[(n0 + j) % BANKS], filled(n0 + j, i))
                        v.tensor_copy(mod[:, bass.ds(i * 8 + (m0 + 2 * j), 2)], bk(n0 + j)[:, 0:2]).then_inc(bank_read[(n0 + j) % BANKS], 1)
                for m in range(n0 + 20, n0 + 24):
                    dve.wait_ge(bank_read[m % BANKS], filled(m))
                ml = mod[:, m0:m0 + 48]
                v.tensor_tensor(ml, ml, V_(f"b_ada{l}"), ALU.add).then_inc(sems["vec_chain"], 1)
                dve.wait_ge(sems["vec_chain"], L.up())
                for g, o in ((GA1, 8), (GA2, 32)):
                    v.tensor_scalar(sm[:, g:g + 8], ml[:, o:o + 8], 1.0, None, ALU.add).then_inc(sems["vec_chain"], 1)
                    dve.wait_ge(sems["vec_chain"], L.up())
                    nm = f"norm{1 if g == GA1 else 2}_g{l}"
                    ins = v.tensor_tensor(sm[:, g:g + 8], sm[:, g:g + 8], V_(nm), ALU.mult)
                    if g == GA1:
                        ins.then_inc(sems["vec_chain"], 1)
                        dve.wait_ge(sems["vec_chain"], L.up())
                ins.then_inc(sems["mod_done"], 1)
                rms_norm(xT[:, :, :], hT[:, :, :], KT, D)
                n0 = BANK_AT[f"w_in{l}"]
                with nc.vector.Fori(0, 5) as i:
                    for j in (0, 2):
                        dve.wait_ge(bank_full[(n0 + j) % BANKS], filled(n0 + j, i))
                        v.tensor_copy(PR[:, bass.ds(i * 8 + 2 * j, 2), :], two(bk(n0 + j)[:, :])).then_inc(bank_read[(n0 + j) % BANKS], 1)
                copy_out(n0 + 20, flat(PR[:, 40:42, :]))
                for m in range(n0 + 17, n0 + 21):
                    dve.wait_ge(bank_read[m % BANKS], filled(m))
                u, cv = PR[:, 30:34, :], R[:, 0:4, :]
                v.tensor_tensor(flat(u), flat(u), flat(PR[:, 38:42, :]), ALU.mult).then_inc(sems["vec_chain"], 1)
                dve.wait_ge(sems["vec_chain"], L.up())
                for c in range(4):
                    v.tensor_scalar(cv[:, c, :], u[:, c, :], layer_vec(f"cw{l}2", c), None, ALU.mult).then_inc(sems["vec_chain"], 1)
                    dve.wait_ge(sems["vec_chain"], L.up())
                    for i in (0, 1):
                        sh = 2 - i
                        v.scalar_tensor_tensor(cv[:, c, sh:S], u[:, c, 0:S - sh], layer_vec(f"cw{l}{i}", c),
                                                    cv[:, c, sh:S], ALU.mult, ALU.add).then_inc(sems["vec_chain"], 1)
                        dve.wait_ge(sems["vec_chain"], L.up())
                v.tensor_tensor(flat(YB[:, 8:12, :]), flat(cv), flat(PR[:, 34:38, :]), ALU.mult).then_inc(sems["vec_chain"], 1)
                dve.wait_ge(sems["vec_chain"], L.up())

                r0 = BANK_AT[f"rot{l}"]
                for j in range(4):
                    dve.wait_ge(bank_full[(r0 + j) % BANKS], filled(r0 + j))
                    q, t_ = PR[:, 2 * j:2 * j + 2, :], R[:, 4 + 2 * (j % 2):6 + 2 * (j % 2), :]
                    v.tensor_tensor(q, q, bcast(cosT[:, :], 2), ALU.mult).then_inc(sems["vec_chain"], 1)
                    dve.wait_ge(sems["vec_chain"], L.up())
                    v.tensor_tensor(t_, two(bk(r0 + j)[:, :]), bcast(sinT[:, :], 2), ALU.mult).then_inc(bank_read[(r0 + j) % BANKS], 1)
                    dve.wait_ge(bank_read[(r0 + j) % BANKS], filled(r0 + j))
                    ins = v.tensor_tensor(q, q, t_, ALU.add)
                    if j < 3:
                        ins.then_inc(sems["vec_chain"], 1)
                        dve.wait_ge(sems["vec_chain"], L.up())
                    else:
                        ins.then_inc(sems["ret_kq"], 1)
                        dve.wait_ge(sems["ret_kq"], L.nxt("ret_kq"))
                VT, KTD, ST, QD, STATE, RY = (flat(GT[:, x:y, :]) for x, y in
                                              ((4, 8), (8, 10), (10, 14), (14, 16), (16, 18), (18, 22)))
                h4 = lambda ap: ap.rearrange("p (h d) -> p h d", h=4)
                v.tensor_tensor(h4(QD), PR[:, 0:4, P:2 * P], h4(C("ret_decay_q")), ALU.mult).then_inc(sems["vec_chain"], 1)
                dve.wait_ge(sems["vec_chain"], L.up())
                n = BANK_AT[f"ret_t{l}"] + 2
                dve.wait_ge(bank_full[n % BANKS], filled(n))
                v.tensor_tensor(h4(KTD), h4(bk(n)[:, :]), C("ret_decay_k").unsqueeze(2).to_broadcast([P, 4, P]), ALU.mult).then_inc(bank_read[n % BANKS], 1)
                r0 = BANK_AT[f"ret{l}"]
                for c in range(TT):
                    dve.wait_ge(bank_full[(r0 + c) % BANKS], filled(r0 + c))
                    v.tensor_tensor(ST[:, c * 512:(c + 1) * 512], bk(r0 + c)[:, :], C("ret_decay_in"), ALU.mult).then_inc(bank_read[(r0 + c) % BANKS], 1)
                copy_out(r0 + 2, STATE)
                dve.wait_ge(sems["g_sig"], L.nxt("g_sig"))
                g_ = PR[:, 12:16, :]
                v.tensor_tensor(flat(g_), flat(g_), flat(GT[:, 0:4, :]), ALU.mult).then_inc(sems["vec_chain"], 1)
                dve.wait_ge(sems["vec_chain"], L.up())
                for c in range(4):
                    v.tensor_scalar(g_[:, c, :], g_[:, c, :], layer_vec(f"ret_gn{l}", c), None, ALU.mult).then_inc(sems["vec_chain"], 1)
                    dve.wait_ge(sems["vec_chain"], L.up())

                def head_norm(n, dst, sq, H, eps, name):
                    hd = lambda ap: ap.rearrange("p (h d) -> p h d", h=H)
                    W = 512 // H
                    mean, var = sm[:, HS:HS + H], sm[:, HV:HV + H]
                    dve.wait_ge(bank_full[n % BANKS], filled(n))
                    v.tensor_reduce(mean, hd(bk(n)[:, :]), AX.X, ALU.add).then_inc(sems["vec_chain"], 1)
                    dve.wait_ge(sems["vec_chain"], L.up())
                    v.tensor_scalar(mean, mean, 1.0 / W, None, ALU.mult).then_inc(sems["vec_chain"], 1)
                    dve.wait_ge(sems["vec_chain"], L.up())
                    v.tensor_tensor(hd(dst), hd(bk(n)[:, :]), mean.unsqueeze(2).to_broadcast([P, H, W]), ALU.subtract).then_inc(bank_read[n % BANKS], 1)
                    dve.wait_ge(bank_read[n % BANKS], filled(n))
                    v.tensor_tensor(sq, dst, dst, ALU.mult).then_inc(sems["vec_chain"], 1)
                    dve.wait_ge(sems["vec_chain"], L.up())
                    v.tensor_reduce(var, hd(sq), AX.X, ALU.add).then_inc(sems["vec_chain"], 1)
                    dve.wait_ge(sems["vec_chain"], L.up())
                    v.tensor_scalar(var, var, 1.0 / W, eps, ALU.mult, ALU.add).then_inc(sems["head_var"], 1)
                    dve.wait_ge(sems["head_std"], L.nxt("head_std"))
                    v.reciprocal(var, var).then_inc(sems["vec_chain"], 1)
                    dve.wait_ge(sems["vec_chain"], L.up())
                    v.tensor_tensor(hd(dst), hd(dst), var.unsqueeze(2).to_broadcast([P, H, W]), ALU.mult).then_inc(sems[name], 1)

                for c in range(TT):
                    head_norm(r0 + 3 + c, RY[:, c * 512:(c + 1) * 512], flat(R[:, 0:2, :]), RET_H, 1e-5, "ret_norm")
                for c in range(TT):
                    n = r0 + 5 + c
                    dve.wait_ge(bank_full[n % BANKS], filled(n))
                    ins = v.tensor_tensor(YB[:, 0:4, c * P:(c + 1) * P], h4(bk(n)[:, :]), g_[:, :, c * P:(c + 1) * P], ALU.mult)
                    ins.then_inc(bank_read[n % BANKS], 1)
                dve.wait_ge(bank_read[(r0 + 6) % BANKS], filled(r0 + 6))

                p_, d_ = PR[:, 16:30, :], PR[:, 0:14, :]
                v.tensor_tensor(d_[:, :, 1:S], p_[:, :, 0:S - 1], p_[:, :, 1:S], ALU.subtract).then_inc(sems["vec_chain"], 1)
                dve.wait_ge(sems["vec_chain"], L.up())
                v.tensor_scalar(d_[:, :, 0:1], p_[:, :, 0:1], -1.0, None, ALU.mult).then_inc(sems["vec_chain"], 1)
                dve.wait_ge(sems["vec_chain"], L.up())
                for t_ in (12, 13, *range(12)):
                    ins = v.scalar_tensor_tensor(p_[:, t_, :], d_[:, t_, :], layer_vec(f"mu{l}", t_), p_[:, t_, :], ALU.mult, ALU.add)
                    if t_ == 13:
                        ins.then_inc(sems["mixed"], 1)
                        dve.wait_ge(sems["mixed"], L.nxt("mixed"))
                    else:
                        ins.then_inc(sems["vec_chain"], 1)
                        dve.wait_ge(sems["vec_chain"], L.up())
                r_, k_, v_ = PR[:, 16:20, :], PR[:, 20:24, :], PR[:, 24:28, :]
                w_, aa = GT[:, 0:4, :], GT[:, 4:8, :]
                for c in range(4):
                    v.tensor_scalar(KKH[:, c, :], k_[:, c, :], layer_vec(f"k_k{l}", c), None, ALU.mult).then_inc(sems["vec_chain"], 1)
                    dve.wait_ge(sems["vec_chain"], L.up())
                v.tensor_tensor(flat(HI[:, 0:4, :]), flat(KKH), flat(KKH), ALU.mult).then_inc(sems["kk_sq"], 1)
                l0 = BANK_AT[f"lora{l}"]
                dve.wait_ge(bank_read[l0 % BANKS], filled(l0))
                dve.wait_ge(bank_read[(l0 + 1) % BANKS], filled(l0 + 1))
                dve.wait_ge(bank_read[(l0 + 2) % BANKS], filled(l0 + 2))
                dve.wait_ge(bank_read[(l0 + 3) % BANKS], filled(l0 + 3))
                v.tensor_scalar(flat(w_), flat(w_), -math.exp(-0.5), None, ALU.mult).then_inc(sems["vec_chain"], 1)
                dve.wait_ge(sems["vec_chain"], L.up())
                for m in range(4):
                    for c in range(TT):
                        cs = slice(c * P, (c + 1) * P)
                        v.tensor_tensor_scan(CUM[:, m, cs], C("ones"), w_[:, m, cs], 0.0, ALU.mult, ALU.add).then_inc(sems["vec_chain"], 1)
                        dve.wait_ge(sems["vec_chain"], L.up())
                cum8 = CUM.rearrange("p m (c t) -> p (m c) t", c=TT)
                mid, end = sm[:, CMID:CMID + 8], sm[:, CEND:CEND + 4]
                v.tensor_copy(mid.unsqueeze(2), cum8[:, :, 63:64]).then_inc(sems["vec_chain"], 1)
                dve.wait_ge(sems["vec_chain"], L.up())
                mid2 = mid.rearrange("p (m c) -> p m c", c=TT)
                v.tensor_copy(end.unsqueeze(2), CUM[:, :, P - 1:P]).then_inc(sems["vec_chain"], 1)
                dve.wait_ge(sems["vec_chain"], L.up())
                v.tensor_tensor(end.unsqueeze(2), end.unsqueeze(2), mid2[:, :, 0:1], ALU.subtract).then_inc(sems["vec_chain"], 1)
                dve.wait_ge(sems["vec_chain"], L.up())
                v.tensor_tensor(end.unsqueeze(2), end.unsqueeze(2), mid2[:, :, 1:2], ALU.add).then_inc(sems["vec_chain"], 1)
                dve.wait_ge(sems["vec_chain"], L.up())
                v.tensor_tensor(cum8, cum8, mid.unsqueeze(2).to_broadcast([P, 8, P]), ALU.subtract).then_inc(sems["vec_chain"], 1)
                dve.wait_ge(sems["vec_chain"], L.up())
                v.tensor_tensor(flat(AT_), flat(CUM), flat(w_), ALU.subtract).then_inc(sems["decay_sum"], 1)
                h0 = BANK_AT[f"head_sum{l}"]
                for j in range(2):
                    dve.wait_ge(bank_full[(h0 + j) % BANKS], filled(h0 + j))
                    v.tensor_scalar(flat(HI[:, 2 * j:2 * j + 2, :]), bk(h0 + j)[:, :], 1e-12, None, ALU.max).then_inc(bank_read[(h0 + j) % BANKS], 1)
                dve.wait_ge(sems["kk_sqrt"], L.nxt("kk_sqrt"))
                v.reciprocal(flat(HI[:, 0:4, :]), flat(HI[:, 0:4, :])).then_inc(sems["vec_chain"], 1)
                dve.wait_ge(sems["vec_chain"], L.up())
                v.tensor_tensor(flat(KKH), flat(KKH), flat(HI[:, 0:4, :]), ALU.mult).then_inc(sems["vec_chain"], 1)
                dve.wait_ge(sems["vec_chain"], L.up())
                om = sm[:, OMKA:OMKA + 4]
                v.tensor_scalar(om, V_(f"k_a{l}"), -1.0, 1.0, ALU.mult, ALU.add).then_inc(sems["vec_chain"], 1)
                dve.wait_ge(sems["vec_chain"], L.up())
                for c in range(4):
                    v.tensor_scalar(KT_[:, c, :], aa[:, c, :], layer_vec(f"k_a{l}", c), om[:, c:c + 1], ALU.mult, ALU.add).then_inc(sems["vec_chain"], 1)
                    dve.wait_ge(sems["vec_chain"], L.up())
                v.tensor_tensor(flat(KT_), flat(KT_), flat(k_), ALU.mult).then_inc(sems["vec_chain"], 1)
                dve.wait_ge(sems["vec_chain"], L.up())
                for c in range(4):
                    ins = v.scalar_tensor_tensor(HI[:, c, :], r_[:, c, :], layer_vec(f"r_k{l}", c), KT_[:, c, :], ALU.mult, ALU.mult)
                    if c < 3:
                        ins.then_inc(sems["vec_chain"], 1)
                        dve.wait_ge(sems["vec_chain"], L.up())
                ins.then_inc(sems["rw_bonus"], 1)
                dve.wait_ge(sems["decay_exp"], L.nxt("decay_exp"))
                Q_, QI = R[:, 0:4, :], R[:, 4:8, :]
                v.tensor_tensor(flat(AT_), flat(AT_), flat(KKH), ALU.mult).then_inc(sems["vec_chain"], 1)
                dve.wait_ge(sems["vec_chain"], L.up())
                v.scalar_tensor_tensor(flat(BT_), flat(aa), -1.0, flat(KKH), ALU.mult, ALU.mult).then_inc(sems["vec_chain"], 1)
                dve.wait_ge(sems["vec_chain"], L.up())
                v.tensor_tensor(flat(BT_), flat(BT_), flat(QI), ALU.mult).then_inc(sems["vec_chain"], 1)
                dve.wait_ge(sems["vec_chain"], L.up())
                v.tensor_tensor(flat(KT_), flat(KT_), flat(QI), ALU.mult).then_inc(sems["vec_chain"], 1)
                dve.wait_ge(sems["vec_chain"], L.up())
                v.tensor_tensor(flat(RT_), flat(RT_), flat(Q_), ALU.mult).then_inc(sems["rw_ops"], 1)
                for j in range(2):
                    n = h0 + 2 + j
                    dve.wait_ge(bank_full[n % BANKS], filled(n))
                    v.tensor_tensor(flat(BV[:, 2 * j:2 * j + 2, :]), bk(n)[:, :], flat(v_[:, 2 * j:2 * j + 2, :]), ALU.mult).then_inc(bank_read[n % BANKS], 1)
                dve.wait_ge(bank_read[(h0 + 3) % BANKS], filled(h0 + 3))
                n = BANK_AT[f"rwkv{l}"]
                for c in range(TT):
                    v.tensor_copy(h8(Xm), bcast(C("ident"), 8)).then_inc(sems["vec_chain"], 1)
                    dve.wait_ge(sems["vec_chain"], L.up())
                    v.tensor_copy(h8(XTm), bcast(C("ident"), 8)).then_inc(sems["x_new"], 1)
                    dve.wait_ge(sems["x_new"], L.nxt("x_new"))
                    for q, (dst, mask) in enumerate(((NTm, "before"), (RBm, "upto"), (RKm, "upto"))):
                        for g in range(2):
                            m = n + 2 + 2 * q + g
                            dve.wait_ge(bank_full[m % BANKS], filled(m))
                            v.tensor_tensor(h4(dst[:, g * 512:(g + 1) * 512]), h4(bk(m)[:, :]), bcast(C(mask), 4), ALU.mult).then_inc(bank_read[m % BANKS], 1)
                    n += 8
                    for lev in range(7):
                        for q, dst in enumerate((Xm, XTm)):
                            for g in range(2):
                                m = n + 2 + 2 * q + g
                                dve.wait_ge(bank_full[m % BANKS], filled(m))
                                v.tensor_tensor(dst[:, g * 512:(g + 1) * 512], dst[:, g * 512:(g + 1) * 512], bk(m)[:, :], ALU.add).then_inc(bank_read[m % BANKS], 1)
                        dve.wait_ge(bank_read[(n + 2) % BANKS], filled(n + 2))
                        dve.wait_ge(bank_read[(n + 3) % BANKS], filled(n + 3))
                        dve.wait_ge(bank_read[(n + 4) % BANKS], filled(n + 4))
                        dve.wait_ge(bank_read[(n + 5) % BANKS], filled(n + 5))
                        n += 6
                    n += 2
                    head_norm(n, YC, YSQ, RW_H, 64e-5, "rw_norm")
                    n += 1
                    if c == 0:
                        dve.wait_ge(bank_full[n % BANKS], filled(n))
                        for m in range(4):
                            ins = v.tensor_scalar(S1[:, m * 64:(m + 1) * 64], bk(n)[:, m * 64:(m + 1) * 64],
                                                  sm[:, CEND + m:CEND + m + 1], None, ALU.mult)
                            if m < 3:
                                ins.then_inc(sems["vec_chain"], 1)
                                dve.wait_ge(sems["vec_chain"], L.up())
                        ins.then_inc(bank_read[n % BANKS], 1)
                        n += 1
                    dve.wait_ge(bank_full[n % BANKS], filled(n))
                    cs = slice(c * P, (c + 1) * P)
                    for m in range(4):
                        ins = v.scalar_tensor_tensor(YB[:, 4 + m, cs], bk(n)[:, m * P:(m + 1) * P], layer_vec(f"rw_gn{l}", m),
                                                     BV[:, m, cs], ALU.mult, ALU.add)
                        if m < 3:
                            ins.then_inc(sems["vec_chain"], 1)
                            dve.wait_ge(sems["vec_chain"], L.up())
                    ins.then_inc(bank_read[n % BANKS], 1)
                    dve.wait_ge(bank_read[n % BANKS], filled(n))
                    n += 1
                    ins = v.tensor_tensor(YB[:, 4:8, cs], YB[:, 4:8, cs], GG[:, :, cs], ALU.mult)
                    if c == 0:
                        ins.then_inc(sems["vec_chain"], 1)
                        dve.wait_ge(sems["vec_chain"], L.up())
                ins.then_inc(sems["branch_done"], 1)

                g0, n0 = BANK_AT[f"w_gate{l}"], BANK_AT[f"w_branch{l}"]
                for m in range(g0 + 8, g0 + 12):
                    dve.wait_ge(bank_read[m % BANKS], filled(m))
                for i in range(3):
                    for j in range(4):
                        n = n0 + 4 * i + j
                        g_ = flat(GT[:, 8 * i + 2 * j:8 * i + 2 * j + 2, :])
                        r_ = flat(R[:, 2 * j:2 * j + 2, :])
                        dve.wait_ge(bank_full[n % BANKS], filled(n))
                        if i == 0:
                            v.tensor_tensor(r_, g_, bk(n)[:, :], ALU.mult).then_inc(bank_read[n % BANKS], 1)
                            dve.wait_ge(bank_read[n % BANKS], filled(n))
                            continue
                        v.tensor_tensor(g_, g_, bk(n)[:, :], ALU.mult).then_inc(bank_read[n % BANKS], 1)
                        dve.wait_ge(bank_read[n % BANKS], filled(n))
                        ins = v.tensor_tensor(r_, r_, g_, ALU.add)
                        if i == 2 and j == 3:
                            ins.then_inc(sems["merged"], 1)
                        else:
                            ins.then_inc(sems["vec_chain"], 1)
                            dve.wait_ge(sems["vec_chain"], L.up())
                n0 = BANK_AT[f"w_o{l}"]
                for j in range(4):
                    n = n0 + j
                    dve.wait_ge(bank_full[n % BANKS], filled(n))
                    for h in range(2):
                        m = 2 * j + h
                        ins = v.scalar_tensor_tensor(xT[:, m, :], bk(n)[:, h * S:(h + 1) * S], ml[:, 16 + m:17 + m], xT[:, m, :],
                                                     ALU.mult, ALU.add)
                        if h == 0:
                            ins.then_inc(sems["vec_chain"], 1)
                            dve.wait_ge(sems["vec_chain"], L.up())
                    ins.then_inc(bank_read[n % BANKS], 1)
                dve.wait_ge(bank_read[n0 % BANKS], filled(n0))
                dve.wait_ge(bank_read[(n0 + 1) % BANKS], filled(n0 + 1))
                dve.wait_ge(bank_read[(n0 + 2) % BANKS], filled(n0 + 2))
                dve.wait_ge(bank_read[(n0 + 3) % BANKS], filled(n0 + 3))
                rms_norm(xT[:, :, :], hT[:, :, :], KT, D)

                n = BANK_AT[f"route{l}"]
                t3 = lambda o, w: sm[:, o:o + 2 * w].rearrange("p (t w) -> p t w", t=TT)
                lg = t3(RL, 36)
                dve.wait_ge(bank_full[n % BANKS], filled(n))
                v.tensor_copy(sm[:, RL:RL + 72], bk(n)[:, 0:72]).then_inc(bank_read[n % BANKS], 1)
                dve.wait_ge(bank_read[n % BANKS], filled(n))
                gl, el = lg[:, :, 0:4], lg[:, :, 4:36]
                mx, eq, ex = t3(RT, 1), t3(RT + 2, 4), t3(RT + 10, 4)
                sums_, v0, v1, dv = t3(RT + 18, 1), t3(RT + 20, 1), t3(RT + 22, 1), t3(RT + 24, 1)
                m1, m2, w1, w2 = t3(RT + 26, 1), t3(RT + 28, 1), t3(RT + 30, 1), t3(RT + 32, 1)
                cw, o1, o2 = t3(CW, 32), t3(W2, 32), t3(W3, 32)
                wide = lambda ap, w: ap.to_broadcast([P, TT, w])

                def first_max(src, dst, top, tmp, order, w):
                    v.tensor_reduce(top, src, AX.X, ALU.max).then_inc(sems["vec_chain"], 1)
                    dve.wait_ge(sems["vec_chain"], L.up())
                    v.tensor_tensor(dst, src, wide(top, w), ALU.is_equal).then_inc(sems["vec_chain"], 1)
                    dve.wait_ge(sems["vec_chain"], L.up())
                    v.tensor_tensor(dst, dst, bcast(C(order), TT), ALU.mult).then_inc(sems["vec_chain"], 1)
                    dve.wait_ge(sems["vec_chain"], L.up())
                    v.tensor_reduce(tmp, dst, AX.X, ALU.max).then_inc(sems["vec_chain"], 1)
                    dve.wait_ge(sems["vec_chain"], L.up())
                    v.tensor_tensor(dst, dst, wide(tmp, w), ALU.is_equal).then_inc(sems["vec_chain"], 1)
                    dve.wait_ge(sems["vec_chain"], L.up())

                first_max(gl, eq, mx, m1, "first4", 4)
                v.tensor_tensor(ex, gl, wide(mx, 4), ALU.subtract).then_inc(sems["vec_chain"], 1)
                dve.wait_ge(sems["vec_chain"], L.up())
                v.tensor_scalar(eq, eq, BIG, -BIG, ALU.mult, ALU.add).then_inc(sems["vec_chain"], 1)
                dve.wait_ge(sems["vec_chain"], L.up())
                for tt in range(TT):
                    v.tensor_tensor(el[:, tt, :].rearrange("p (g e) -> p g e", g=4), el[:, tt, :].rearrange("p (g e) -> p g e", g=4),
                                         eq[:, tt, :].unsqueeze(2).to_broadcast([P, 4, 8]), ALU.add).then_inc(sems["vec_chain"], 1)
                    dve.wait_ge(sems["vec_chain"], L.up())
                first_max(el, o1, v0, m1, "first32", 32)
                v.scalar_tensor_tensor(el, o1, -2 * BIG, el, ALU.mult, ALU.add).then_inc(sems["vec_chain"], 1)
                dve.wait_ge(sems["vec_chain"], L.up())
                first_max(el, o2, v1, m2, "first32", 32)
                v.tensor_tensor(dv, v1, v0, ALU.subtract).then_inc(sems["router_max"], 1)
                dve.wait_ge(sems["router_exp"], L.nxt("router_exp"))
                v.tensor_reduce(sums_, ex, AX.X, ALU.add).then_inc(sems["vec_chain"], 1)
                dve.wait_ge(sems["vec_chain"], L.up())
                v.tensor_scalar(w1, dv, 1.0, None, ALU.add).then_inc(sems["vec_chain"], 1)
                dve.wait_ge(sems["vec_chain"], L.up())
                v.tensor_tensor(w1, w1, sums_, ALU.mult).then_inc(sems["vec_chain"], 1)
                dve.wait_ge(sems["vec_chain"], L.up())
                v.reciprocal(w1, w1).then_inc(sems["vec_chain"], 1)
                dve.wait_ge(sems["vec_chain"], L.up())
                v.tensor_tensor(w2, w1, dv, ALU.mult).then_inc(sems["vec_chain"], 1)
                dve.wait_ge(sems["vec_chain"], L.up())
                v.tensor_tensor(o1, o1, wide(w1, 32), ALU.mult).then_inc(sems["vec_chain"], 1)
                dve.wait_ge(sems["vec_chain"], L.up())
                v.tensor_tensor(o2, o2, wide(w2, 32), ALU.mult).then_inc(sems["vec_chain"], 1)
                dve.wait_ge(sems["vec_chain"], L.up())
                v.tensor_tensor(cw, o1, o2, ALU.add).then_inc(sems["router_w"], 1)
                dve.wait_ge(bank_full[(n + 1) % BANKS], filled(n + 1))
                v.tensor_copy(pT[0:N_EXP, 0, :], bk(n + 1)[0:N_EXP, 0:S]).then_inc(bank_read[(n + 1) % BANKS], 1)
                dve.wait_ge(sems["cw_loaded"], L.nxt("cw_loaded", 16))
                n0 = BANK_AT[f"moe{l}"]
                b_sig, b_g = L.seen.get("moe_sig", 0), L.seen.get("moe_gated", 0)
                with nc.vector.Fori(0, N_EXP) as e:
                    for f in range(4):
                        n = n0 + f
                        dve.wait_ge(sems["moe_sig"], e * 4 + (b_sig + f + 1))
                        v.tensor_tensor(SQ[:, f, :], SQ[:, f, :], bk(n)[:, 0:S], ALU.mult).then_inc(sems["moe_gated"], 1)
                        dve.wait_ge(sems["moe_gated"], e * 4 + (b_g + f + 1))
                        v.tensor_tensor(SQ[:, f, :], SQ[:, f, :], bk(n)[:, S:2 * S], ALU.mult).then_inc(bank_read[n % BANKS], 1)
                        dve.wait_ge(bank_read[n % BANKS], e + (n // BANKS + 1))
                        v.tensor_tensor(FF[:, f, :], SQ[:, f, :], PR[:, bass.ds(e, 1), :].rearrange("p o s -> p (o s)"), ALU.mult).then_inc(sems["moe_h"], 1)
                L.seen["moe_sig"], L.seen["moe_gated"] = b_sig + 4 * N_EXP, b_g + 4 * N_EXP
                dve.wait_ge(sems["down_done"], L.nxt("down_done", N_EXP))
                for m in range(KT):
                    ins = v.scalar_tensor_tensor(xT[:, m, :], acc[m // 2][:, (m % 2) * S:(m % 2 + 1) * S], ml[:, 40 + m:41 + m],
                                                 xT[:, m, :], ALU.mult, ALU.add)
                    if m < KT - 1:
                        ins.then_inc(sems["vec_chain"], 1)
                        dve.wait_ge(sems["vec_chain"], L.up())
                ins.then_inc(sems["x_new_layer"], 1)
                dve.wait_ge(sems["x_new_layer"], L.nxt("x_new_layer"))
            rms_norm(xT[:, :, :], hT[:, :, :], KT, D)
            Rtok = R[:].rearrange("p (t k) s -> p t (k s)", t=TT)
            for j in range(4):
                copy_out(BANK_AT["x_out"] + j, Rtok[:, j // 2, (j % 2) * 512:(j % 2 + 1) * 512])

        @block.scalar
        def _(act):
            L = Count()
            f = nc.scalar.activation

            def copy_out(n, dst, src=None):
                act.wait_ge(bank_full[n % BANKS], filled(n))
                f(dst, bk(n)[:, :] if src is None else src, ACT.Copy).then_inc(bank_read[n % BANKS], 1)

            def finish_norm(dst, K, gain, bias, layer=None):
                act.wait_ge(sems["norm_var"], L.nxt("norm_var"))
                f(stat[:, 1, :], stat[:, 1, :], ACT.Sqrt).then_inc(sems["norm_std"], 1)
                act.wait_ge(sems["norm_scaled"], L.nxt("norm_scaled"))
                src = R if layer else dst
                for k in range(K):
                    b = 0.0 if bias is None else bias[:, k:k + 1]
                    ins = f(dst[:, k, :], src[:, k, :], ACT.Identity, bias=b, scale=gain[:, k:k + 1])
                ins.then_inc(sems["norm_out"], 1)

            def layer_norm(dst, g, b):
                act.wait_ge(sems["norm_centered"], L.nxt("norm_centered"))
                f(flat(SQ[:, :, :]), flat(R[:, :, :]), ACT.Square).then_inc(sems["norm_sq"], 1)
                finish_norm(dst, KT, V_(g), V_(b), True)

            def rms_norm(src, dst, gain, bias, K=KT, k0=0):
                f(flat(SQ[:, k0:k0 + K, :]), flat(src), ACT.Square).then_inc(sems["norm_sq"], 1)
                finish_norm(dst, K, gain, bias)

            act.wait_ge(sems["lam_abs"], L.nxt("lam_abs"))
            lam = sm[:, LAM:LAM + 4]
            f(lam, lam, ACT.Exp).then_inc(sems["act_chain"], 1)
            act.wait_ge(sems["act_chain"], L.up())
            f(lam, lam, ACT.Ln, bias=1.0).then_inc(sems["lam_log"], 1)
            n0 = BANK_AT["hy_in"]
            for j in range(1, 8, 2):
                copy_out(n0 + j, flat(PR[:, 2 * j:2 * j + 2, :]))
            z = flat(R[:, 0:4, :])
            act.wait_ge(sems["gelu_in"], L.nxt("gelu_in"))
            f(z, z, ACT.Sigmoid, scale=2 * math.sqrt(2 / math.pi)).then_inc(sems["gelu_sig"], 1)
            g0 = BANK_AT["rg_gates"]
            for g, (dst, b) in enumerate(((RG, "ga_b"), (IG, "gx_b"))):
                for j in range(2):
                    n = g0 + 2 * g + j
                    act.wait_ge(bank_full[n % BANKS], filled(n))
                    for h in range(2):
                        ins = f(PR[:, dst + 2 * j + h, :], bk(n)[:, h * S:(h + 1) * S], ACT.Sigmoid,
                                bias=V_(b)[:, 2 * j + h:2 * j + h + 1])
                    ins.then_inc(bank_read[n % BANKS], 1)
            th = flat(PR[:, RG:RG + 4, :])
            act.wait_ge(sems["decay_in"], L.nxt("decay_in"))
            f(th, th, ACT.Tanh).then_inc(sems["decay_tanh"], 1)
            i0 = BANK_AT["idx"]
            for q in range(4):
                act.wait_ge(bank_full[(i0 + q) % BANKS], filled(i0 + q))
                f(flat(RELU[:, 2 * q:2 * q + 2, :]), bk(i0 + q)[:, :], ACT.Relu).then_inc(bank_read[(i0 + q) % BANKS], 1)
            act.wait_ge(sems["decay_den"], L.nxt("decay_den"))
            f(th, th, ACT.Sqrt).then_inc(sems["decay_sqrt"], 1)

            def attention(name, pairs, scale):
                order = attention_order(BANK_AT[name], pairs)
                for hp in range(pairs + 1):
                    if hp < pairs:
                        q = 4 * (hp % 2)
                        act.wait_ge(sems["dsa_max"], L.nxt("dsa_max"))
                        for j in range(4):
                            ins = f(LG[:, q + j, :], LG[:, q + j, :], ACT.Exp, bias=sm[:, NB + q + j:NB + q + j + 1],
                                    scale=scale, accum_out=sm[:, RS + q + j:RS + q + j + 1])
                        ins.then_inc(sems["dsa_exp"], 1)
                    if hp:
                        for h in range(2):
                            copy_out(order["t", hp - 1, h], flat(PTB[:, 2 * h:2 * h + 2, :]))

            def ffn_and_ple(l):
                layer_norm(hT, f"ln1_g{l}", f"ln1_b{l}")
                copy_out(BANK_AT[f"p_in{l}"], flat(pT[:, :, :]))
                n0 = BANK_AT[f"mlp{l}"]
                with nc.scalar.Fori(0, 4) as i:
                    for q in range(4):
                        n = n0 + q
                        tile_ = flat(FF[:, 2 * q:2 * q + 2, :])
                        act.wait_ge(bank_full[n % BANKS], filled(n, i))
                        f(tile_, bk(n)[:, :], ACT.Relu).then_inc(bank_read[n % BANKS], 1)
                        act.wait_ge(bank_read[n % BANKS], i + (n // BANKS + 1))
                        f(tile_, tile_, ACT.Square).then_inc(sems["ff_act"], 1)
                for j in range(4):
                    n = BANK_AT[f"ple_gate{l}"] + j
                    act.wait_ge(bank_full[n % BANKS], filled(n))
                    f(flat(SQ[:, 2 * j:2 * j + 2, :]), bk(n)[:, :], ACT.Sigmoid).then_inc(bank_read[n % BANKS], 1)
                layer_norm(xT, f"ln2_g{l}", f"ln2_b{l}")

            attention("dsa", 4, DSA_D ** -0.5)
            ffn_and_ple(0)

            n0 = BANK_AT["mla_down"]
            act.wait_ge(bank_read[n0 % BANKS], filled(n0))
            act.wait_ge(bank_read[(n0 + 1) % BANKS], filled(n0 + 1))
            rms_norm(CQ[:, 0:4, :], CQ[:, 0:4, :], V_("q_norm"), None, 4)
            act.wait_ge(bank_read[(n0 + 2) % BANKS], filled(n0 + 2))
            rms_norm(CQ[:, 4:6, :], CQ[:, 4:6, :], V_("kv_norm"), None, 2, 4)
            for j in range(1, 8, 2):
                n = BANK_AT["mla_uq"] + j
                act.wait_ge(bank_full[n % BANKS], filled(n))
                f(flat(QH[0:96, 2 * j:2 * j + 2, :]), bk(n)[0:96, :], ACT.Copy).then_inc(bank_read[n % BANKS], 1)
            act.wait_ge(sems["kr_rope"], L.nxt("kr_rope"))
            f(KH[64:96, :, :], KROT[64:96, :].unsqueeze(1).to_broadcast([32, MLA_H, S]), ACT.Copy).then_inc(sems["kr_spread"], 1)
            for j in range(8):
                n = BANK_AT["mla_k"] + j
                act.wait_ge(bank_full[n % BANKS], filled(n))
                f(flat(KH[0:64, 2 * j:2 * j + 2, :]), bk(n)[0:64, :], ACT.Copy).then_inc(bank_read[n % BANKS], 1)
            for q in range(4):
                copy_out(BANK_AT["mla_v"] + q, flat(VH)[:, q * 512:(q + 1) * 512])
            attention("mla", 8, (NOPE + ROPE) ** -0.5)
            ffn_and_ple(1)

            f(sm[:, CS:CS + 8], V_("c"), ACT.Sigmoid).then_inc(sems["c_sig"], 1)
            for t_ in (sinT, cosT):
                act.wait_ge(sems["rot_in"], L.nxt("rot_in"))
                f(t_[:, :], t_[:, :], ACT.Sin).then_inc(sems["rot_tables"], 1)
            for l in range(DEPTH):
                m0 = 48 * l
                act.wait_ge(sems["norm_out" if l == 0 else "x_new_layer"], L.nxt("norm_out" if l == 0 else "x_new_layer"))
                f(flat(SQ[:, :, :]), flat(xT[:, :, :]), ACT.Square).then_inc(sems["norm_sq"], 1)
                act.wait_ge(sems["mod_done"], L.nxt("mod_done"))
                finish_norm(hT, KT, sm[:, GA1:GA1 + 8], mod[:, m0:m0 + 8])
                n0 = BANK_AT[f"w_in{l}"]
                with nc.scalar.Fori(0, 5) as i:
                    for j in (1, 3):
                        act.wait_ge(bank_full[(n0 + j) % BANKS], filled(n0 + j, i))
                        f(PR[:, bass.ds(i * 8 + 2 * j, 2), :], two(bk(n0 + j)[:, :]), ACT.Copy).then_inc(bank_read[(n0 + j) % BANKS], 1)
                for m in range(n0 + 16, n0 + 20):
                    act.wait_ge(bank_read[m % BANKS], filled(m))
                f(flat(GT[:, 0:4, :]), flat(PR[:, 12:16, :]), ACT.Sigmoid).then_inc(sems["g_sig"], 1)
                n0 = BANK_AT[f"ret_t{l}"]
                VT = flat(GT[:, 4:8, :])
                for c in range(TT):
                    copy_out(n0 + c, VT[:, c * 512:(c + 1) * 512])

                def head_sqrt(H):
                    act.wait_ge(sems["head_var"], L.nxt("head_var"))
                    f(sm[:, HV:HV + H], sm[:, HV:HV + H], ACT.Sqrt).then_inc(sems["head_std"], 1)

                head_sqrt(RET_H)
                head_sqrt(RET_H)
                act.wait_ge(sems["mixed"], L.nxt("mixed"))
                f(PR[0:64, 28, :], PR[0:64, 28, :], ACT.Tanh).then_inc(sems["lora_in"], 1)
                f(PR[:, 29, :], PR[:, 29, :], ACT.Sigmoid).then_inc(sems["lora_in"], 1)
                l0 = BANK_AT[f"lora{l}"]
                for g, b in enumerate(("w0", "a0")):
                    for j in range(2):
                        n = l0 + 2 * g + j
                        act.wait_ge(bank_full[n % BANKS], filled(n))
                        for h in range(2):
                            m = 2 * j + h
                            ins = f(GT[:, 4 * g + m, :], bk(n)[:, h * S:(h + 1) * S], ACT.Sigmoid, bias=V_(f"{b}{l}")[:, m:m + 1])
                        ins.then_inc(bank_read[n % BANKS], 1)
                for j in range(2):
                    copy_out(l0 + 4 + j, flat(GG[:, 2 * j:2 * j + 2, :]))
                act.wait_ge(sems["decay_sum"], L.nxt("decay_sum"))
                f(flat(R[:, 0:4, :]), flat(CUM), ACT.Exp)
                f(flat(R[:, 4:8, :]), flat(CUM), ACT.Exp, scale=-1.0)
                f(sm[:, CEND:CEND + 4], sm[:, CEND:CEND + 4], ACT.Exp)
                f(flat(AT_), flat(AT_), ACT.Exp).then_inc(sems["decay_exp"], 1)
                h0 = BANK_AT[f"head_sum{l}"]
                act.wait_ge(bank_read[h0 % BANKS], filled(h0))
                act.wait_ge(bank_read[(h0 + 1) % BANKS], filled(h0 + 1))
                f(flat(HI[:, 0:4, :]), flat(HI[:, 0:4, :]), ACT.Sqrt).then_inc(sems["kk_sqrt"], 1)
                n0 = BANK_AT[f"rw_t{l}"]
                for q, dst in enumerate((VT2[:, 0:512], VT2[:, 512:1024], BT0, KT0)):
                    copy_out(n0 + q, dst)
                n = BANK_AT[f"rwkv{l}"]
                for c in range(TT):
                    for g in range(2):
                        copy_out(n + g, MTraw[:, g * 512:(g + 1) * 512])
                    n += 8
                    for lev in range(7):
                        for g in range(2):
                            copy_out(n + g, Tm[:, g * 512:(g + 1) * 512])
                        n += 6
                    copy_out(n, Zm)
                    copy_out(n + 1, Um)
                    head_sqrt(RW_H)
                    n += 5 if c == 0 else 4
                act.wait_ge(sems["branch_done"], L.nxt("branch_done"))
                n0 = BANK_AT[f"w_gate{l}"]
                o = VEC_AT[f"b_gate{l}"][0]
                with nc.scalar.Fori(0, 3) as i:
                    for j in range(4):
                        n = n0 + j
                        act.wait_ge(bank_full[n % BANKS], filled(n, i))
                        for h in range(2):
                            m = 2 * j + h
                            ins = f(GT[:, bass.ds(i * 8 + m, 1), :].rearrange("p o s -> p (o s)"), bk(n)[:, h * S:(h + 1) * S],
                                    ACT.Sigmoid, bias=vec[:, bass.ds(i * 8 + (o + m), 1)])
                        ins.then_inc(bank_read[n % BANKS], 1)
                n0 = BANK_AT[f"w_o{l}"]
                for m in range(n0, n0 + 4):
                    act.wait_ge(bank_read[m % BANKS], filled(m))
                f(flat(SQ[:, :, :]), flat(xT[:, :, :]), ACT.Square).then_inc(sems["norm_sq"], 1)
                finish_norm(hT, KT, sm[:, GA2:GA2 + 8], mod[:, m0 + 24:m0 + 32])
                act.wait_ge(sems["router_max"], L.nxt("router_max"))
                ex, dv = sm[:, RT + 10:RT + 18], sm[:, RT + 24:RT + 26]
                f(ex, ex, ACT.Exp)
                f(dv, dv, ACT.Exp).then_inc(sems["router_exp"], 1)
                n0 = BANK_AT[f"moe{l}"]
                with nc.scalar.Fori(0, N_EXP) as e:
                    for q in range(4):
                        n = n0 + q
                        act.wait_ge(bank_full[n % BANKS], filled(n, e))
                        f(SQ[:, q, :], bk(n)[:, 0:S], ACT.Sigmoid).then_inc(sems["moe_sig"], 1)
            act.wait_ge(sems["x_new_layer"], L.nxt("x_new_layer"))
            rms_norm(xT[:, :, :], hT, V_("final_g"), None)

        @block.gpsimd
        def _(pool):
            L = Count()
            for l in range(DEPTH):
                n = BANK_AT[f"rwkv{l}"]
                masked = [None, None]
                for c in range(TT):
                    pool.wait_ge(bank_read[n % BANKS], filled(n))
                    pool.wait_ge(bank_read[(n + 1) % BANKS], filled(n + 1))
                    n += 8
                    for lev in range(7):
                        b = lev % 2
                        if masked[b] is not None:
                            pool.wait_ge(bank_full[(masked[b]) % BANKS], filled(masked[b]))
                        elif c == 0:
                            if lev == 0:
                                pool.wait_ge(sems["rw_ops"], L.nxt("rw_ops"))
                        mask = C("levels")[:, lev * P:(lev + 1) * P]
                        nc.gpsimd.tensor_tensor(h8(MMs[b]), h8(MTraw), bcast(mask, 8), ALU.mult).then_inc(sems["mm_mask"], 1)
                        masked[b] = n + 1
                        n += 6
                    n += 5 if c == 0 else 4
                pool.wait_ge(bank_read[(BANK_AT[f"route{l}"] + 1) % BANKS], filled(BANK_AT[f"route{l}"] + 1))
                nc.gpsimd.dma_start(cw_dram[l], pT[0:N_EXP, 0, :]).then_inc(sems["cw_stored"], 16)
                pool.wait_ge(sems["cw_stored"], L.nxt("cw_stored", 16))
                nc.gpsimd.dma_start(PR[:, 0:N_EXP, :].rearrange("p e s -> p (e s)"),
                                    cw_dram[l:l + 1].rearrange("o e s -> o (e s)").to_broadcast([P, N_EXP * S])).then_inc(sems["cw_loaded"], 16)


_RAW = ["x", "p", "mlp_w1", "mlp_w2", "ple_w_proj", "ple_w_gate", "hy_w_in", "hy_w_out", "mla_w_down", "mla_w_uq",
        "mla_w_ukv", "mla_w_out", "positions_2", "w_ada_2", "w_in_2", "w_gate_2", "rwkv_w_lora_2", "rwkv_a_lora_2",
        "rwkv_g_lora_2", "w_branch_2", "w_o_2", "w_router_group_2", "b_router_group_2", "w_router_expert_2",
        "b_router_expert_2", "w_exp_gate_2", "w_exp_up_2", "w_exp_down_2"]


def lay_out(inputs):
    arrays = {n: np.ascontiguousarray(inputs[n]) for n in _RAW}
    cols = []
    for _, tiles, name, at in VECTORS:
        v = inputs[name] if at is None else inputs[name][at]
        cols.append(np.asarray(v).reshape(tiles, P).T)
    arrays["vectors"] = np.ascontiguousarray(np.concatenate(cols, 1))
    blocks = np.zeros((P, 2, 4, P), np.float32)
    for g, name in enumerate(("hy_ga_w", "hy_gx_w")):
        w = np.asarray(inputs[name][0])
        for c in range(4):
            for h in range(2):
                blocks[64 * h:64 * h + 64, g, c, 64 * h:64 * h + 64] = w[2 * c + h]
    arrays["gate_blocks"] = blocks.reshape(P, 1024)
    arrays["const"] = CONST
    return arrays


def program(nc, shapes):
    a = {n: nc.dram_tensor(f"in_{n}", s, mybir.dt.from_np(d), kind="ExternalInput").ap() for n, (s, d) in shapes.items()}
    out = nc.dram_tensor("out_0", (1, S, D), F32, kind="ExternalOutput").ap()
    build(nc, a, out)


def kernel(**inputs):
    import concourse.bacc as bacc
    from concourse.bass_utils import run_bass_kernel_spmd
    arrays = lay_out(inputs)
    nc = bacc.Bacc("TRN2", target_bir_lowering=False, num_devices=1)
    program(nc, {n: (v.shape, v.dtype) for n, v in arrays.items()})
    r = run_bass_kernel_spmd(nc, [{f"in_{n}": v for n, v in arrays.items()}], core_ids=[0])
    return r.results[0]["out_0"]
```

```python
import math
from contextlib import ExitStack

import numpy as np
import concourse.bass as bass
from concourse import mybir
from concourse.alu_op_type import AluOpType as ALU

ACT = mybir.ActivationFunctionType
AX = mybir.AxisListType
F32 = mybir.dt.float32
I32 = mybir.dt.int32

P = 128
D = 1024
KT = D // P
S = 256
TT = S // P
DEPTH = 2
FFN = 4 * D
RNN = 512
DSA_H, DSA_D = 8, 64
IDX_H = 4
TOPK = min(256, S // 4)
MLA_H, NOPE, ROPE, VD = 16, 64, 32, 64
QL, KVL = 512, 256
RET_H = 4
RW_H, RW_D = 8, 64
N_GROUP, PER_GROUP = 4, 8
N_EXP = N_GROUP * PER_GROUP
IN_TILES = 5376 // P
ALPHA = (2 * DEPTH) ** 0.25
BIG = 1e30
TAKEN = -3e38
CAP = 64
GROUP = 4
N_ROUND = N_EXP // GROUP
MOE_BLOCKS = [(0, 0), (1, 0), (0, 1), (1, 1), (0, 2), (1, 2), (2, 0), (2, 1), (0, 3), (1, 3), (2, 2), (2, 3)]
SLOTS = 4
SLOT = 4096
BANKS = 4


def constant_table():
    cols, at, n = [], {}, 0

    def put(name, a):
        nonlocal n
        full = np.zeros((P, a.shape[1]), np.float32)
        full[:a.shape[0]] = a
        cols.append(full)
        at[name] = (n, a.shape[1])
        n += a.shape[1]

    p = np.arange(P)
    put("ident", np.eye(P))
    put("ones", np.ones((P, P)))
    put("head_ones", (p[:, None] // 64 == p[None, :] // 64).astype(np.float32))
    put("swap", (p[:, None] == (p[None, :] + 64) % P).astype(np.float32))
    swap96 = np.zeros((96, 96), np.float32)
    for m in range(ROPE):
        swap96[NOPE + (m + ROPE // 2) % ROPE, NOPE + m] = 1.0
    put("swap_rope", swap96)
    t = np.arange(S)
    q = p[:, None] + P * np.arange(TT)[None, :]
    dist = q[:, :, None] - t[None, None, :]
    put("dist", dist.reshape(P, TT * S))
    put("causal", (dist >= 0).astype(np.float32).reshape(P, TT * S))
    put("noncausal", np.where(dist >= 0, 0.0, -BIG).reshape(P, TT * S))
    freq = (np.float32(10000.0) ** (-np.arange(0, ROPE, 2, dtype=np.float32) / ROPE)).astype(np.float32)
    ang = (t.astype(np.float32)[None, :] * freq[:, None]).astype(np.float32)
    cos, sin = np.ones((96, S)), np.zeros((96, S))
    cos[NOPE:] = np.concatenate([np.cos(ang)] * 2)
    sin[NOPE:] = np.concatenate([-np.sin(ang), np.sin(ang)])
    put("rope_cos", cos)
    put("rope_sin", sin)
    inv = (np.float32(10000.0) ** (-np.arange(64, dtype=np.float32) / np.float32(64))).astype(np.float32)
    put("inv_freq", np.concatenate([inv, inv])[:, None])
    put("sin_sign", np.where(p < 64, -1.0, 1.0)[:, None])
    lg = np.log1p(-np.exp2(-5.0 - np.arange(RET_H)))
    rel = p[None, :] - p[:, None]
    put("ret_decay_in", np.stack([np.where(rel >= 0, np.exp(g * np.maximum(rel, 0)), 0.0) for g in lg], 1)
        .reshape(P, -1) * P ** -0.5)
    put("ret_decay_k", np.stack([np.exp(g * (P - 1 - p)) for g in lg], 1) * P ** -0.5)
    put("ret_decay_q", np.stack([np.broadcast_to(np.exp(g * (p + 1.0))[None, :], (P, P)) for g in lg], 1)
        .reshape(P, -1))
    put("zeros", np.zeros((P, P)))
    put("before", (p[:, None] < p[None, :]).astype(np.float32))
    put("upto", (p[:, None] <= p[None, :]).astype(np.float32))
    levels = []
    for lev in range(7):
        b = 1 << lev
        s_, t_ = p[:, None], p[None, :]
        levels.append(((s_ // (2 * b) == t_ // (2 * b)) & ((t_ // b) % 2 == 1) & ((s_ // b) % 2 == 0)))
    put("levels", np.concatenate(levels, 1).astype(np.float32))
    put("ramp", np.broadcast_to(np.arange(CAP, dtype=np.float32), (P, CAP)))
    put("first4", np.broadcast_to(np.arange(4, 0, -1.0), (P, 4)))
    put("first32", np.broadcast_to(np.arange(32, 0, -1.0), (P, 32)))
    return np.ascontiguousarray(np.concatenate(cols, 1), dtype=np.float32), at


CONST, CONST_AT = constant_table()
TWO_PI = (6.28125, 0.0019350051879882812, 3.019915981956753e-07)


def h8(ap):
    return ap.rearrange("p (h d) -> p h d", h=8)

VECTORS = []
for _l in range(DEPTH):
    for _n in ("ln1_g", "ln1_b", "ln2_g", "ln2_b"):
        VECTORS.append((f"{_n}{_l}", KT, _n, _l))
VECTORS += [(f"conv_w{i}", 4, "hy_conv_w", (0, i)) for i in range(4)]
VECTORS += [("conv_b", 4, "hy_conv_b", 0), ("ga_b", 4, "hy_ga_b", 0), ("gx_b", 4, "hy_gx_b", 0),
            ("lam", 4, "hy_lambda", 0), ("q_norm", 4, "mla_q_norm", 0), ("kv_norm", 2, "mla_kv_norm", 0),
            ("c", KT, "c_2", 0), ("final_g", KT, "final_norm_g_2", None)]
for _l in range(DEPTH):
    VECTORS += [(f"norm1_g{_l}", KT, "norm1_g_2", _l), (f"norm2_g{_l}", KT, "norm2_g_2", _l),
                (f"b_ada{_l}", 48, "b_ada_2", _l), (f"b_gate{_l}", 24, "b_gate_2", _l),
                (f"ret_gn{_l}", 4, "ret_gn_g_2", _l), (f"mu{_l}", 14, "rwkv_mu_2", _l),
                (f"w0{_l}", 4, "rwkv_w0_2", _l), (f"a0{_l}", 4, "rwkv_a0_2", _l),
                (f"k_k{_l}", 4, "rwkv_k_k_2", _l), (f"k_a{_l}", 4, "rwkv_k_a_2", _l),
                (f"r_k{_l}", 4, "rwkv_r_k_2", _l), (f"rw_gn{_l}", 4, "rwkv_gn_g_2", _l)]
    VECTORS += [(f"cw{_l}{i}", 4, "conv_w_2", (_l, i)) for i in range(3)]
VEC_AT, _n = {}, 0
for _v in VECTORS:
    VEC_AT[_v[0]] = (_n, _v[1])
    _n += _v[1]
N_VEC = _n

STREAM = [("hy_in", (0, 1), 2), ("hy_out", (2, 3), 1)]
for _l in range(DEPTH):
    if _l == 1:
        STREAM += [("mla_down", (0, 1), 1), ("mla_uq", (2, 3), 1), ("mla_ukv", (0,), 1), ("mla_out", (2, 3), 1)]
    STREAM += [(f"mlp{_l}", (0, 1, 2, 3), 4), (f"ple_gate{_l}", (0, 1), 1), (f"ple_proj{_l}", (2,), 1)]
for _l in range(DEPTH):
    STREAM += [(f"w_in{_l}", (2, 3), 5), (f"w_in_last{_l}", (0,), 1),
               (f"w_gate{_l}", (2, 3), 3), (f"w_branch{_l}", (0, 1, 2), 1), (f"w_o{_l}", (0, 1), 1),
               (f"moe{_l}", (0, 1, 2, 3), 3 * N_EXP // GROUP)]
SLOT_AT, _uses = {}, [0] * SLOTS
for _name, _slots, _times in STREAM:
    SLOT_AT[_name] = [(s, _uses[s]) for s in _slots]
    for s in _slots:
        _uses[s] += _times

BANK_USES = [("x_in", 4), ("hy_in", 8), ("dsa_v", 1), ("rg_gates", 4), ("idx", 4), ("dsa", 4 * 5), ("hy_out", 4)]
for _l in range(DEPTH):
    if _l == 1:
        BANK_USES += [("mla_down", 4), ("mla_uq", 8), ("mla_rope", 9), ("mla_k", 8), ("mla_v", 4),
                      ("mla", 8 * 5), ("mla_out", 4)]
    BANK_USES += [(f"p_in{_l}", 1), (f"mlp{_l}", 16), (f"ple_gate{_l}", 4), (f"ple_proj{_l}", 4),
                  (f"ada{_l}", 1)]
for _l in range(DEPTH):
    BANK_USES += [(f"w_in{_l}", 21), (f"rot{_l}", 4), (f"ret_t{_l}", 3), (f"ret{_l}", 7),
                  (f"lora{_l}", 6), (f"head_sum{_l}", 4), (f"rw_t{_l}", 4), (f"rwkv{_l}", 2 * (8 + 7 * 6 + 4) + 1),
                  (f"w_gate{_l}", 12), (f"w_branch{_l}", 12), (f"w_o{_l}", 4),
                  (f"route{_l}", 8)]
BANK_USES += [("x_out", 4)]
BANK_AT, _n = {}, 0
for _name, _k in BANK_USES:
    BANK_AT[_name] = _n
    _n += _k


class Count:

    def __init__(self):
        self.own, self.seen = 0, {}

    def up(self):
        self.own += 1
        return self.own

    def nxt(self, name, k=1):
        self.seen[name] = self.seen.get(name, 0) + k
        return self.seen[name]


def filled(n, i=0):
    return i + (n // BANKS + 1)


def emptied(n, i=0):
    return i + n // BANKS


def loaded(u, i=0):
    return i * 16 + 16 * (u + 1)


def attention_order(n0, pairs):
    order = {}
    for hp in range(pairs + 1):
        if hp < pairs:
            for tt in range(TT):
                order["l", hp, tt] = n0 + len(order)
        if hp:
            for h in range(2):
                order["t", hp - 1, h] = n0 + len(order)
            order["o", hp - 1, 0] = n0 + len(order)
    return order


def build(nc, a, out):
    with ExitStack() as ctx:
        def sb(name, shape, dt=F32):
            return ctx.enter_context(nc.sbuf_tensor(name, shape, dt))

        ring = [sb(f"ring{s}", [P, SLOT]) for s in range(SLOTS)]
        const = sb("const", [P, CONST.shape[1]])
        vec = sb("vec", [P, N_VEC])
        xT = sb("xT", [P, KT, S])
        hT = sb("hT", [P, KT, S])
        R = sb("R", [P, KT, S])
        SQ = sb("SQ", [P, KT, S])
        PR = sb("PR", [P, IN_TILES, S])
        GT = sb("GT", [P, 24, S])
        YB = sb("YB", [P, 12, S])
        stat = sb("stat", [P, 2, S])
        pin = sb("pin", [P, 2, S])
        pT = sb("pT", [P, 2, S])
        sm = sb("sm", [P, 512])
        CW, W2, W3, ASG = 256, 320, 384, 448
        mod = sb("mod", [P, DEPTH * 48])
        small_w = sb("small_w", [P, 1024])
        cosT, sinT = pin[:, 0, :], pin[:, 1, :]
        posi = pT[:, 1, :].bitcast(I32)
        S1 = pT[:, 0, :]
        bank = [ctx.enter_context(nc.psum_tensor(f"bank{b}", [P, 512], F32)) for b in range(8)]
        acc = bank[4:8]
        cw_dram = nc.dram_tensor("expert_weights", (DEPTH, N_EXP, S), F32).ap()

        def C(name):
            o, w = CONST_AT[name]
            return const[:, o:o + w]

        def V_(name):
            o, w = VEC_AT[name]
            return vec[:, o:o + w]

        def bk(n):
            return bank[n % BANKS]

        def two(ap):
            return ap.rearrange("p (a b) -> p a b", a=2)

        def flat(ap):
            return ap.rearrange("p a b -> p (a b)")

        def bcast(ap, n):
            return ap.unsqueeze(1).to_broadcast([ap.shape[0], n, ap.shape[1]])

        names = [
            "inputs_loaded", "x_loaded", "p_loaded", "small_loaded", "kvw_loaded", "tail_loaded", "pos_loaded",
            "lam_abs", "lam_log", "conv_done", "decay_in", "decay_tanh", "decay_den", "decay_sqrt", "gelu_in", "gelu_sig",
            "dsa_max", "dsa_exp", "dsa_probs",
            "norm_in", "norm_sum", "norm_centered", "norm_sq", "norm_var", "norm_std", "norm_scaled", "norm_out",
            "ff_act", "down_done", "kr_rope", "kr_spread", "q_roped",
            "c_sig", "c_silu", "ada_loaded0", "ada_loaded1", "ada_summed", "mod_done", "rot_in", "rot_tables",
            "g_sig", "ret_kq", "ret_norm", "y_ret", "head_var", "head_std",
            "mixed", "lora_in", "decay_sum", "decay_exp", "kk_sq", "kk_max", "kk_sqrt", "rw_bonus", "rw_ops",
            "mm_mask", "x_new", "rw_norm", "branch_done", "merged",
            "router_max", "router_exp", "router_w", "moe_sig", "moe_gated",
            "assigned", "over_found", "over_known", "sel_ready", "xs_full", "xs_read_v", "xs_read_a", "swt_full", "swt_read",
            "gate_used", "gu_full", "gu_read", "ht_full", "ht_read", "y_full", "y_read_v", "y_read_a", "scattered",
            "x_new_layer", "out_stored", "vec_chain", "act_chain", "pe_chain", "pool_chain"]
        sems = {n: ctx.enter_context(nc.semaphore(n)) for n in names}
        bank_full = [ctx.enter_context(nc.semaphore(f"bank_full{b}")) for b in range(BANKS)]
        bank_read = [ctx.enter_context(nc.semaphore(f"bank_read{b}")) for b in range(BANKS)]
        slot_full = [ctx.enter_context(nc.semaphore(f"slot_full{s}")) for s in range(SLOTS)]
        spill = [{n: ctx.enter_context(nc.semaphore(f"{n}_{l}")) for n in
                  ("spill_stored", "spill_cw", "spill_slot0", "spill_slot1", "spill_slot2", "spill_full0", "spill_full1", "spill_full2",
                   "spill_full3", "spill_read0", "spill_read1", "spill_read2", "spill_read3", "spill_sig", "spill_gated",
                   "spill_h", "spill_down")} for l in range(DEPTH)]
        block = ctx.enter_context(nc.Block())

        XR, YR, Q0, KD, IQ, IK = 0, 4, 8, 12, 13, 15
        XC, RG, IG = 16, 20, 24
        LG = PR[:, 28:36, :]
        PTB = PR[:, 36:40, :]
        ADM = GT[:, 0:2, :]
        ISC = GT[:, 2:4, :]
        RELU = GT[:, 4:12, :]
        VI = GT[:, 12:13, :]
        MIX = YB[:, 0:8, :]
        QH = PR[:, 0:16, :]
        KH = GT[:, 0:16, :]
        VH = PR[:, 16:24, :]
        CQ = PR[:, 24:30, :]
        KRAW = PR[:, 30, :]
        KROT = PR[:, 31, :]
        FF = PR[:, 32:40, :]

        ADA_N = 6 * D // 2
        ADA = [flat(PR[:, 12 * h:12 * h + 12, :]) for h in range(2)]
        ADA_SUM = flat(GT[:, :, :])

        HI = PR[:, 30:42, :]
        AT_, BT_, KT_, RT_ = SQ[:, 0:4, :], GT[:, 4:8, :], HI[:, 4:8, :], PR[:, 16:20, :]
        KKH, BV, GG, CUM = SQ[:, 4:8, :], HI[:, 8:12, :], GT[:, 8:12, :], GT[:, 12:16, :]
        MMs = (flat(R[:, 0:4, :]), flat(R[:, 4:8, :]))
        MTraw, Xm, XTm, Tm = (flat(PR[:, q:q + 4, :]) for q in (0, 4, 8, 12))
        VT2, NTm, RBm, RKm = (flat(GT[:, q:q + 4, :]) for q in (0, 12, 16, 20))
        BT0, KT0 = flat(PR[:, 20:22, :]), flat(PR[:, 22:24, :])
        Zm, Um = flat(SQ[:, 4:6, :]), flat(SQ[:, 6:8, :])
        YC, YSQ = flat(HI[:, 0:2, :]), flat(HI[:, 2:4, :])

        flag = sb("flag", [1, 1], I32)
        XS = PR[:, 0:8, :]
        HTOK = flat(PR[:, 8:16, :])
        SEL, SELW, SWT = PR[:, 16:18, :], PR[:, 18:20, :], PR[:, 20:22, :]
        SG, HE = flat(PR[:, 22:24, :]), flat(PR[:, 24:26, :])
        YE = flat(PR[:, 26:30, :])

        def vi(tt, c0, c1):
            return flat(VI)[:, tt * 68 + c0:tt * 68 + c1]

        @block.sync
        def _(sp):
            L = Count()
            released = [None] * SLOTS
            down = [0]

            def stream(name, srcs, per_bank, between=None):
                slots = SLOT_AT[name]
                times = [t for n_, _, t in STREAM if n_ == name][0]
                for s, _ in slots:
                    if released[s]:
                        sp.wait_ge(*released[s])

                def body(i):
                    for j, (s, u) in enumerate(slots):
                        kind, k, stride = per_bank[j]
                        if not isinstance(i, int):
                            if kind == "bank":
                                n = BANK_AT[name] + k
                                sp.wait_ge(bank_full[n % BANKS], i + n // BANKS)
                            else:
                                sp.wait_ge(sems["down_done"], i * stride + (down[0] + k + 1 - stride))
                        for dst, src in srcs(i, j):
                            sp.dma_start(dst, src).then_inc(slot_full[s], 16)
                        if between and not isinstance(i, int):
                            between(i, j)
                    if between and isinstance(i, int):
                        for j in range(4):
                            between(i, j)
                body(0)
                if times > 1:
                    with nc.sync.Fori(1, times) as i:
                        body(i)
                for j, (s, _) in enumerate(slots):
                    kind, k, stride = per_bank[j]
                    if kind == "bank":
                        n = BANK_AT[name] + k
                        released[s] = (bank_full[n % BANKS], n // BANKS + 1 + (times - 1))
                    else:
                        released[s] = (sems["down_done"], down[0] + k + 1 + stride * (times - 1))
                if any(p[0] == "down" for p in per_bank):
                    down[0] += 8

            def cols(w, i, j, n=512, kt=KT):
                return w[:, bass.ds(i * (2 * n) + j * n, n)].rearrange("(k p) n -> p k n", p=P)

            def lin8(name, w):
                stream(name, lambda i, j: [(ring[SLOT_AT[name][j][0]][:].rearrange("p (k n) -> p k n", k=KT),
                                            cols(w, i, j))], [("bank", 1, 1), ("bank", 3, 1)])

            sp.dma_start(const[:], a["const"]).then_inc(sems["inputs_loaded"], 16)
            sp.dma_start(vec[:], a["vectors"]).then_inc(sems["inputs_loaded"], 16)
            sp.dma_start(R[:].rearrange("p (t k) s -> p t (k s)", t=TT), a["x"][0].rearrange("(t p) d -> p t d", p=P)).then_inc(sems["x_loaded"], 16)
            sp.dma_start(small_w[:], a["gate_blocks"]).then_inc(sems["small_loaded"], 16)
            w_in = a["hy_w_in"][0]
            tail = w_in[:, 1536:1988].rearrange("(k p) n -> p k n", p=P)
            sp.dma_start(GT[:, 20:24, :].rearrange("p a b -> p (a b)")[:, 0:KT * 68].rearrange("p (k n) -> p k n", k=KT)[:, :, 0:64],
                         tail[:, :, 64:128]).then_inc(sems["kvw_loaded"], 16)
            sp.dma_start(GT[:, 20:24, :].rearrange("p a b -> p (a b)")[:, 0:KT * 68].rearrange("p (k n) -> p k n", k=KT)[:, :, 64:68],
                         tail[:, :, 448:452]).then_inc(sems["kvw_loaded"], 16)

            s0, s1 = 0, 1
            r0 = ring[0][:].rearrange("p (k n) -> p k n", k=KT)
            r1 = ring[1][:].rearrange("p (k n) -> p k n", k=KT)
            sp.dma_start(r0, w_in[:, 0:512].rearrange("(k p) n -> p k n", p=P)).then_inc(slot_full[0], 16)
            sp.dma_start(r1, w_in[:, 512:1024].rearrange("(k p) n -> p k n", p=P)).then_inc(slot_full[1], 16)
            n0 = BANK_AT["hy_in"]
            sp.wait_ge(bank_full[(n0 + 1) % BANKS], filled(n0 + 1))
            sp.dma_start(r0, w_in[:, 1024:1536].rearrange("(k p) n -> p k n", p=P)).then_inc(slot_full[0], 16)
            sp.wait_ge(bank_full[(n0 + 3) % BANKS], filled(n0 + 3))
            for c, (c0, c1) in ((0, (0, 64)), (64, (0, 64)), (128, (128, 384)), (384, (384, 448)), (448, (384, 448))):
                sp.dma_start(r1[:, :, c:c + c1 - c0], tail[:, :, c0:c1]).then_inc(
                    slot_full[1] if c == 448 else sems["tail_loaded"], 16)
            released[0] = (bank_full[(n0 + 5) % BANKS], (n0 + 5) // BANKS + 1)
            released[1] = (bank_full[(n0 + 7) % BANKS], (n0 + 7) // BANKS + 1)
            lin8("hy_out", a["hy_w_out"][0])

            def mlp(l):
                w1, w2 = a["mlp_w1"][l], a["mlp_w2"][l]
                nm = f"mlp{l}"

                def src(i, j):
                    c, is_down = j // 2, j % 2
                    s = SLOT_AT[nm][j][0]
                    if not is_down:
                        return [(ring[s][:].rearrange("p (k n) -> p k n", k=KT), cols(w1, i, c))]
                    return [(ring[s][:].rearrange("p (k n) -> p k n", k=4),
                             w2[bass.ds(i * 1024 + c * 512, 512), :].rearrange("(k p) n -> p k n", p=P))]

                def ada(i, j):
                    r, h = j // 2, j % 2
                    if isinstance(i, int):
                        if j == 0:
                            sp.wait_ge(sems["norm_out"], 1 + 4 * l)
                        if r:
                            sp.wait_ge(sems["ada_summed"], 16 * l + h + 1)
                    else:
                        sp.wait_ge(sems["ada_summed"], i * 4 + (16 * l + 2 * r + h - 1))
                    sp.dma_start(ADA[h], a["w_ada_2"][l][bass.ds(i * 256 + r * P, P), h * ADA_N:(h + 1) * ADA_N]).then_inc(
                        sems[f"ada_loaded{h}"], 16)
                stream(nm, src, [("bank", 1, 1), ("down", 0, 2), ("bank", 3, 1), ("down", 1, 2)], ada)
                lin8(f"ple_gate{l}", a["ple_w_gate"][l])
                stream(f"ple_proj{l}", lambda i, j: [(ring[2][:, 0:2048].rearrange("p (k n) -> p k n", k=2),
                                                      a["ple_w_proj"][l].rearrange("(k p) n -> p k n", p=P))],
                       [("bank", 3, 1)])

            def load_p(l):
                if l:
                    sp.wait_ge(bank_full[(BANK_AT[f"p_in{l - 1}"]) % BANKS], filled(BANK_AT[f"p_in{l - 1}"]))
                sp.dma_start(pin[:], a["p"][l, 0].rearrange("(t p) f -> p t f", p=P)).then_inc(sems["p_loaded"], 16)

            load_p(0)
            mlp(0)
            wd = a["mla_w_down"][0]
            stream("mla_down", lambda i, j: [
                (ring[j][:].rearrange("p (k n) -> p k n", k=KT)[:, :, 0:(512, 288)[j]],
                 wd[:, j * 512:(512, 800)[j]].rearrange("(k p) n -> p k n", p=P))], [("bank", 1, 1), ("bank", 3, 1)])
            uq = a["mla_w_uq"][0]
            stream("mla_uq", lambda i, j: [(ring[2 + j][:, 0:3072].rearrange("p (k n) -> p k n", k=4),
                                            uq[:, j * 768:(j + 1) * 768].rearrange("(k p) n -> p k n", p=P))],
                   [("bank", 3, 1), ("bank", 7, 1)])
            n_v = BANK_AT["mla_v"] + 3
            sp.wait_ge(*released[0])
            sp.dma_start(ring[0][:].rearrange("p (k n) -> p k n", k=2),
                         a["mla_w_ukv"][0].rearrange("(k p) n -> p k n", p=P)).then_inc(slot_full[0], 16)
            released[0] = (bank_full[n_v % BANKS], n_v // BANKS + 1)
            lin8("mla_out", a["mla_w_out"][0])
            load_p(1)
            mlp(1)
            sp.wait_ge(bank_full[(BANK_AT["ple_proj1"] + 3) % BANKS], filled(BANK_AT["ple_proj1"] + 3))
            sp.dma_start(posi, a["positions_2"].to_broadcast([P, S])).then_inc(sems["pos_loaded"], 16)
            for l in range(DEPTH):
                lin8(f"w_in{l}", a["w_in_2"][l])
                n_last = BANK_AT[f"w_in{l}"] + 20
                sp.wait_ge(*released[0])
                sp.dma_start(ring[0][:, 0:2048].rearrange("p (k n) -> p k n", k=KT),
                             a["w_in_2"][l][:, 5120:5376].rearrange("(k p) n -> p k n", p=P)).then_inc(slot_full[0], 16)
                released[0] = (bank_full[n_last % BANKS], n_last // BANKS + 1)
                last_small = BANK_AT["rg_gates"] + 3 if l == 0 else BANK_AT["route0"]
                sp.wait_ge(bank_full[last_small % BANKS], filled(last_small))
                sp.dma_start(small_w[0:64, 0:512], a["rwkv_w_lora_2"][l]).then_inc(sems["small_loaded"], 16)
                sp.dma_start(small_w[64:128, 0:512], a["rwkv_a_lora_2"][l]).then_inc(sems["small_loaded"], 16)
                sp.dma_start(small_w[:, 512:1024], a["rwkv_g_lora_2"][l]).then_inc(sems["small_loaded"], 16)
                lin8(f"w_gate{l}", a["w_gate_2"][l])
                stream(f"w_branch{l}", lambda i, j: [(ring[j][:].rearrange("p (k n) -> p k n", k=4),
                                                      a["w_branch_2"][l, j].rearrange("(k p) n -> p k n", p=P))],
                       [("bank", 3, 1), ("bank", 7, 1), ("bank", 11, 1)])
                lin8(f"w_o{l}", a["w_o_2"][l])
                sp.wait_ge(bank_full[(BANK_AT[f"lora{l}"] + 5) % BANKS], filled(BANK_AT[f"lora{l}"] + 5))
                sp.dma_start(small_w[:, 0:288].rearrange("p (k n) -> p k n", k=KT)[:, :, 0:4],
                             a["w_router_group_2"][l].rearrange("(k p) n -> p k n", p=P)).then_inc(sems["small_loaded"], 16)
                sp.dma_start(small_w[:, 0:288].rearrange("p (k n) -> p k n", k=KT)[:, :, 4:36],
                             a["w_router_expert_2"][l].rearrange("(k p) n -> p k n", p=P)).then_inc(sems["small_loaded"], 16)
                sp.dma_start(small_w[0:1, 288:292], a["b_router_group_2"][l:l + 1]).then_inc(sems["small_loaded"], 16)
                sp.dma_start(small_w[0:1, 292:324], a["b_router_expert_2"][l:l + 1]).then_inc(sems["small_loaded"], 16)
                wg, wu, wdn = a["w_exp_gate_2"][l], a["w_exp_up_2"][l], a["w_exp_down_2"][l]

                e0 = N_EXP * l

                def expert_block(b, i):
                    kind, e = MOE_BLOCKS[b]
                    w = (wg, wu, wdn)[kind][bass.ds(i * GROUP + e, 1)]
                    sp.dma_start(ring[b % SLOTS][:].rearrange("p (k n) -> p k n", k=(KT, KT, 4)[kind]),
                                 w.rearrange("o (k p) n -> p (o k) n", p=P)).then_inc(slot_full[b % SLOTS], 16)

                def group_tail(i):
                    for b in range(SLOTS, 12):
                        kind, e = MOE_BLOCKS[b - SLOTS]
                        used_up = ("gate_used", "gu_full", "y_full")[kind]
                        sp.wait_ge(sems[used_up], i * GROUP + (e0 + e + 1))
                        expert_block(b, i)

                for b in range(SLOTS):
                    sp.wait_ge(*released[b])
                    expert_block(b, 0)
                group_tail(0)
                with nc.sync.Fori(1, N_ROUND) as i:
                    sp.wait_ge(sems["gate_used"], i * GROUP + e0)
                    expert_block(0, i)
                    sp.wait_ge(sems["gu_full"], i * GROUP + e0)
                    expert_block(1, i)
                    sp.wait_ge(sems["y_full"], i * GROUP + (e0 - 1))
                    expert_block(2, i)
                    sp.wait_ge(sems["y_full"], i * GROUP + e0)
                    expert_block(3, i)
                    group_tail(i)
                e1 = e0 + N_EXP
                released[0], released[1] = (sems["gate_used"], e1), (sems["gu_full"], e1)
                released[2], released[3] = (sems["y_full"], e1 - 1), (sems["y_full"], e1)

                sp.wait_ge(sems["over_known"], L.nxt("over_known"))
                with nc.sync.If(nc.sync.value_load(flag[0:1, 0:1], min_val=0, max_val=2 * S) > 0):
                    sp.wait_ge(sems["scattered"], e1 // 2)
                    F_ = spill[l]

                    def spill_block(j, e):
                        w = (wg, wu, wdn)[j][bass.ds(e, 1)]
                        sp.dma_start(ring[1 + j][:].rearrange("p (k n) -> p k n", k=(KT, KT, 4)[j]),
                                     w.rearrange("o (k p) n -> p (o k) n", p=P)).then_inc(F_[f"spill_slot{j}"], 16)
                    for j in range(3):
                        spill_block(j, 0)
                    with nc.sync.Fori(1, N_EXP) as e:
                        sp.wait_ge(F_["spill_full3"], e)
                        spill_block(0, e)
                        spill_block(1, e)
                        sp.wait_ge(F_["spill_down"], e)
                        spill_block(2, e)
                    sp.wait_ge(F_["spill_down"], N_EXP)
            for m in range(BANK_AT["x_out"], BANK_AT["x_out"] + 4):
                sp.wait_ge(bank_read[m % BANKS], filled(m))
            sp.dma_start(out[0].rearrange("(t p) d -> p t d", p=P), R[:].rearrange("p (t k) s -> p t (k s)", t=TT)).then_inc(sems["out_stored"], 16)
            sp.wait_ge(sems["out_stored"], 16)

        @block.tensor
        def _(pe):
            L = Count()
            mm = nc.tensor.matmul
            used = [0]

            def mul(o, lhsT, rhs, first=True, last=True, **kw):
                return mm(o, lhsT=lhsT, rhs=rhs, start=first, stop=last, **kw)

            def slot(s, k, n=None):
                n = n or SLOT // k
                return ring[s][:, 0:k * n].rearrange("p (k n) -> p k n", k=k)

            def pair(n, lhs, rhs, K, i=0, w=S, rows=slice(0, P)):
                pe.wait_ge(bank_read[n % BANKS], emptied(n, i))
                for h in range(2):
                    for k in range(K):
                        ins = mul(bk(n)[rows, h * w:(h + 1) * w], lhs(h, k), rhs(k), k == 0, k == K - 1)
                ins.then_inc(bank_full[n % BANKS], 1)

            def lin8(name, rhs, w=S):
                n0, slots = BANK_AT[name], SLOT_AT[name]
                times = [t for n_, _, t in STREAM if n_ == name][0]

                def body(i):
                    for b, (s, u) in enumerate(slots):
                        pe.wait_ge(slot_full[s], loaded(u, i))
                        W = slot(s, KT)
                        for j in range(2):
                            pair(n0 + 2 * b + j, lambda h, k: W[:, k, (2 * j + h) * P:(2 * j + h + 1) * P], rhs,
                                 KT, i, w)
                if times > 1:
                    with nc.tensor.Fori(0, times) as i:
                        body(i)
                else:
                    body(0)

            def sums(src, k0, K):
                for k in range(K):
                    ins = mul(acc[3][:, 0:S], C("ones"), src[:, k0 + k, :], k == 0, k == K - 1)
                ins.then_inc(sems["norm_sum"], 1)

            def layer_norm():
                sums(R, 0, KT)
                pe.wait_ge(sems["norm_sq"], L.nxt("norm_sq"))
                sums(SQ, 0, KT)

            def rms_norm(src=SQ, K=KT):
                pe.wait_ge(sems["norm_sq"], L.nxt("norm_sq"))
                sums(src, 0, K)

            def clear_acc():
                for b in range(4):
                    mul(acc[b][:, :], C("zeros")[0:1, :], C("causal")[0:1, 0:512], True, False, skip_group_check=True)

            def down(W, src, last_too):
                for kk in range(4):
                    if kk % last_too == 0:
                        yield kk
                    for m in range(KT):
                        ins = mul(acc[m // 2][:, (m % 2) * S:(m % 2 + 1) * S], W[:, kk, m * P:(m + 1) * P],
                                  src(kk), False, False, skip_group_check=True)
                ins.then_inc(sems["down_done"], 1)

            pe.wait_ge(sems["inputs_loaded"], 32)
            pe.wait_ge(sems["x_loaded"], L.nxt("x_loaded", 16))
            n0 = BANK_AT["x_in"]
            Rtok = R[:].rearrange("p (t k) s -> p t (k s)", t=TT)
            for j in range(4):
                for h in range(2):
                    for tt in range(TT):
                        ins = nc.tensor.transpose(bk(n0 + j)[:, h * S + tt * P:h * S + (tt + 1) * P],
                                                  Rtok[:, tt, (2 * j + h) * P:(2 * j + h + 1) * P], C("ident"))
                ins.then_inc(bank_full[(n0 + j) % BANKS], 1)
            for m in range(n0, n0 + 4):
                pe.wait_ge(bank_read[m % BANKS], filled(m))

            n0 = BANK_AT["hy_in"]
            for b in range(4):
                pe.wait_ge(slot_full[b % 2], loaded(b // 2))
                if b == 3:
                    pe.wait_ge(sems["tail_loaded"], L.nxt("tail_loaded", 64))
                W = slot(b % 2, KT)
                for j in range(2):
                    pair(n0 + 2 * b + j, lambda h, k: W[:, k, (2 * j + h) * P:(2 * j + h + 1) * P],
                         lambda k: xT[:, k, :], KT)
            pe.wait_ge(sems["kvw_loaded"], L.nxt("kvw_loaded", 32))
            n = BANK_AT["dsa_v"]
            pe.wait_ge(bank_read[n % BANKS], emptied(n))
            kvw = flat(GT[:, 20:24, :])[:, 0:KT * 68].rearrange("p (k n) -> p k n", k=KT)
            for tt in range(TT):
                for k in range(KT):
                    ins = mul(bk(n)[:, tt * 68:(tt + 1) * 68], xT[:, k, tt * P:(tt + 1) * P], kvw[:, k, :],
                              k == 0, k == KT - 1)
            ins.then_inc(bank_full[n % BANKS], 1)
            pe.wait_ge(sems["small_loaded"], L.nxt("small_loaded", 16))
            pe.wait_ge(sems["conv_done"], L.nxt("conv_done"))
            n0 = BANK_AT["rg_gates"]
            for g in range(2):
                for j in range(2):
                    n = n0 + 2 * g + j
                    pe.wait_ge(bank_read[n % BANKS], emptied(n))
                    for h in range(2):
                        c = 2 * j + h
                        ins = mul(bk(n)[:, h * S:(h + 1) * S], small_w[:, g * 512 + c * P:g * 512 + (c + 1) * P],
                                  PR[:, XC + c, :])
                    ins.then_inc(bank_full[n % BANKS], 1)
            for m in range(BANK_AT["hy_in"] + 4, BANK_AT["hy_in"] + 8):
                pe.wait_ge(bank_read[m % BANKS], filled(m))
            n0 = BANK_AT["idx"]
            for tt in range(TT):
                for j in range(2):
                    n = n0 + 2 * tt + j
                    pe.wait_ge(bank_read[n % BANKS], emptied(n))
                    for h in range(2):
                        half = slice(64 * h, 64 * h + 64)
                        ins = mul(bk(n)[:, h * S:(h + 1) * S], PR[half, IQ + j, tt * P:(tt + 1) * P], PR[half, IK, :])
                        if h == 0:
                            ins.then_inc(sems["pe_chain"], 1)
                            pe.wait_ge(sems["pe_chain"], L.up())
                    ins.then_inc(bank_full[n % BANKS], 1)

            def attention(name, pairs, q, k, v):
                n0 = BANK_AT[name]

                def logits(hp):
                    for tt in range(TT):
                        n = order[("l", hp, tt)]
                        pe.wait_ge(bank_read[n % BANKS], emptied(n))
                        for h in range(2):
                            ins = mul(bk(n)[:, h * S:(h + 1) * S], q(hp, h, tt), k(hp, h))
                            if h == 0 and name == "dsa":
                                ins.then_inc(sems["pe_chain"], 1)
                                pe.wait_ge(sems["pe_chain"], L.up())
                        ins.then_inc(bank_full[n % BANKS], 1)

                def output(hp):
                    pe.wait_ge(sems["dsa_probs"], L.nxt("dsa_probs"))
                    for h in range(2):
                        n = order[("t", hp, h)]
                        pe.wait_ge(bank_read[n % BANKS], emptied(n))
                        for kt in range(TT):
                            for tt in range(TT):
                                ins = nc.tensor.transpose(
                                    bk(n)[:, kt * S + tt * P:kt * S + (tt + 1) * P],
                                    LG[:, (hp % 2) * 4 + tt * 2 + h, kt * P:(kt + 1) * P], C("ident"))
                        ins.then_inc(bank_full[n % BANKS], 1)
                    n = order[("o", hp, 0)]
                    pe.wait_ge(bank_read[n % BANKS], emptied(n))
                    for h in range(2):
                        pe.wait_ge(bank_read[(order[("t", hp, h)]) % BANKS], filled(order[("t", hp, h)]))
                        for kt in range(TT):
                            ins = mul(bk(n)[64 * h:64 * h + 64, 0:S], v(hp, h, kt), PTB[:, 2 * h + kt, :],
                                      kt == 0, kt == TT - 1)
                    ins.then_inc(bank_full[n % BANKS], 1)
                order = attention_order(n0, pairs)
                for hp in range(pairs + 1):
                    if hp < pairs:
                        logits(hp)
                    if hp:
                        output(hp - 1)

            def lin_out(name, mixer, pairs):
                pe.wait_ge(bank_read[(attention_order(BANK_AT[mixer], pairs)["o", pairs - 1, 0]) % BANKS], filled(attention_order(BANK_AT[mixer], pairs)["o", pairs - 1, 0]))
                lin8(name, lambda k: MIX[:, k, :])
                for m in range(BANK_AT[name], BANK_AT[name] + 4):
                    pe.wait_ge(bank_read[m % BANKS], filled(m))

            def ffn_and_ple(l):
                layer_norm()
                pe.wait_ge(sems["p_loaded"], L.nxt("p_loaded", 16))
                n = BANK_AT[f"p_in{l}"]
                pe.wait_ge(bank_read[n % BANKS], emptied(n))
                for f in range(2):
                    for tt in range(TT):
                        ins = nc.tensor.transpose(bk(n)[:, f * S + tt * P:f * S + (tt + 1) * P],
                                                  pin[:, tt, f * P:(f + 1) * P], C("ident"))
                ins.then_inc(bank_full[n % BANKS], 1)
                pe.wait_ge(sems["norm_out"], L.nxt("norm_out"))
                clear_acc()
                nm = f"mlp{l}"
                n0, slots = BANK_AT[nm], SLOT_AT[nm]
                base = L.seen.get("ff_act", 0)
                with nc.tensor.Fori(0, 4) as i:
                    for c in range(2):
                        s, u = slots[2 * c]
                        pe.wait_ge(slot_full[s], loaded(u, i))
                        for j in range(2):
                            W = slot(s, KT)
                            pair(n0 + 2 * c + j, lambda h, k: W[:, k, (2 * j + h) * P:(2 * j + h + 1) * P],
                                 lambda k: hT[:, k, :], KT, i)
                        s, u = slots[2 * c + 1]
                        pe.wait_ge(slot_full[s], loaded(u, i))
                        for kk in down(slot(s, 4), lambda kk: FF[:, 4 * c + kk, :], 2):
                            pe.wait_ge(sems["ff_act"], i * 4 + (base + 2 * c + kk // 2 + 1))
                L.seen["ff_act"] = base + 16
                lin8(f"ple_gate{l}", lambda k: hT[:, k, :])
                s, u = SLOT_AT[f"ple_proj{l}"][0]
                pe.wait_ge(slot_full[s], loaded(u))
                pe.wait_ge(bank_read[(BANK_AT[f"p_in{l}"]) % BANKS], filled(BANK_AT[f"p_in{l}"]))
                W = slot(s, 2, D)
                for j in range(4):
                    pair(BANK_AT[f"ple_proj{l}"] + j, lambda h, k: W[:, k, (2 * j + h) * P:(2 * j + h + 1) * P],
                         lambda k: pT[:, k, :], 2)
                pe.wait_ge(sems["ada_summed"], L.nxt("ada_summed", 16))
                n = BANK_AT[f"ada{l}"]
                pe.wait_ge(bank_read[n % BANKS], emptied(n))
                for j in range(48):
                    ins = mul(bk(n)[:, j:j + 1], ADA_SUM[:, j * P:(j + 1) * P], C("ones")[:, 0:1])
                ins.then_inc(bank_full[n % BANKS], 1)
                pe.wait_ge(sems["norm_in"], L.nxt("norm_in"))
                layer_norm()
                pe.wait_ge(sems["norm_out"], L.nxt("norm_out"))

            pe.wait_ge(bank_read[(BANK_AT["dsa_v"]) % BANKS], filled(BANK_AT["dsa_v"]))
            attention("dsa", 4, lambda hp, h, tt: PR[64 * h:64 * h + 64, Q0 + hp, tt * P:(tt + 1) * P],
                      lambda hp, h: PR[64 * h:64 * h + 64, KD, :], lambda hp, h, kt: vi(kt, 0, 64))
            lin_out("hy_out", "dsa", 4)
            ffn_and_ple(0)

            n0 = BANK_AT["mla_down"]
            (s0, u0), (s1, u1) = SLOT_AT["mla_down"]
            pe.wait_ge(slot_full[s0], loaded(u0))
            W0, W1 = slot(s0, KT), slot(s1, KT)
            for j in range(2):
                pair(n0 + j, lambda h, k: W0[:, k, (2 * j + h) * P:(2 * j + h + 1) * P], lambda k: xT[:, k, :], KT)
            pe.wait_ge(slot_full[s1], loaded(u1))
            pair(n0 + 2, lambda h, k: W1[:, k, h * P:(h + 1) * P], lambda k: xT[:, k, :], KT)
            pe.wait_ge(bank_read[(n0 + 3) % BANKS], emptied(n0 + 3))
            for k in range(KT):
                ins = mul(bk(n0 + 3)[64:96, 0:S], W1[:, k, 256:288], xT[:, k, :], k == 0, k == KT - 1)
            ins.then_inc(bank_full[(n0 + 3) % BANKS], 1)
            rms_norm(SQ[:, 0:4, :], 4)
            rms_norm(SQ[:, 4:6, :], 2)
            pe.wait_ge(sems["norm_out"], L.nxt("norm_out"))
            n0 = BANK_AT["mla_uq"]
            for b, (s, u) in enumerate(SLOT_AT["mla_uq"]):
                pe.wait_ge(slot_full[s], loaded(u))
                W = slot(s, 4, 768)
                for j in range(4):
                    pair(n0 + 4 * b + j, lambda h, k: W[:, k, (2 * j + h) * 96:(2 * j + h + 1) * 96],
                         lambda k: CQ[:, k, :], 4, rows=slice(0, 96))
            n0 = BANK_AT["mla_rope"]
            pe.wait_ge(bank_read[(BANK_AT["mla_down"] + 3) % BANKS], filled(BANK_AT["mla_down"] + 3))
            pe.wait_ge(bank_read[n0 % BANKS], emptied(n0))
            mul(bk(n0)[64:96, 0:S], C("swap_rope")[64:96, 64:96], KRAW[64:96, :]).then_inc(bank_full[n0 % BANKS], 1)
            for j in range(8):
                n = n0 + 1 + j
                pe.wait_ge(bank_read[(BANK_AT["mla_uq"] + j) % BANKS], filled(BANK_AT["mla_uq"] + j))
                pe.wait_ge(bank_read[n % BANKS], emptied(n))
                mul(bk(n)[0:96, :], C("swap_rope")[0:96, 0:96], flat(QH[0:96, 2 * j:2 * j + 2, :])).then_inc(bank_full[n % BANKS], 1)
            pe.wait_ge(sems["norm_out"], L.nxt("norm_out"))
            s, u = SLOT_AT["mla_ukv"][0]
            pe.wait_ge(slot_full[s], loaded(u))
            W = slot(s, 2, 2048)
            for j in range(8):
                pair(BANK_AT["mla_k"] + j, lambda h, k: W[:, k, (2 * j + h) * P:(2 * j + h) * P + 64],
                     lambda k: CQ[:, 4 + k, :], 2, rows=slice(0, 64))
            Wv = W.rearrange("p k (h c) -> p k h c", h=MLA_H)
            for tt in range(TT):
                for j in range(2):
                    n = BANK_AT["mla_v"] + 2 * tt + j
                    pe.wait_ge(bank_read[n % BANKS], emptied(n))
                    for k in range(2):
                        ins = mul(bk(n)[:, :], CQ[:, 4 + k, tt * P:(tt + 1) * P], Wv[:, k, 8 * j:8 * j + 8, 64:128],
                                  k == 0, k == 1)
                    ins.then_inc(bank_full[n % BANKS], 1)
            pe.wait_ge(sems["q_roped"], L.nxt("q_roped"))
            pe.wait_ge(sems["kr_spread"], L.nxt("kr_spread"))
            for m in range(BANK_AT["mla_k"] + 4, BANK_AT["mla_k"] + 8):
                pe.wait_ge(bank_read[m % BANKS], filled(m))
            for m in range(BANK_AT["mla_v"], BANK_AT["mla_v"] + 4):
                pe.wait_ge(bank_read[m % BANKS], filled(m))
            vh = flat(VH)
            attention("mla", 8, lambda hp, h, tt: QH[0:96, 2 * hp + h, tt * P:(tt + 1) * P],
                      lambda hp, h: KH[0:96, 2 * hp + h, :],
                      lambda hp, h, kt: vh[:, kt * D + (2 * hp + h) * 64:kt * D + (2 * hp + h + 1) * 64])
            lin_out("mla_out", "mla", 8)
            ffn_and_ple(1)

            for l in range(DEPTH):
                rms_norm()
                pe.wait_ge(sems["norm_out"], L.nxt("norm_out"))
                lin8(f"w_in{l}", lambda k: hT[:, k, :])
                s, u = SLOT_AT[f"w_in_last{l}"][0]
                pe.wait_ge(slot_full[s], loaded(u))
                W = slot(s, KT, 256)
                n0 = BANK_AT[f"w_in{l}"]
                pair(n0 + 20, lambda h, k: W[:, k, h * P:(h + 1) * P], lambda k: hT[:, k, :], KT)
                for m in range(n0 + 17, n0 + 21):
                    pe.wait_ge(bank_read[m % BANKS], filled(m))
                for j in range(4):
                    n = BANK_AT[f"rot{l}"] + j
                    pe.wait_ge(bank_read[n % BANKS], emptied(n))
                    mul(bk(n)[:, :], C("swap"), flat(PR[:, 2 * j:2 * j + 2, :])).then_inc(bank_full[n % BANKS], 1)
                n0 = BANK_AT[f"ret_t{l}"]
                for c in range(TT):
                    pe.wait_ge(bank_read[(n0 + c) % BANKS], emptied(n0 + c))
                    for m in range(4):
                        ins = nc.tensor.transpose(bk(n0 + c)[:, m * P:(m + 1) * P], PR[:, 8 + m, c * P:(c + 1) * P],
                                                  C("ident"))
                    ins.then_inc(bank_full[(n0 + c) % BANKS], 1)
                pe.wait_ge(sems["ret_kq"], L.nxt("ret_kq"))
                pe.wait_ge(bank_read[(n0 + 2) % BANKS], emptied(n0 + 2))
                for m in range(4):
                    ins = nc.tensor.transpose(bk(n0 + 2)[:, m * P:(m + 1) * P], PR[:, 4 + m, 0:P], C("ident"))
                ins.then_inc(bank_full[(n0 + 2) % BANKS], 1)
                n0 = BANK_AT[f"ret{l}"]
                for c in range(TT):
                    pe.wait_ge(bank_read[(n0 + c) % BANKS], emptied(n0 + c))
                    for h in range(RET_H):
                        ins = mul(bk(n0 + c)[:, h * P:(h + 1) * P], PR[:, 4 + h, c * P:(c + 1) * P],
                                  PR[:, h, c * P:(c + 1) * P])
                    ins.then_inc(bank_full[(n0 + c) % BANKS], 1)
                VT, KTD, ST, QD, STATE, RY = (flat(GT[:, x:y, :]) for x, y in
                                              ((4, 8), (8, 10), (10, 14), (14, 16), (16, 18), (18, 22)))
                for m in range(BANK_AT[f"ret_t{l}"], BANK_AT[f"ret_t{l}"] + 3):
                    pe.wait_ge(bank_read[m % BANKS], filled(m))
                pe.wait_ge(bank_read[(n0 + 2) % BANKS], emptied(n0 + 2))
                for h in range(RET_H):
                    ins = mul(bk(n0 + 2)[:, h * P:(h + 1) * P], KTD[:, h * P:(h + 1) * P], VT[:, h * P:(h + 1) * P])
                ins.then_inc(bank_full[(n0 + 2) % BANKS], 1)
                for c in range(TT):
                    pe.wait_ge(bank_read[(n0 + c) % BANKS], filled(n0 + c))
                    if c:
                        pe.wait_ge(bank_read[(n0 + 2) % BANKS], filled(n0 + 2))
                    pe.wait_ge(bank_read[(n0 + 3 + c) % BANKS], emptied(n0 + 3 + c))
                    for h in range(RET_H):
                        hs = slice(h * P, (h + 1) * P)
                        ins = mul(bk(n0 + 3 + c)[:, hs], ST[:, c * 512 + h * P:c * 512 + (h + 1) * P],
                                  VT[:, c * 512 + h * P:c * 512 + (h + 1) * P], True, c == 0)
                        if c:
                            ins = mul(bk(n0 + 3 + c)[:, hs], QD[:, hs], STATE[:, hs], False, True)
                    ins.then_inc(bank_full[(n0 + 3 + c) % BANKS], 1)
                for c in range(TT):
                    pe.wait_ge(sems["ret_norm"], L.nxt("ret_norm"))
                    pe.wait_ge(bank_read[(n0 + 5 + c) % BANKS], emptied(n0 + 5 + c))
                    for h in range(RET_H):
                        ins = nc.tensor.transpose(bk(n0 + 5 + c)[:, h * P:(h + 1) * P],
                                                  RY[:, c * 512 + h * P:c * 512 + (h + 1) * P], C("ident"))
                    ins.then_inc(bank_full[(n0 + 5 + c) % BANKS], 1)

                pe.wait_ge(sems["small_loaded"], L.nxt("small_loaded", 48))
                pe.wait_ge(sems["lora_in"], L.nxt("lora_in", 2))
                n0 = BANK_AT[f"lora{l}"]
                for g in range(3):
                    rows = (slice(0, 64), slice(64, 128), slice(0, 128))[g]
                    w = small_w[rows, 512:1024] if g == 2 else small_w[rows, 0:512]
                    for j in range(2):
                        n = n0 + 2 * g + j
                        pe.wait_ge(bank_read[n % BANKS], emptied(n))
                        for h in range(2):
                            ins = mul(bk(n)[:, h * S:(h + 1) * S], w[:, (2 * j + h) * P:(2 * j + h + 1) * P],
                                      PR[rows, 28 if g < 2 else 29, :])
                        ins.then_inc(bank_full[n % BANKS], 1)
                n0 = BANK_AT[f"head_sum{l}"]
                for g in range(2):
                    pe.wait_ge(sems[("kk_sq", "rw_bonus")[g]], L.nxt(("kk_sq", "rw_bonus")[g]))
                    src = (HI[:, 0:4, :], HI[:, 0:4, :])[g]
                    for j in range(2):
                        n = n0 + 2 * g + j
                        pe.wait_ge(bank_read[n % BANKS], emptied(n))
                        mul(bk(n)[:, :], C("head_ones"), flat(src[:, 2 * j:2 * j + 2, :])).then_inc(bank_full[n % BANKS], 1)
                pe.wait_ge(sems["rw_ops"], L.nxt("rw_ops"))
                n0 = BANK_AT[f"rw_t{l}"]
                for q, (src, c) in enumerate(((PR[:, 24:28, :], 0), (PR[:, 24:28, :], 1), (BT_, 0), (KT_, 0))):
                    pe.wait_ge(bank_read[(n0 + q) % BANKS], emptied(n0 + q))
                    for m in range(4):
                        ins = nc.tensor.transpose(bk(n0 + q)[:, m * P:(m + 1) * P], src[:, m, c * P:(c + 1) * P],
                                                  C("ident"))
                    ins.then_inc(bank_full[(n0 + q) % BANKS], 1)
                n = BANK_AT[f"rwkv{l}"]

                def heads(n, a_, b_, c):
                    for g in range(2):
                        pe.wait_ge(bank_read[(n + g) % BANKS], emptied(n + g))
                        for q in (0, 2, 1, 3):
                            h = 4 * g + q
                            half = slice(64 * (h % 2), 64 * (h % 2) + 64)
                            ins = mul(bk(n + g)[:, q * P:(q + 1) * P], a_[half, h // 2, c * P:(c + 1) * P],
                                      b_[half, h // 2, c * P:(c + 1) * P])
                            if q == 2:
                                ins.then_inc(sems["pe_chain"], 1)
                                pe.wait_ge(sems["pe_chain"], L.up())
                        ins.then_inc(bank_full[(n + g) % BANKS], 1)
                    return n + 2

                def square(n, a_, b_):
                    for g in range(2):
                        pe.wait_ge(bank_read[(n + g) % BANKS], emptied(n + g))
                        for q in range(4):
                            hs = slice((4 * g + q) * P, (4 * g + q + 1) * P)
                            ins = mul(bk(n + g)[:, q * P:(q + 1) * P], a_[:, hs], b_[:, hs])
                        ins.then_inc(bank_full[(n + g) % BANKS], 1)
                    return n + 2

                for c in range(TT):
                    m0 = n
                    n = heads(n, BT_, AT_, c)
                    n = heads(n, KT_, AT_, c)
                    n = heads(n, BT_, RT_, c)
                    n = heads(n, KT_, RT_, c)
                    pe.wait_ge(sems["x_new"], L.nxt("x_new"))
                    for lev in range(7):
                        pe.wait_ge(sems["mm_mask"], L.nxt("mm_mask"))
                        n = square(n, MMs[lev % 2], Xm)
                        pe.wait_ge(bank_read[(n - 2) % BANKS], filled(n - 2))
                        pe.wait_ge(bank_read[(n - 1) % BANKS], filled(n - 1))
                        n = square(n, XTm, Tm)
                        n = square(n, Tm, XTm)
                        pe.wait_ge(bank_read[(n - 4) % BANKS], filled(n - 4))
                        pe.wait_ge(bank_read[(n - 3) % BANKS], filled(n - 3))
                        pe.wait_ge(bank_read[(n - 2) % BANKS], filled(n - 2))
                        pe.wait_ge(bank_read[(n - 1) % BANKS], filled(n - 1))
                    if c == 0:
                        for m in range(BANK_AT[f"rw_t{l}"], BANK_AT[f"rw_t{l}"] + 4):
                            pe.wait_ge(bank_read[m % BANKS], filled(m))
                    def from_state(n, a_, ins):
                        for par in range(2):
                            ins.then_inc(sems["pe_chain"], 1)
                            pe.wait_ge(sems["pe_chain"], L.up())
                            for h in range(par, RW_H, 2):
                                half = slice(64 * par, 64 * par + 64)
                                ins = mul(bk(n)[:, h * 64:h * 64 + 64], a_[half, h // 2, P:2 * P],
                                          S1[half, (h // 2) * 64:(h // 2) * 64 + 64], False, False, skip_group_check=True)
                        return ins

                    pe.wait_ge(bank_read[n % BANKS], emptied(n))
                    for h in range(RW_H):
                        ins = mul(bk(n)[:, h * 64:h * 64 + 64], NTm[:, h * P:(h + 1) * P],
                                  VT2[:, c * 512 + h * 64:c * 512 + h * 64 + 64], h == 0, False, skip_group_check=True)
                    if c:
                        ins = from_state(n, AT_, ins)
                    ins.then_inc(bank_full[n % BANKS], 1)
                    pe.wait_ge(bank_read[n % BANKS], filled(n))
                    n += 1
                    pe.wait_ge(bank_read[n % BANKS], emptied(n))
                    for h in range(RW_H):
                        ins = mul(bk(n)[:, h * 64:h * 64 + 64], XTm[:, h * P:(h + 1) * P], Zm[:, h * 64:h * 64 + 64])
                    ins.then_inc(bank_full[n % BANKS], 1)
                    pe.wait_ge(bank_read[n % BANKS], filled(n))
                    n += 1
                    pe.wait_ge(bank_read[n % BANKS], emptied(n))
                    for h in range(RW_H):
                        o, hp = slice(h * 64, h * 64 + 64), slice(h * P, (h + 1) * P)
                        mul(bk(n)[:, o], RBm[:, hp], Um[:, o], h == 0, False, skip_group_check=True)
                        ins = mul(bk(n)[:, o], RKm[:, hp], VT2[:, c * 512 + h * 64:c * 512 + h * 64 + 64], False, False,
                                  skip_group_check=True)
                    if c:
                        ins = from_state(n, RT_, ins)
                    ins.then_inc(bank_full[n % BANKS], 1)
                    n += 1
                    if c == 0:
                        pe.wait_ge(bank_read[n % BANKS], emptied(n))
                        for h in range(RW_H):
                            half, o = slice(64 * (h % 2), 64 * (h % 2) + 64), slice(h * 64, h * 64 + 64)
                            so = slice((h // 2) * 64, (h // 2) * 64 + 64)
                            mul(bk(n)[half, so], BT0[:, o], Um[:, o], True, False)
                            ins = mul(bk(n)[half, so], KT0[:, o], VT2[:, o], False, True)
                        ins.then_inc(bank_full[n % BANKS], 1)
                        pe.wait_ge(bank_read[n % BANKS], filled(n))
                        n += 1
                    pe.wait_ge(sems["rw_norm"], L.nxt("rw_norm"))
                    pe.wait_ge(bank_read[n % BANKS], emptied(n))
                    for m in range(4):
                        ins = nc.tensor.transpose(bk(n)[:, m * P:(m + 1) * P], YC[:, m * P:(m + 1) * P], C("ident"))
                    ins.then_inc(bank_full[n % BANKS], 1)
                    n += 1
                assert n == BANK_AT[f"rwkv{l}"] + 2 * (8 + 7 * 6 + 4) + 1

                lin8(f"w_gate{l}", lambda k: hT[:, k, :])
                pe.wait_ge(sems["branch_done"], L.nxt("branch_done"))
                for i in range(3):
                    s, u = SLOT_AT[f"w_branch{l}"][i]
                    pe.wait_ge(slot_full[s], loaded(u))
                    W = slot(s, 4)
                    for j in range(4):
                        pair(BANK_AT[f"w_branch{l}"] + 4 * i + j, lambda h, k: W[:, k, (2 * j + h) * P:(2 * j + h + 1) * P],
                             lambda k: YB[:, 4 * i + k, :], 4)
                pe.wait_ge(sems["merged"], L.nxt("merged"))
                lin8(f"w_o{l}", lambda k: R[:, k, :])
                rms_norm()
                pe.wait_ge(sems["norm_out"], L.nxt("norm_out"))
                pe.wait_ge(sems["small_loaded"], L.nxt("small_loaded", 64))
                n0 = BANK_AT[f"route{l}"]
                wr = small_w[:, 0:288].rearrange("p (k n) -> p k n", k=KT)
                pe.wait_ge(bank_read[n0 % BANKS], emptied(n0))
                for tt in range(TT):
                    o = bk(n0)[:, tt * 36:(tt + 1) * 36]
                    mul(o, C("ones")[0:1, :], small_w[0:1, 288:324], True, False)
                    for k in range(KT):
                        ins = mul(o, hT[:, k, tt * P:(tt + 1) * P], wr[:, k, :], False, k == KT - 1)
                ins.then_inc(bank_full[n0 % BANKS], 1)
                for q in range(4):
                    n = n0 + 4 + q
                    tt, d0 = q // 2, 4 * (q % 2)
                    if q == 0:
                        pe.wait_ge(sems["assigned"], L.nxt("assigned"))
                        asg = sm[:, ASG:ASG + 64]
                        pe.wait_ge(bank_read[(n0 + 1) % BANKS], emptied(n0 + 1))
                        mul(bk(n0 + 1)[:, 0:32], C("before"), asg[:, 0:32])
                        mul(bk(n0 + 1)[:, 32:64], C("before"), asg[:, 32:64], True, False)
                        mul(bk(n0 + 1)[:, 32:64], C("ones"), asg[:, 0:32], False, True).then_inc(bank_full[(n0 + 1) % BANKS], 1)
                        pe.wait_ge(sems["over_found"], L.nxt("over_found"))
                        pe.wait_ge(bank_read[(n0 + 2) % BANKS], emptied(n0 + 2))
                        mul(bk(n0 + 2)[:, 0:64], C("ones"), sm[:, W3:W3 + 64]).then_inc(bank_full[(n0 + 2) % BANKS], 1)
                        pe.wait_ge(sems["router_w"], L.nxt("router_w"))
                        pe.wait_ge(bank_read[(n0 + 3) % BANKS], emptied(n0 + 3))
                        for t_ in range(TT):
                            ins = nc.tensor.transpose(bk(n0 + 3)[0:N_EXP, t_ * P:(t_ + 1) * P], sm[:, W3 + t_ * 32:W3 + (t_ + 1) * 32],
                                                      C("ident"))
                        ins.then_inc(bank_full[(n0 + 3) % BANKS], 1)
                    pe.wait_ge(bank_read[n % BANKS], emptied(n))
                    for k in range(4):
                        ins = nc.tensor.transpose(bk(n)[:, k * P:(k + 1) * P], hT[:, d0 + k, tt * P:(tt + 1) * P], C("ident"))
                    ins.then_inc(bank_full[n % BANKS], 1)
                clear_acc()
                for m in range(n0 + 4, n0 + 8):
                    pe.wait_ge(bank_read[m % BANKS], filled(m))
                slots = SLOT_AT[f"moe{l}"]
                e0, r0 = N_EXP * l, N_ROUND * l
                with nc.tensor.Fori(0, N_ROUND) as i:
                    pe.wait_ge(sems["sel_ready"], i + (r0 + l + 1))
                    for q in range(4):
                        if q >= 2:
                            pe.wait_ge(sems[("xs_read_v", "xs_read_a")[q % 2]], i * 2 + (2 * r0 + 1))
                        for h in range(2):
                            for tt in range(TT):
                                d = 2 * q + h
                                ins = mul(bank[q % 2][:, h * S:(h + 1) * S], HTOK[:, tt * D + d * P:tt * D + (d + 1) * P],
                                          SEL[:, tt, :], tt == 0, tt == TT - 1)
                        ins.then_inc(sems["xs_full"], 1)
                    for pr in range(2):
                        for tt in range(TT):
                            ins = nc.tensor.transpose(bank[2][:, pr * S + tt * P:pr * S + (tt + 1) * P],
                                                      SELW[:, tt, pr * P:(pr + 1) * P], C("ident"))
                    ins.then_inc(sems["swt_full"], 1)
                    pe.wait_ge(sems["xs_read_v"], i * 2 + (2 * r0 + 2))
                    pe.wait_ge(sems["xs_read_a"], i * 2 + (2 * r0 + 2))

                    def weights(kind, e):
                        b = MOE_BLOCKS.index((kind, e))
                        s, u = slots[b % SLOTS]
                        pe.wait_ge(slot_full[s], loaded(u + b // SLOTS, i * 3))
                        return slot(s, (KT, KT, 4)[kind])

                    def gate_up(e):
                        if e == 2:
                            pe.wait_ge(sems["gu_read"], i * 2 + (2 * r0 + 1))
                        lo = CAP * (e % 2)
                        half = slice(lo, lo + CAP)
                        for kind in range(2):
                            W = weights(kind, e)
                            for k in range(KT):
                                ins = mul(bank[kind][half, :], XS[:, k, e * CAP:(e + 1) * CAP], W[:, k, :], k == 0, k == KT - 1)
                            ins.then_inc(sems[("gate_used", "gu_full")[kind]], 1)

                    def hidden_transposed(pr):
                        pe.wait_ge(sems["gu_read"], i * 2 + (2 * r0 + pr + 1))
                        if pr == 0:
                            pe.wait_ge(sems["swt_read"], i + (r0 + 1))
                        else:
                            pe.wait_ge(sems["y_read_v"], i * 2 + (2 * r0 + 1))
                        for kk in range(4):
                            ins = nc.tensor.transpose(bank[2][:, kk * P:(kk + 1) * P], SG[:, kk * P:(kk + 1) * P], C("ident"))
                        ins.then_inc(sems["ht_full"], 1)

                    def down_product(e):
                        W = weights(2, e)
                        if e % 2 == 0:
                            pe.wait_ge(sems["ht_read"], i * 2 + (2 * r0 + e // 2 + 1))
                        lo = CAP * (e % 2)
                        half = slice(lo, lo + CAP)
                        for b in range(2):
                            for kk in range(4):
                                ins = mul(bank[2 + b][half, :], HE[:, kk * P + lo:kk * P + lo + CAP],
                                          W[:, kk, b * 512:(b + 1) * 512], kk == 0, kk == 3)
                        ins.then_inc(sems["y_full"], 1)

                    def scatter(pr):
                        pe.wait_ge(sems["y_read_v"], i * 2 + (2 * r0 + pr + 1))
                        pe.wait_ge(sems["y_read_a"], i * 2 + (2 * r0 + pr + 1))
                        for m in range(KT):
                            ins = mul(acc[m // 2][:, (m % 2) * S:(m % 2 + 1) * S], YE[:, m * P:(m + 1) * P], SWT[:, pr, :],
                                      False, False, skip_group_check=True)
                        ins.then_inc(sems["scattered"], 1)

                    gate_up(0)
                    gate_up(1)
                    gate_up(2)
                    hidden_transposed(0)
                    down_product(0)
                    down_product(1)
                    gate_up(3)
                    scatter(0)
                    hidden_transposed(1)
                    down_product(2)
                    down_product(3)
                    scatter(1)

                pe.wait_ge(sems["over_known"], L.nxt("over_known"))
                with nc.tensor.If(nc.tensor.value_load(flag[0:1, 0:1], min_val=0, max_val=2 * S) > 0):
                    F_ = spill[l]

                    def spill_expert(e):
                        for j in range(2):
                            pe.wait_ge(F_[f"spill_slot{j}"], e * 16 + 16)
                        Wg, Wu = slot(1, KT), slot(2, KT)
                        for f in range(4):
                            if not isinstance(e, int):
                                pe.wait_ge(F_[f"spill_read{f}"], e)
                            for h in range(2):
                                for k in range(KT):
                                    ins = mul(bank[f][:, h * S:(h + 1) * S], (Wg, Wu)[h][:, k, f * P:(f + 1) * P], hT[:, k, :],
                                              k == 0, k == KT - 1)
                            ins.then_inc(F_[f"spill_full{f}"], 1)
                        pe.wait_ge(F_["spill_slot2"], e * 16 + 16)
                        W = slot(3, 4)
                        for kk in range(4):
                            pe.wait_ge(F_["spill_h"], e * 4 + (kk + 1))
                            for m in range(KT):
                                ins = mul(acc[m // 2][:, (m % 2) * S:(m % 2 + 1) * S], W[:, kk, m * P:(m + 1) * P], FF[:, kk, :],
                                          False, False, skip_group_check=True)
                        ins.then_inc(F_["spill_down"], 1)
                    spill_expert(0)
                    with nc.tensor.Fori(1, N_EXP) as e:
                        spill_expert(e)
            rms_norm()
            pe.wait_ge(sems["norm_out"], L.nxt("norm_out"))
            n0 = BANK_AT["x_out"]
            for j in range(4):
                tt, q = j // 2, j % 2
                pe.wait_ge(bank_read[(n0 + j) % BANKS], emptied(n0 + j))
                for k in range(4):
                    ins = nc.tensor.transpose(bk(n0 + j)[:, k * P:(k + 1) * P], hT[:, 4 * q + k, tt * P:(tt + 1) * P],
                                              C("ident"))
                ins.then_inc(bank_full[(n0 + j) % BANKS], 1)

        CS, GA1, GA2 = 0, 8, 16
        IW, M8, MX, NB, RS = 24, 32, 48, 56, 64
        LAM, LIN = 72, 80
        CMID, CEND, CEXP, OMKA = 84, 92, 96, 100
        HS, HV = 104, 112
        RL, RT, R8 = 128, 200, 250

        def layer_vec(name, k):
            return V_(name)[:, k:k + 1]

        @block.vector
        def _(dve):
            L = Count()
            v = nc.vector

            def copy_out(n, dst, src=None):
                dve.wait_ge(bank_full[n % BANKS], filled(n))
                v.tensor_copy(dst, bk(n)[:, :] if src is None else src).then_inc(bank_read[n % BANKS], 1)

            def stats(width, eps):
                dve.wait_ge(sems["norm_sum"], L.nxt("norm_sum"))
                v.tensor_scalar(stat[:, 1, :], acc[3][:, 0:S], 1.0 / width, eps, ALU.mult, ALU.add).then_inc(sems["norm_var"], 1)
                dve.wait_ge(sems["norm_std"], L.nxt("norm_std"))
                v.reciprocal(stat[:, 1, :], stat[:, 1, :]).then_inc(sems["vec_chain"], 1)
                dve.wait_ge(sems["vec_chain"], L.up())

            def layer_norm():
                dve.wait_ge(sems["norm_sum"], L.nxt("norm_sum"))
                v.tensor_scalar(stat[:, 0, :], acc[3][:, 0:S], 1.0 / D, None, ALU.mult).then_inc(sems["vec_chain"], 1)
                dve.wait_ge(sems["vec_chain"], L.up())
                v.tensor_tensor(R[:, :, :], R[:, :, :], bcast(stat[:, 0, :], KT), ALU.subtract).then_inc(sems["norm_centered"], 1)
                dve.wait_ge(sems["norm_centered"], L.nxt("norm_centered"))
                stats(D, 1e-5)
                v.tensor_tensor(R[:, :, :], R[:, :, :], bcast(stat[:, 1, :], KT), ALU.mult).then_inc(sems["norm_scaled"], 1)
                dve.wait_ge(sems["norm_out"], L.nxt("norm_out"))

            def rms_norm(src, dst, K, width):
                stats(width, 1e-6)
                v.tensor_tensor(dst, src, bcast(stat[:, 1, :], K), ALU.mult).then_inc(sems["norm_scaled"], 1)
                dve.wait_ge(sems["norm_out"], L.nxt("norm_out"))

            n0 = BANK_AT["x_in"]
            for j in range(4):
                copy_out(n0 + j, flat(xT[:, 2 * j:2 * j + 2, :]))
            dve.wait_ge(sems["inputs_loaded"], 32)
            lam = V_("lam")
            v.scalar_tensor_tensor(sm[:, LAM:LAM + 4], lam, -1.0, lam, ALU.mult, ALU.min).then_inc(sems["lam_abs"], 1)
            v.tensor_scalar(sm[:, LIN:LIN + 4], lam, -1.0, 0.0, ALU.mult, ALU.max).then_inc(sems["vec_chain"], 1)
            dve.wait_ge(sems["vec_chain"], L.up())
            dve.wait_ge(sems["lam_log"], L.nxt("lam_log"))
            v.tensor_tensor(sm[:, LIN:LIN + 4], sm[:, LIN:LIN + 4], sm[:, LAM:LAM + 4], ALU.add).then_inc(sems["vec_chain"], 1)
            dve.wait_ge(sems["vec_chain"], L.up())
            v.tensor_scalar(sm[:, LIN:LIN + 4], sm[:, LIN:LIN + 4], 4.0, None, ALU.mult).then_inc(sems["vec_chain"], 1)
            dve.wait_ge(sems["vec_chain"], L.up())

            dve.wait_ge(sems["c_sig"], L.nxt("c_sig"))
            v.tensor_tensor(sm[:, CS:CS + 8], sm[:, CS:CS + 8], V_("c"), ALU.mult).then_inc(sems["c_silu"], 1)
            dve.wait_ge(sems["c_silu"], L.nxt("c_silu"))

            n0 = BANK_AT["hy_in"]
            for j in range(0, 8, 2):
                copy_out(n0 + j, flat(PR[:, 2 * j:2 * j + 2, :]))
            n = BANK_AT["dsa_v"]
            dve.wait_ge(bank_full[n % BANKS], filled(n))
            v.tensor_copy(flat(VI)[:, 0:136], bk(n)[:, 0:136]).then_inc(bank_read[n % BANKS], 1)
            dve.wait_ge(bank_read[n % BANKS], filled(n))
            for tt in range(TT):
                v.tensor_scalar(sm[:, IW + 4 * tt:IW + 4 * tt + 4], vi(tt, 64, 68), IDX_H ** -0.5 * 64 ** -0.5, None, ALU.mult).then_inc(sems["vec_chain"], 1)
                dve.wait_ge(sems["vec_chain"], L.up())
            dve.wait_ge(bank_read[n0 % BANKS], filled(n0))
            dve.wait_ge(bank_read[(n0 + 1) % BANKS], filled(n0 + 1))
            for c in range(4):
                src, dst = PR[:, XR + c, :], PR[:, XC + c, :]
                v.tensor_scalar(dst, src, layer_vec("conv_w3", c), layer_vec("conv_b", c), ALU.mult, ALU.add).then_inc(sems["vec_chain"], 1)
                dve.wait_ge(sems["vec_chain"], L.up())
                for i in (2, 1, 0):
                    sh = 3 - i
                    ins = v.scalar_tensor_tensor(dst[:, sh:S], src[:, 0:S - sh], layer_vec(f"conv_w{i}", c), dst[:, sh:S],
                                                 ALU.mult, ALU.add)
                    if i == 0 and c == 3:
                        ins.then_inc(sems["conv_done"], 1)
                    else:
                        ins.then_inc(sems["vec_chain"], 1)
                        dve.wait_ge(sems["vec_chain"], L.up())
            dve.wait_ge(sems["conv_done"], L.nxt("conv_done"))
            yr, z = flat(PR[:, YR:YR + 4, :]), flat(R[:, 0:4, :])
            dve.wait_ge(bank_read[(n0 + 2) % BANKS], filled(n0 + 2))
            dve.wait_ge(bank_read[(n0 + 3) % BANKS], filled(n0 + 3))
            v.tensor_tensor(z, yr, yr, ALU.mult).then_inc(sems["vec_chain"], 1)
            dve.wait_ge(sems["vec_chain"], L.up())
            v.tensor_scalar(z, z, 0.044715, 1.0, ALU.mult, ALU.add).then_inc(sems["vec_chain"], 1)
            dve.wait_ge(sems["vec_chain"], L.up())
            v.tensor_tensor(z, z, yr, ALU.mult).then_inc(sems["gelu_in"], 1)
            g0 = BANK_AT["rg_gates"]
            dve.wait_ge(bank_read[g0 % BANKS], filled(g0))
            dve.wait_ge(bank_read[(g0 + 1) % BANKS], filled(g0 + 1))
            dve.wait_ge(bank_read[(g0 + 2) % BANKS], filled(g0 + 2))
            dve.wait_ge(bank_read[(g0 + 3) % BANKS], filled(g0 + 3))
            for c in range(4):
                ins = v.tensor_scalar(PR[:, RG + c, :], PR[:, RG + c, :], sm[:, LIN + c:LIN + c + 1], None, ALU.mult)
                if c < 3:
                    ins.then_inc(sems["vec_chain"], 1)
                    dve.wait_ge(sems["vec_chain"], L.up())
            ins.then_inc(sems["decay_in"], 1)
            xc, th, ig, den = (flat(q) for q in (PR[:, XC:XC + 4, :], PR[:, RG:RG + 4, :], PR[:, IG:IG + 4, :], R[:, 4:8, :]))
            v.tensor_tensor(ig, ig, xc, ALU.mult).then_inc(sems["vec_chain"], 1)
            dve.wait_ge(sems["vec_chain"], L.up())
            dve.wait_ge(sems["decay_tanh"], L.nxt("decay_tanh"))
            v.tensor_scalar(den, th, 1.0, None, ALU.add).then_inc(sems["decay_den"], 1)
            dve.wait_ge(sems["decay_den"], L.nxt("decay_den"))
            v.reciprocal(den, den).then_inc(sems["vec_chain"], 1)
            dve.wait_ge(sems["vec_chain"], L.up())
            v.tensor_tensor(ig, ig, den, ALU.mult).then_inc(sems["vec_chain"], 1)
            dve.wait_ge(sems["vec_chain"], L.up())
            dve.wait_ge(sems["decay_sqrt"], L.nxt("decay_sqrt"))
            v.scalar_tensor_tensor(ig, th, 2.0, ig, ALU.mult, ALU.mult).then_inc(sems["vec_chain"], 1)
            dve.wait_ge(sems["vec_chain"], L.up())
            v.tensor_scalar(den, den, 2.0, -1.0, ALU.mult, ALU.add).then_inc(sems["vec_chain"], 1)
            dve.wait_ge(sems["vec_chain"], L.up())
            for c in range(4):
                v.tensor_tensor_scan(PR[:, XC + c, :], R[:, 4 + c, :], PR[:, IG + c, :], 0.0, ALU.mult, ALU.add).then_inc(sems["vec_chain"], 1)
                dve.wait_ge(sems["vec_chain"], L.up())
            dve.wait_ge(sems["gelu_sig"], L.nxt("gelu_sig"))
            v.tensor_tensor(z, z, yr, ALU.mult).then_inc(sems["vec_chain"], 1)
            dve.wait_ge(sems["vec_chain"], L.up())
            v.tensor_tensor(flat(MIX[:, 0:4, :]), z, xc, ALU.mult).then_inc(sems["vec_chain"], 1)
            dve.wait_ge(sems["vec_chain"], L.up())
            i0 = BANK_AT["idx"]
            for m in range(i0, i0 + 4):
                dve.wait_ge(bank_read[m % BANKS], filled(m))
            for tt in range(TT):
                for h in range(IDX_H):
                    w = sm[:, IW + 4 * tt + h:IW + 4 * tt + h + 1]
                    if h == 0:
                        v.tensor_scalar(ISC[:, tt, :], RELU[:, 4 * tt, :], w, None, ALU.mult).then_inc(sems["vec_chain"], 1)
                        dve.wait_ge(sems["vec_chain"], L.up())
                    else:
                        v.scalar_tensor_tensor(ISC[:, tt, :], RELU[:, 4 * tt + h, :], w, ISC[:, tt, :], ALU.mult, ALU.add).then_inc(sems["vec_chain"], 1)
                        dve.wait_ge(sems["vec_chain"], L.up())
            isc, adm = flat(ISC), flat(ADM)
            v.tensor_tensor(isc, isc, C("causal"), ALU.mult).then_inc(sems["vec_chain"], 1)
            dve.wait_ge(sems["vec_chain"], L.up())
            v.tensor_tensor(isc, isc, C("noncausal"), ALU.add).then_inc(sems["vec_chain"], 1)
            dve.wait_ge(sems["vec_chain"], L.up())
            for _ in range(TOPK // 8):
                for tt in range(TT):
                    m8 = sm[:, M8 + 8 * tt:M8 + 8 * tt + 8]
                    v.max(m8, ISC[:, tt, :]).then_inc(sems["vec_chain"], 1)
                    dve.wait_ge(sems["vec_chain"], L.up())
                    v.match_replace(ISC[:, tt, :], m8, ISC[:, tt, :], TAKEN).then_inc(sems["vec_chain"], 1)
                    dve.wait_ge(sems["vec_chain"], L.up())
            v.tensor_scalar(adm, isc, -2e38, BIG, ALU.is_le, ALU.mult).then_inc(sems["vec_chain"], 1)
            dve.wait_ge(sems["vec_chain"], L.up())
            v.tensor_tensor(adm, adm, C("causal"), ALU.mult).then_inc(sems["vec_chain"], 1)
            dve.wait_ge(sems["vec_chain"], L.up())
            v.tensor_scalar(adm, adm, -BIG, None, ALU.add).then_inc(sems["vec_chain"], 1)
            dve.wait_ge(sems["vec_chain"], L.up())

            def attention(name, pairs, scale, mix0, slopes=None):
                order = attention_order(BANK_AT[name], pairs)

                def softmax(hp):
                    q = 4 * (hp % 2)
                    for tt in range(TT):
                        n = order["l", hp, tt]
                        dve.wait_ge(bank_full[n % BANKS], filled(n))
                        dst = LG[:, q + 2 * tt:q + 2 * tt + 2, :]
                        if slopes:
                            for h in range(2):
                                ins = v.scalar_tensor_tensor(dst[:, h, :], C("dist")[:, tt * S:(tt + 1) * S],
                                                             -slopes[2 * hp + h] / scale, bk(n)[:, h * S:(h + 1) * S],
                                                             ALU.mult, ALU.add)
                                if h:
                                    ins.then_inc(bank_read[n % BANKS], 1)
                                else:
                                    ins.then_inc(sems["vec_chain"], 1)
                                    dve.wait_ge(sems["vec_chain"], L.up())
                            dve.wait_ge(bank_read[n % BANKS], filled(n))
                            v.tensor_tensor(dst, dst, bcast(ADM[:, tt, :], 2), ALU.add).then_inc(sems["vec_chain"], 1)
                            dve.wait_ge(sems["vec_chain"], L.up())
                        else:
                            v.tensor_tensor(dst, two(bk(n)[:, :]), bcast(C("noncausal")[:, tt * S:(tt + 1) * S], 2), ALU.add).then_inc(bank_read[n % BANKS], 1)
                            dve.wait_ge(bank_read[n % BANKS], filled(n))
                    p_ = q
                    v.tensor_reduce(sm[:, MX + p_:MX + p_ + 4], LG[:, q:q + 4, :], AX.X, ALU.max).then_inc(sems["vec_chain"], 1)
                    dve.wait_ge(sems["vec_chain"], L.up())
                    v.tensor_scalar(sm[:, NB + p_:NB + p_ + 4], sm[:, MX + p_:MX + p_ + 4], -scale, None, ALU.mult).then_inc(sems["dsa_max"], 1)
                    dve.wait_ge(sems["dsa_exp"], L.nxt("dsa_exp"))
                    v.reciprocal(sm[:, RS + p_:RS + p_ + 4], sm[:, RS + p_:RS + p_ + 4]).then_inc(sems["vec_chain"], 1)
                    dve.wait_ge(sems["vec_chain"], L.up())
                    v.tensor_tensor(LG[:, q:q + 4, :], LG[:, q:q + 4, :],
                                        sm[:, RS + p_:RS + p_ + 4].unsqueeze(2).to_broadcast([P, 4, S]), ALU.mult).then_inc(sems["dsa_probs"], 1)

                for hp in range(pairs + 1):
                    if hp < pairs:
                        softmax(hp)
                    if hp:
                        n = order["o", hp - 1, 0]
                        dve.wait_ge(bank_full[n % BANKS], filled(n))
                        v.tensor_copy(MIX[:, mix0 + hp - 1, :], bk(n)[:, 0:S]).then_inc(bank_read[n % BANKS], 1)
                        dve.wait_ge(bank_read[n % BANKS], filled(n))

            def out_and_norm(name):
                for j in range(4):
                    n = BANK_AT[name] + j
                    dve.wait_ge(bank_full[n % BANKS], filled(n))
                    v.scalar_tensor_tensor(R[:, 2 * j:2 * j + 2, :], xT[:, 2 * j:2 * j + 2, :], ALPHA, two(bk(n)[:, :]),
                                                ALU.mult, ALU.add).then_inc(bank_read[n % BANKS], 1)
                for m in range(BANK_AT[name], BANK_AT[name] + 4):
                    dve.wait_ge(bank_read[m % BANKS], filled(m))
                layer_norm()

            def ada(l):
                a0 = 16 * l

                def half(k, h):
                    dve.wait_ge(sems[f"ada_loaded{h}"], k * 16 + (8 * a0 + 16))
                    total = ADA_SUM[:, h * ADA_N:(h + 1) * ADA_N]
                    if isinstance(k, int):
                        v.tensor_scalar(total, ADA[h], sm[:, CS:CS + 1], None, ALU.mult).then_inc(sems["ada_summed"], 1)
                    else:
                        dve.wait_ge(sems["ada_summed"], k * 2 + (a0 + h - 1))
                        v.scalar_tensor_tensor(total, ADA[h], sm[:, bass.ds(k, 1)], total, ALU.mult, ALU.add).then_inc(
                            sems["ada_summed"], 1)
                half(0, 0)
                half(0, 1)
                with nc.vector.Fori(1, KT) as k:
                    half(k, 0)
                    half(k, 1)

            def ffn_and_ple(l):
                ada(l)
                dve.wait_ge(sems["down_done"], L.nxt("down_done", 8))
                for b in range(4):
                    ins = v.scalar_tensor_tensor(R[:, 2 * b:2 * b + 2, :], hT[:, 2 * b:2 * b + 2, :], ALPHA, two(acc[b][:, :]),
                                                 ALU.mult, ALU.add)
                    ins.then_inc(sems["vec_chain"], 1)
                    dve.wait_ge(sems["vec_chain"], L.up())
                g0, n0 = BANK_AT[f"ple_gate{l}"], BANK_AT[f"ple_proj{l}"]
                for j in range(4):
                    dve.wait_ge(bank_read[(g0 + j) % BANKS], filled(g0 + j))
                    dve.wait_ge(bank_full[(n0 + j) % BANKS], filled(n0 + j))
                    q = flat(SQ[:, 2 * j:2 * j + 2, :])
                    v.tensor_tensor(q, q, bk(n0 + j)[:, :], ALU.mult).then_inc(bank_read[(n0 + j) % BANKS], 1)
                for m in range(n0, n0 + 4):
                    dve.wait_ge(bank_read[m % BANKS], filled(m))
                v.tensor_tensor(flat(R[:, :, :]), flat(R[:, :, :]), flat(SQ[:, :, :]), ALU.add).then_inc(sems["norm_in"], 1)
                dve.wait_ge(sems["norm_in"], L.nxt("norm_in"))
                n = BANK_AT[f"ada{l}"]
                dve.wait_ge(bank_full[n % BANKS], filled(n))
                v.tensor_tensor(mod[:, 48 * l:48 * l + 48], bk(n)[:, 0:48], V_(f"b_ada{l}"), ALU.add).then_inc(bank_read[n % BANKS], 1)
                dve.wait_ge(bank_read[n % BANKS], filled(n))
                layer_norm()

            attention("dsa", 4, DSA_D ** -0.5, 4, [2.0 ** (-8.0 * (h + 1) / DSA_H) for h in range(DSA_H)])
            out_and_norm("hy_out")
            ffn_and_ple(0)

            n0 = BANK_AT["mla_down"]
            for j in range(3):
                copy_out(n0 + j, flat(CQ[:, 2 * j:2 * j + 2, :]))
            dve.wait_ge(bank_full[(n0 + 3) % BANKS], filled(n0 + 3))
            v.tensor_copy(KRAW[64:96, :], bk(n0 + 3)[64:96, 0:S]).then_inc(bank_read[(n0 + 3) % BANKS], 1)
            for m in range(n0, n0 + 4):
                dve.wait_ge(bank_read[m % BANKS], filled(m))
            rms_norm(CQ[:, 0:4, :], CQ[:, 0:4, :], 4, QL)
            rms_norm(CQ[:, 4:6, :], CQ[:, 4:6, :], 2, KVL)
            n0 = BANK_AT["mla_uq"]
            r0 = BANK_AT["mla_rope"]
            for j in range(0, 8, 2):
                dve.wait_ge(bank_full[(n0 + j) % BANKS], filled(n0 + j))
                v.tensor_copy(flat(QH[0:96, 2 * j:2 * j + 2, :]), bk(n0 + j)[0:96, :]).then_inc(bank_read[(n0 + j) % BANKS], 1)
            dve.wait_ge(bank_full[r0 % BANKS], filled(r0))
            v.tensor_tensor(R[64:96, 7, :], bk(r0)[64:96, 0:S], C("rope_sin")[64:96, :], ALU.mult).then_inc(bank_read[r0 % BANKS], 1)
            v.tensor_tensor(KROT[64:96, :], KRAW[64:96, :], C("rope_cos")[64:96, :], ALU.mult).then_inc(sems["vec_chain"], 1)
            dve.wait_ge(sems["vec_chain"], L.up())
            dve.wait_ge(bank_read[r0 % BANKS], filled(r0))
            v.tensor_tensor(KROT[64:96, :], KROT[64:96, :], R[64:96, 7, :], ALU.add).then_inc(sems["kr_rope"], 1)
            for j in range(8):
                n = r0 + 1 + j
                dve.wait_ge(bank_full[n % BANKS], filled(n))
                dve.wait_ge(bank_read[(n0 + j) % BANKS], filled(n0 + j))
                q, t_ = QH[0:96, 2 * j:2 * j + 2, :], R[0:96, 2 * (j % 2):2 * (j % 2) + 2, :]
                v.tensor_tensor(q, q, bcast(C("rope_cos")[0:96, :], 2), ALU.mult).then_inc(sems["vec_chain"], 1)
                dve.wait_ge(sems["vec_chain"], L.up())
                v.tensor_tensor(t_, two(bk(n)[0:96, :]), bcast(C("rope_sin")[0:96, :], 2), ALU.mult).then_inc(bank_read[n % BANKS], 1)
                dve.wait_ge(bank_read[n % BANKS], filled(n))
                ins = v.tensor_tensor(q, q, t_, ALU.add)
                if j < 7:
                    ins.then_inc(sems["vec_chain"], 1)
                    dve.wait_ge(sems["vec_chain"], L.up())
                else:
                    ins.then_inc(sems["q_roped"], 1)
            attention("mla", 8, (NOPE + ROPE) ** -0.5, 0)
            out_and_norm("mla_out")
            ffn_and_ple(1)

            dve.wait_ge(sems["pos_loaded"], 16)
            ang, red, tmp = R[:, 0, :], R[:, 1, :], R[:, 2, :]
            v.tensor_copy(ang, posi[:, :]).then_inc(sems["vec_chain"], 1)
            dve.wait_ge(sems["vec_chain"], L.up())
            v.tensor_scalar(ang, ang, C("inv_freq"), None, ALU.mult).then_inc(sems["vec_chain"], 1)
            dve.wait_ge(sems["vec_chain"], L.up())
            for q, (dst, shift) in enumerate(((sinT, 0.0), (cosT, 0.25))):
                v.tensor_scalar(tmp, ang, 1.0 / (2 * math.pi), shift, ALU.mult, ALU.add).then_inc(sems["vec_chain"], 1)
                dve.wait_ge(sems["vec_chain"], L.up())
                v.tensor_scalar(tmp, tmp, 12582912.0, None, ALU.add).then_inc(sems["vec_chain"], 1)
                dve.wait_ge(sems["vec_chain"], L.up())
                v.tensor_scalar(tmp, tmp, -12582912.0, None, ALU.add).then_inc(sems["vec_chain"], 1)
                dve.wait_ge(sems["vec_chain"], L.up())
                v.tensor_copy(red, ang).then_inc(sems["vec_chain"], 1)
                dve.wait_ge(sems["vec_chain"], L.up())
                for part in TWO_PI:
                    v.scalar_tensor_tensor(red, tmp, -part, red, ALU.mult, ALU.add).then_inc(sems["vec_chain"], 1)
                    dve.wait_ge(sems["vec_chain"], L.up())
                v.tensor_scalar(red, red, shift * 2 * math.pi, 3.1415925, ALU.add, ALU.min).then_inc(sems["vec_chain"], 1)
                dve.wait_ge(sems["vec_chain"], L.up())
                v.tensor_scalar(dst[:, :], red, -3.1415925, None, ALU.max).then_inc(sems["rot_in"], 1)
                dve.wait_ge(sems["rot_in"], L.nxt("rot_in"))
            dve.wait_ge(sems["rot_tables"], L.nxt("rot_tables", 2))
            v.tensor_scalar(sinT[:, :], sinT[:, :], C("sin_sign"), None, ALU.mult).then_inc(sems["vec_chain"], 1)
            dve.wait_ge(sems["vec_chain"], L.up())

            for l in range(DEPTH):
                m0 = 48 * l
                ml = mod[:, m0:m0 + 48]
                for g, o in ((GA1, 8), (GA2, 32)):
                    v.tensor_scalar(sm[:, g:g + 8], ml[:, o:o + 8], 1.0, None, ALU.add).then_inc(sems["vec_chain"], 1)
                    dve.wait_ge(sems["vec_chain"], L.up())
                    nm = f"norm{1 if g == GA1 else 2}_g{l}"
                    ins = v.tensor_tensor(sm[:, g:g + 8], sm[:, g:g + 8], V_(nm), ALU.mult)
                    if g == GA1:
                        ins.then_inc(sems["vec_chain"], 1)
                        dve.wait_ge(sems["vec_chain"], L.up())
                ins.then_inc(sems["mod_done"], 1)
                rms_norm(xT[:, :, :], hT[:, :, :], KT, D)
                n0 = BANK_AT[f"w_in{l}"]
                with nc.vector.Fori(0, 5) as i:
                    for j in (0, 2):
                        dve.wait_ge(bank_full[(n0 + j) % BANKS], filled(n0 + j, i))
                        v.tensor_copy(PR[:, bass.ds(i * 8 + 2 * j, 2), :], two(bk(n0 + j)[:, :])).then_inc(bank_read[(n0 + j) % BANKS], 1)
                copy_out(n0 + 20, flat(PR[:, 40:42, :]))
                for m in range(n0 + 17, n0 + 21):
                    dve.wait_ge(bank_read[m % BANKS], filled(m))
                u, cv = PR[:, 30:34, :], R[:, 0:4, :]
                v.tensor_tensor(flat(u), flat(u), flat(PR[:, 38:42, :]), ALU.mult).then_inc(sems["vec_chain"], 1)
                dve.wait_ge(sems["vec_chain"], L.up())
                for c in range(4):
                    v.tensor_scalar(cv[:, c, :], u[:, c, :], layer_vec(f"cw{l}2", c), None, ALU.mult).then_inc(sems["vec_chain"], 1)
                    dve.wait_ge(sems["vec_chain"], L.up())
                    for i in (0, 1):
                        sh = 2 - i
                        v.scalar_tensor_tensor(cv[:, c, sh:S], u[:, c, 0:S - sh], layer_vec(f"cw{l}{i}", c),
                                                    cv[:, c, sh:S], ALU.mult, ALU.add).then_inc(sems["vec_chain"], 1)
                        dve.wait_ge(sems["vec_chain"], L.up())
                v.tensor_tensor(flat(YB[:, 8:12, :]), flat(cv), flat(PR[:, 34:38, :]), ALU.mult).then_inc(sems["vec_chain"], 1)
                dve.wait_ge(sems["vec_chain"], L.up())

                r0 = BANK_AT[f"rot{l}"]
                for j in range(4):
                    dve.wait_ge(bank_full[(r0 + j) % BANKS], filled(r0 + j))
                    q, t_ = PR[:, 2 * j:2 * j + 2, :], R[:, 4 + 2 * (j % 2):6 + 2 * (j % 2), :]
                    v.tensor_tensor(q, q, bcast(cosT[:, :], 2), ALU.mult).then_inc(sems["vec_chain"], 1)
                    dve.wait_ge(sems["vec_chain"], L.up())
                    v.tensor_tensor(t_, two(bk(r0 + j)[:, :]), bcast(sinT[:, :], 2), ALU.mult).then_inc(bank_read[(r0 + j) % BANKS], 1)
                    dve.wait_ge(bank_read[(r0 + j) % BANKS], filled(r0 + j))
                    ins = v.tensor_tensor(q, q, t_, ALU.add)
                    if j < 3:
                        ins.then_inc(sems["vec_chain"], 1)
                        dve.wait_ge(sems["vec_chain"], L.up())
                    else:
                        ins.then_inc(sems["ret_kq"], 1)
                        dve.wait_ge(sems["ret_kq"], L.nxt("ret_kq"))
                VT, KTD, ST, QD, STATE, RY = (flat(GT[:, x:y, :]) for x, y in
                                              ((4, 8), (8, 10), (10, 14), (14, 16), (16, 18), (18, 22)))
                h4 = lambda ap: ap.rearrange("p (h d) -> p h d", h=4)
                v.tensor_tensor(h4(QD), PR[:, 0:4, P:2 * P], h4(C("ret_decay_q")), ALU.mult).then_inc(sems["vec_chain"], 1)
                dve.wait_ge(sems["vec_chain"], L.up())
                n = BANK_AT[f"ret_t{l}"] + 2
                dve.wait_ge(bank_full[n % BANKS], filled(n))
                v.tensor_tensor(h4(KTD), h4(bk(n)[:, :]), C("ret_decay_k").unsqueeze(2).to_broadcast([P, 4, P]), ALU.mult).then_inc(bank_read[n % BANKS], 1)
                r0 = BANK_AT[f"ret{l}"]
                for c in range(TT):
                    dve.wait_ge(bank_full[(r0 + c) % BANKS], filled(r0 + c))
                    v.tensor_tensor(ST[:, c * 512:(c + 1) * 512], bk(r0 + c)[:, :], C("ret_decay_in"), ALU.mult).then_inc(bank_read[(r0 + c) % BANKS], 1)
                copy_out(r0 + 2, STATE)
                dve.wait_ge(sems["g_sig"], L.nxt("g_sig"))
                g_ = PR[:, 12:16, :]
                v.tensor_tensor(flat(g_), flat(g_), flat(GT[:, 0:4, :]), ALU.mult).then_inc(sems["vec_chain"], 1)
                dve.wait_ge(sems["vec_chain"], L.up())
                for c in range(4):
                    v.tensor_scalar(g_[:, c, :], g_[:, c, :], layer_vec(f"ret_gn{l}", c), None, ALU.mult).then_inc(sems["vec_chain"], 1)
                    dve.wait_ge(sems["vec_chain"], L.up())

                def head_norm(n, dst, sq, H, eps, name):
                    hd = lambda ap: ap.rearrange("p (h d) -> p h d", h=H)
                    W = 512 // H
                    mean, var = sm[:, HS:HS + H], sm[:, HV:HV + H]
                    dve.wait_ge(bank_full[n % BANKS], filled(n))
                    v.tensor_reduce(mean, hd(bk(n)[:, :]), AX.X, ALU.add).then_inc(sems["vec_chain"], 1)
                    dve.wait_ge(sems["vec_chain"], L.up())
                    v.tensor_scalar(mean, mean, 1.0 / W, None, ALU.mult).then_inc(sems["vec_chain"], 1)
                    dve.wait_ge(sems["vec_chain"], L.up())
                    v.tensor_tensor(hd(dst), hd(bk(n)[:, :]), mean.unsqueeze(2).to_broadcast([P, H, W]), ALU.subtract).then_inc(bank_read[n % BANKS], 1)
                    dve.wait_ge(bank_read[n % BANKS], filled(n))
                    v.tensor_tensor(sq, dst, dst, ALU.mult).then_inc(sems["vec_chain"], 1)
                    dve.wait_ge(sems["vec_chain"], L.up())
                    v.tensor_reduce(var, hd(sq), AX.X, ALU.add).then_inc(sems["vec_chain"], 1)
                    dve.wait_ge(sems["vec_chain"], L.up())
                    v.tensor_scalar(var, var, 1.0 / W, eps, ALU.mult, ALU.add).then_inc(sems["head_var"], 1)
                    dve.wait_ge(sems["head_std"], L.nxt("head_std"))
                    v.reciprocal(var, var).then_inc(sems["vec_chain"], 1)
                    dve.wait_ge(sems["vec_chain"], L.up())
                    v.tensor_tensor(hd(dst), hd(dst), var.unsqueeze(2).to_broadcast([P, H, W]), ALU.mult).then_inc(sems[name], 1)

                for c in range(TT):
                    head_norm(r0 + 3 + c, RY[:, c * 512:(c + 1) * 512], flat(R[:, 0:2, :]), RET_H, 1e-5, "ret_norm")
                for c in range(TT):
                    n = r0 + 5 + c
                    dve.wait_ge(bank_full[n % BANKS], filled(n))
                    ins = v.tensor_tensor(YB[:, 0:4, c * P:(c + 1) * P], h4(bk(n)[:, :]), g_[:, :, c * P:(c + 1) * P], ALU.mult)
                    ins.then_inc(bank_read[n % BANKS], 1)
                dve.wait_ge(bank_read[(r0 + 6) % BANKS], filled(r0 + 6))

                p_, d_ = PR[:, 16:30, :], PR[:, 0:14, :]
                v.tensor_tensor(d_[:, :, 1:S], p_[:, :, 0:S - 1], p_[:, :, 1:S], ALU.subtract).then_inc(sems["vec_chain"], 1)
                dve.wait_ge(sems["vec_chain"], L.up())
                v.tensor_scalar(d_[:, :, 0:1], p_[:, :, 0:1], -1.0, None, ALU.mult).then_inc(sems["vec_chain"], 1)
                dve.wait_ge(sems["vec_chain"], L.up())
                for t_ in (12, 13, *range(12)):
                    ins = v.scalar_tensor_tensor(p_[:, t_, :], d_[:, t_, :], layer_vec(f"mu{l}", t_), p_[:, t_, :], ALU.mult, ALU.add)
                    if t_ == 13:
                        ins.then_inc(sems["mixed"], 1)
                        dve.wait_ge(sems["mixed"], L.nxt("mixed"))
                    else:
                        ins.then_inc(sems["vec_chain"], 1)
                        dve.wait_ge(sems["vec_chain"], L.up())
                r_, k_, v_ = PR[:, 16:20, :], PR[:, 20:24, :], PR[:, 24:28, :]
                w_, aa = GT[:, 0:4, :], GT[:, 4:8, :]
                for c in range(4):
                    v.tensor_scalar(KKH[:, c, :], k_[:, c, :], layer_vec(f"k_k{l}", c), None, ALU.mult).then_inc(sems["vec_chain"], 1)
                    dve.wait_ge(sems["vec_chain"], L.up())
                v.tensor_tensor(flat(HI[:, 0:4, :]), flat(KKH), flat(KKH), ALU.mult).then_inc(sems["kk_sq"], 1)
                l0 = BANK_AT[f"lora{l}"]
                dve.wait_ge(bank_read[l0 % BANKS], filled(l0))
                dve.wait_ge(bank_read[(l0 + 1) % BANKS], filled(l0 + 1))
                dve.wait_ge(bank_read[(l0 + 2) % BANKS], filled(l0 + 2))
                dve.wait_ge(bank_read[(l0 + 3) % BANKS], filled(l0 + 3))
                v.tensor_scalar(flat(w_), flat(w_), -math.exp(-0.5), None, ALU.mult).then_inc(sems["vec_chain"], 1)
                dve.wait_ge(sems["vec_chain"], L.up())
                for m in range(4):
                    for c in range(TT):
                        cs = slice(c * P, (c + 1) * P)
                        v.tensor_tensor_scan(CUM[:, m, cs], C("ones"), w_[:, m, cs], 0.0, ALU.mult, ALU.add).then_inc(sems["vec_chain"], 1)
                        dve.wait_ge(sems["vec_chain"], L.up())
                cum8 = CUM.rearrange("p m (c t) -> p (m c) t", c=TT)
                mid, end = sm[:, CMID:CMID + 8], sm[:, CEND:CEND + 4]
                v.tensor_copy(mid.unsqueeze(2), cum8[:, :, 63:64]).then_inc(sems["vec_chain"], 1)
                dve.wait_ge(sems["vec_chain"], L.up())
                mid2 = mid.rearrange("p (m c) -> p m c", c=TT)
                v.tensor_copy(end.unsqueeze(2), CUM[:, :, P - 1:P]).then_inc(sems["vec_chain"], 1)
                dve.wait_ge(sems["vec_chain"], L.up())
                v.tensor_tensor(end.unsqueeze(2), end.unsqueeze(2), mid2[:, :, 0:1], ALU.subtract).then_inc(sems["vec_chain"], 1)
                dve.wait_ge(sems["vec_chain"], L.up())
                v.tensor_tensor(end.unsqueeze(2), end.unsqueeze(2), mid2[:, :, 1:2], ALU.add).then_inc(sems["vec_chain"], 1)
                dve.wait_ge(sems["vec_chain"], L.up())
                v.tensor_tensor(cum8, cum8, mid.unsqueeze(2).to_broadcast([P, 8, P]), ALU.subtract).then_inc(sems["vec_chain"], 1)
                dve.wait_ge(sems["vec_chain"], L.up())
                v.tensor_tensor(flat(AT_), flat(CUM), flat(w_), ALU.subtract).then_inc(sems["decay_sum"], 1)
                h0 = BANK_AT[f"head_sum{l}"]
                for j in range(2):
                    dve.wait_ge(bank_full[(h0 + j) % BANKS], filled(h0 + j))
                    v.tensor_scalar(flat(HI[:, 2 * j:2 * j + 2, :]), bk(h0 + j)[:, :], 1e-12, None, ALU.max).then_inc(bank_read[(h0 + j) % BANKS], 1)
                dve.wait_ge(sems["kk_sqrt"], L.nxt("kk_sqrt"))
                v.reciprocal(flat(HI[:, 0:4, :]), flat(HI[:, 0:4, :])).then_inc(sems["vec_chain"], 1)
                dve.wait_ge(sems["vec_chain"], L.up())
                v.tensor_tensor(flat(KKH), flat(KKH), flat(HI[:, 0:4, :]), ALU.mult).then_inc(sems["vec_chain"], 1)
                dve.wait_ge(sems["vec_chain"], L.up())
                om = sm[:, OMKA:OMKA + 4]
                v.tensor_scalar(om, V_(f"k_a{l}"), -1.0, 1.0, ALU.mult, ALU.add).then_inc(sems["vec_chain"], 1)
                dve.wait_ge(sems["vec_chain"], L.up())
                for c in range(4):
                    v.tensor_scalar(KT_[:, c, :], aa[:, c, :], layer_vec(f"k_a{l}", c), om[:, c:c + 1], ALU.mult, ALU.add).then_inc(sems["vec_chain"], 1)
                    dve.wait_ge(sems["vec_chain"], L.up())
                v.tensor_tensor(flat(KT_), flat(KT_), flat(k_), ALU.mult).then_inc(sems["vec_chain"], 1)
                dve.wait_ge(sems["vec_chain"], L.up())
                for c in range(4):
                    ins = v.scalar_tensor_tensor(HI[:, c, :], r_[:, c, :], layer_vec(f"r_k{l}", c), KT_[:, c, :], ALU.mult, ALU.mult)
                    if c < 3:
                        ins.then_inc(sems["vec_chain"], 1)
                        dve.wait_ge(sems["vec_chain"], L.up())
                ins.then_inc(sems["rw_bonus"], 1)
                dve.wait_ge(sems["decay_exp"], L.nxt("decay_exp"))
                Q_, QI = R[:, 0:4, :], R[:, 4:8, :]
                v.tensor_tensor(flat(AT_), flat(AT_), flat(KKH), ALU.mult).then_inc(sems["vec_chain"], 1)
                dve.wait_ge(sems["vec_chain"], L.up())
                v.scalar_tensor_tensor(flat(BT_), flat(aa), -1.0, flat(KKH), ALU.mult, ALU.mult).then_inc(sems["vec_chain"], 1)
                dve.wait_ge(sems["vec_chain"], L.up())
                v.tensor_tensor(flat(BT_), flat(BT_), flat(QI), ALU.mult).then_inc(sems["vec_chain"], 1)
                dve.wait_ge(sems["vec_chain"], L.up())
                v.tensor_tensor(flat(KT_), flat(KT_), flat(QI), ALU.mult).then_inc(sems["vec_chain"], 1)
                dve.wait_ge(sems["vec_chain"], L.up())
                v.tensor_tensor(flat(RT_), flat(RT_), flat(Q_), ALU.mult).then_inc(sems["rw_ops"], 1)
                for j in range(2):
                    n = h0 + 2 + j
                    dve.wait_ge(bank_full[n % BANKS], filled(n))
                    v.tensor_tensor(flat(BV[:, 2 * j:2 * j + 2, :]), bk(n)[:, :], flat(v_[:, 2 * j:2 * j + 2, :]), ALU.mult).then_inc(bank_read[n % BANKS], 1)
                dve.wait_ge(bank_read[(h0 + 3) % BANKS], filled(h0 + 3))
                n = BANK_AT[f"rwkv{l}"]
                for c in range(TT):
                    v.tensor_copy(h8(Xm), bcast(C("ident"), 8)).then_inc(sems["vec_chain"], 1)
                    dve.wait_ge(sems["vec_chain"], L.up())
                    v.tensor_copy(h8(XTm), bcast(C("ident"), 8)).then_inc(sems["x_new"], 1)
                    dve.wait_ge(sems["x_new"], L.nxt("x_new"))
                    for q, (dst, mask) in enumerate(((NTm, "before"), (RBm, "upto"), (RKm, "upto"))):
                        for g in range(2):
                            m = n + 2 + 2 * q + g
                            dve.wait_ge(bank_full[m % BANKS], filled(m))
                            v.tensor_tensor(h4(dst[:, g * 512:(g + 1) * 512]), h4(bk(m)[:, :]), bcast(C(mask), 4), ALU.mult).then_inc(bank_read[m % BANKS], 1)
                    n += 8
                    for lev in range(7):
                        for q, dst in enumerate((Xm, XTm)):
                            for g in range(2):
                                m = n + 2 + 2 * q + g
                                dve.wait_ge(bank_full[m % BANKS], filled(m))
                                v.tensor_tensor(dst[:, g * 512:(g + 1) * 512], dst[:, g * 512:(g + 1) * 512], bk(m)[:, :], ALU.add).then_inc(bank_read[m % BANKS], 1)
                        dve.wait_ge(bank_read[(n + 2) % BANKS], filled(n + 2))
                        dve.wait_ge(bank_read[(n + 3) % BANKS], filled(n + 3))
                        dve.wait_ge(bank_read[(n + 4) % BANKS], filled(n + 4))
                        dve.wait_ge(bank_read[(n + 5) % BANKS], filled(n + 5))
                        n += 6
                    n += 2
                    head_norm(n, YC, YSQ, RW_H, 64e-5, "rw_norm")
                    n += 1
                    if c == 0:
                        dve.wait_ge(bank_full[n % BANKS], filled(n))
                        for m in range(4):
                            ins = v.tensor_scalar(S1[:, m * 64:(m + 1) * 64], bk(n)[:, m * 64:(m + 1) * 64],
                                                  sm[:, CEND + m:CEND + m + 1], None, ALU.mult)
                            if m < 3:
                                ins.then_inc(sems["vec_chain"], 1)
                                dve.wait_ge(sems["vec_chain"], L.up())
                        ins.then_inc(bank_read[n % BANKS], 1)
                        n += 1
                    dve.wait_ge(bank_full[n % BANKS], filled(n))
                    cs = slice(c * P, (c + 1) * P)
                    for m in range(4):
                        ins = v.scalar_tensor_tensor(YB[:, 4 + m, cs], bk(n)[:, m * P:(m + 1) * P], layer_vec(f"rw_gn{l}", m),
                                                     BV[:, m, cs], ALU.mult, ALU.add)
                        if m < 3:
                            ins.then_inc(sems["vec_chain"], 1)
                            dve.wait_ge(sems["vec_chain"], L.up())
                    ins.then_inc(bank_read[n % BANKS], 1)
                    dve.wait_ge(bank_read[n % BANKS], filled(n))
                    n += 1
                    ins = v.tensor_tensor(YB[:, 4:8, cs], YB[:, 4:8, cs], GG[:, :, cs], ALU.mult)
                    if c == 0:
                        ins.then_inc(sems["vec_chain"], 1)
                        dve.wait_ge(sems["vec_chain"], L.up())
                ins.then_inc(sems["branch_done"], 1)

                g0, n0 = BANK_AT[f"w_gate{l}"], BANK_AT[f"w_branch{l}"]
                for m in range(g0 + 8, g0 + 12):
                    dve.wait_ge(bank_read[m % BANKS], filled(m))
                for i in range(3):
                    for j in range(4):
                        n = n0 + 4 * i + j
                        g_ = flat(GT[:, 8 * i + 2 * j:8 * i + 2 * j + 2, :])
                        r_ = flat(R[:, 2 * j:2 * j + 2, :])
                        dve.wait_ge(bank_full[n % BANKS], filled(n))
                        if i == 0:
                            v.tensor_tensor(r_, g_, bk(n)[:, :], ALU.mult).then_inc(bank_read[n % BANKS], 1)
                            dve.wait_ge(bank_read[n % BANKS], filled(n))
                            continue
                        v.tensor_tensor(g_, g_, bk(n)[:, :], ALU.mult).then_inc(bank_read[n % BANKS], 1)
                        dve.wait_ge(bank_read[n % BANKS], filled(n))
                        ins = v.tensor_tensor(r_, r_, g_, ALU.add)
                        if i == 2 and j == 3:
                            ins.then_inc(sems["merged"], 1)
                        else:
                            ins.then_inc(sems["vec_chain"], 1)
                            dve.wait_ge(sems["vec_chain"], L.up())
                n0 = BANK_AT[f"w_o{l}"]
                for j in range(4):
                    n = n0 + j
                    dve.wait_ge(bank_full[n % BANKS], filled(n))
                    for h in range(2):
                        m = 2 * j + h
                        ins = v.scalar_tensor_tensor(xT[:, m, :], bk(n)[:, h * S:(h + 1) * S], ml[:, 16 + m:17 + m], xT[:, m, :],
                                                     ALU.mult, ALU.add)
                        if h == 0:
                            ins.then_inc(sems["vec_chain"], 1)
                            dve.wait_ge(sems["vec_chain"], L.up())
                    ins.then_inc(bank_read[n % BANKS], 1)
                dve.wait_ge(bank_read[n0 % BANKS], filled(n0))
                dve.wait_ge(bank_read[(n0 + 1) % BANKS], filled(n0 + 1))
                dve.wait_ge(bank_read[(n0 + 2) % BANKS], filled(n0 + 2))
                dve.wait_ge(bank_read[(n0 + 3) % BANKS], filled(n0 + 3))
                rms_norm(xT[:, :, :], hT[:, :, :], KT, D)

                n = BANK_AT[f"route{l}"]
                t3 = lambda o, w: sm[:, o:o + 2 * w].rearrange("p (t w) -> p t w", t=TT)
                lg = t3(RL, 36)
                dve.wait_ge(bank_full[n % BANKS], filled(n))
                v.tensor_copy(sm[:, RL:RL + 72], bk(n)[:, 0:72]).then_inc(bank_read[n % BANKS], 1)
                dve.wait_ge(bank_read[n % BANKS], filled(n))
                gl, el = lg[:, :, 0:4], lg[:, :, 4:36]
                mx, eq, ex = t3(RT, 1), t3(RT + 2, 4), t3(RT + 10, 4)
                sums_, v0, v1, dv = t3(RT + 18, 1), t3(RT + 20, 1), t3(RT + 22, 1), t3(RT + 24, 1)
                m1, m2, w1, w2 = t3(RT + 26, 1), t3(RT + 28, 1), t3(RT + 30, 1), t3(RT + 32, 1)
                cw, o1, o2 = t3(CW, 32), t3(W2, 32), t3(W3, 32)
                wide = lambda ap, w: ap.to_broadcast([P, TT, w])

                def first_max(src, dst, top, tmp, order, w):
                    v.tensor_reduce(top, src, AX.X, ALU.max).then_inc(sems["vec_chain"], 1)
                    dve.wait_ge(sems["vec_chain"], L.up())
                    v.tensor_tensor(dst, src, wide(top, w), ALU.is_equal).then_inc(sems["vec_chain"], 1)
                    dve.wait_ge(sems["vec_chain"], L.up())
                    v.tensor_tensor(dst, dst, bcast(C(order), TT), ALU.mult).then_inc(sems["vec_chain"], 1)
                    dve.wait_ge(sems["vec_chain"], L.up())
                    v.tensor_reduce(tmp, dst, AX.X, ALU.max).then_inc(sems["vec_chain"], 1)
                    dve.wait_ge(sems["vec_chain"], L.up())
                    v.tensor_tensor(dst, dst, wide(tmp, w), ALU.is_equal).then_inc(sems["vec_chain"], 1)
                    dve.wait_ge(sems["vec_chain"], L.up())

                first_max(gl, eq, mx, m1, "first4", 4)
                v.tensor_tensor(ex, gl, wide(mx, 4), ALU.subtract).then_inc(sems["vec_chain"], 1)
                dve.wait_ge(sems["vec_chain"], L.up())
                v.tensor_scalar(eq, eq, BIG, -BIG, ALU.mult, ALU.add).then_inc(sems["vec_chain"], 1)
                dve.wait_ge(sems["vec_chain"], L.up())
                for tt in range(TT):
                    v.tensor_tensor(el[:, tt, :].rearrange("p (g e) -> p g e", g=4), el[:, tt, :].rearrange("p (g e) -> p g e", g=4),
                                         eq[:, tt, :].unsqueeze(2).to_broadcast([P, 4, 8]), ALU.add).then_inc(sems["vec_chain"], 1)
                    dve.wait_ge(sems["vec_chain"], L.up())
                first_max(el, o1, v0, m1, "first32", 32)
                v.scalar_tensor_tensor(el, o1, -2 * BIG, el, ALU.mult, ALU.add).then_inc(sems["vec_chain"], 1)
                dve.wait_ge(sems["vec_chain"], L.up())
                first_max(el, o2, v1, m2, "first32", 32)
                v.tensor_tensor(dv, v1, v0, ALU.subtract).then_inc(sems["router_max"], 1)
                dve.wait_ge(sems["router_exp"], L.nxt("router_exp"))
                v.tensor_reduce(sums_, ex, AX.X, ALU.add).then_inc(sems["vec_chain"], 1)
                dve.wait_ge(sems["vec_chain"], L.up())
                v.tensor_scalar(w1, dv, 1.0, None, ALU.add).then_inc(sems["vec_chain"], 1)
                dve.wait_ge(sems["vec_chain"], L.up())
                v.tensor_tensor(w1, w1, sums_, ALU.mult).then_inc(sems["vec_chain"], 1)
                dve.wait_ge(sems["vec_chain"], L.up())
                v.reciprocal(w1, w1).then_inc(sems["vec_chain"], 1)
                dve.wait_ge(sems["vec_chain"], L.up())
                v.tensor_tensor(w2, w1, dv, ALU.mult).then_inc(sems["vec_chain"], 1)
                dve.wait_ge(sems["vec_chain"], L.up())
                v.tensor_tensor(sm[:, ASG:ASG + 64], sm[:, W2:W2 + 64], sm[:, W3:W3 + 64], ALU.add).then_inc(sems["assigned"], 1)
                dve.wait_ge(sems["assigned"], L.nxt("assigned"))
                v.tensor_tensor(o1, o1, wide(w1, 32), ALU.mult).then_inc(sems["vec_chain"], 1)
                dve.wait_ge(sems["vec_chain"], L.up())
                v.tensor_tensor(o2, o2, wide(w2, 32), ALU.mult).then_inc(sems["vec_chain"], 1)
                dve.wait_ge(sems["vec_chain"], L.up())
                v.tensor_tensor(cw, o1, o2, ALU.add).then_inc(sems["vec_chain"], 1)
                dve.wait_ge(sems["vec_chain"], L.up())
                dve.wait_ge(bank_full[(n + 1) % BANKS], filled(n + 1))
                v.scalar_tensor_tensor(sm[:, W2:W2 + 64], bk(n + 1)[:, 0:64], 1.0, sm[:, ASG:ASG + 64], ALU.add, ALU.mult).then_inc(
                    bank_read[(n + 1) % BANKS], 1)
                dve.wait_ge(bank_read[(n + 1) % BANKS], filled(n + 1))
                v.tensor_scalar(sm[:, W2:W2 + 64], sm[:, W2:W2 + 64], -1.0, None, ALU.add).then_inc(sems["vec_chain"], 1)
                dve.wait_ge(sems["vec_chain"], L.up())
                v.tensor_scalar(sm[:, W3:W3 + 64], sm[:, W2:W2 + 64], float(CAP), None, ALU.is_ge).then_inc(sems["over_found"], 1)
                dve.wait_ge(sems["over_found"], L.nxt("over_found"))
                dve.wait_ge(bank_full[(n + 2) % BANKS], filled(n + 2))
                v.tensor_reduce(sm[:, RT:RT + 1], bk(n + 2)[:, 0:64], AX.X, ALU.add).then_inc(bank_read[(n + 2) % BANKS], 1)
                dve.wait_ge(bank_read[(n + 2) % BANKS], filled(n + 2))
                v.tensor_copy(flag[:, :], sm[0:1, RT:RT + 1]).then_inc(sems["over_known"], 1)
                dve.wait_ge(sems["over_known"], L.nxt("over_known"))
                v.tensor_tensor(sm[:, W3:W3 + 64], sm[:, W3:W3 + 64], sm[:, CW:CW + 64], ALU.mult).then_inc(sems["router_w"], 1)
                dve.wait_ge(bank_full[(n + 3) % BANKS], filled(n + 3))
                v.tensor_copy(pT[0:N_EXP, 0, :], bk(n + 3)[0:N_EXP, 0:S]).then_inc(bank_read[(n + 3) % BANKS], 1)
                for q in range(4):
                    copy_out(n + 4 + q, HTOK[:, q * 512:(q + 1) * 512])

                def choose(i):
                    e4 = lambda ap: ap.rearrange("p (e c) -> p e c", e=GROUP)
                    for tt in range(TT):
                        place = sm[:, bass.ds(i * GROUP + (W2 + 32 * tt), GROUP)]
                        weight = sm[:, bass.ds(i * GROUP + (CW + 32 * tt), GROUP)]
                        v.tensor_tensor(e4(SEL[:, tt, :]), bcast(C("ramp"), GROUP), place.unsqueeze(2).to_broadcast([P, GROUP, CAP]),
                                        ALU.is_equal).then_inc(sems["moe_gated"], 1)
                        dve.wait_ge(sems["moe_gated"], i * 4 + (g0 + 3 + tt))
                        ins = v.tensor_tensor(e4(SELW[:, tt, :]), e4(SEL[:, tt, :]), weight.unsqueeze(2).to_broadcast([P, GROUP, CAP]),
                                              ALU.mult)
                    ins.then_inc(sems["sel_ready"], 1)

                e0, r0 = N_EXP * l, N_ROUND * l
                g0 = (4 * N_ROUND + 2) * l - 2
                choose(0)
                with nc.vector.Fori(0, N_ROUND) as i:
                    for q in (0, 2):
                        dve.wait_ge(sems["xs_full"], i * 4 + (4 * r0 + q + 1))
                        v.tensor_copy(flat(XS[:, 2 * q:2 * q + 2, :]), bank[0][:, :]).then_inc(sems["xs_read_v"], 1)

                    def gated(pr):
                        dve.wait_ge(sems["moe_sig"], i * 2 + (2 * r0 + pr + 1))
                        if pr:
                            dve.wait_ge(sems["ht_full"], i * 2 + (2 * r0 + 1))
                        v.tensor_tensor(SG, SG, bank[0][:, :], ALU.mult).then_inc(sems["moe_gated"], 1)
                        dve.wait_ge(sems["moe_gated"], i * 4 + (g0 + 4 + pr + 1))
                        v.tensor_tensor(SG, SG, bank[1][:, :], ALU.mult).then_inc(sems["gu_read"], 1)

                    def outputs(pr):
                        dve.wait_ge(sems["y_full"], i * GROUP + (e0 + 2 * pr + 2))
                        v.tensor_copy(YE[:, 0:512], bank[2][:, :]).then_inc(sems["y_read_v"], 1)

                    gated(0)
                    outputs(0)
                    gated(1)
                    dve.wait_ge(sems["xs_full"], i * 4 + (4 * r0 + 4))
                    dve.wait_ge(sems["swt_full"], i + (r0 + 1))
                    choose(i + 1)
                    outputs(1)

                with nc.vector.If(nc.vector.value_load(flag[0:1, 0:1], min_val=0, max_val=2 * S) > 0):
                    F_ = spill[l]
                    dve.wait_ge(F_["spill_cw"], 16)
                    with nc.vector.Fori(0, N_EXP) as e:
                        for f in range(4):
                            dve.wait_ge(F_["spill_sig"], e * 4 + (f + 1))
                            v.tensor_tensor(SQ[:, f, :], SQ[:, f, :], bank[f][:, 0:S], ALU.mult).then_inc(F_["spill_gated"], 1)
                            dve.wait_ge(F_["spill_gated"], e * 4 + (f + 1))
                            v.tensor_tensor(SQ[:, f, :], SQ[:, f, :], bank[f][:, S:2 * S], ALU.mult).then_inc(F_[f"spill_read{f}"], 1)
                            dve.wait_ge(F_[f"spill_read{f}"], e + 1)
                            v.tensor_tensor(FF[:, f, :], SQ[:, f, :], PR[:, bass.ds(e, 1), :].rearrange("p o s -> p (o s)"),
                                            ALU.mult).then_inc(F_["spill_h"], 1)
                    dve.wait_ge(F_["spill_down"], N_EXP)
                dve.wait_ge(sems["scattered"], (e0 + N_EXP) // 2)
                for m in range(KT):
                    ins = v.scalar_tensor_tensor(xT[:, m, :], acc[m // 2][:, (m % 2) * S:(m % 2 + 1) * S], ml[:, 40 + m:41 + m],
                                                 xT[:, m, :], ALU.mult, ALU.add)
                    if m < KT - 1:
                        ins.then_inc(sems["vec_chain"], 1)
                        dve.wait_ge(sems["vec_chain"], L.up())
                ins.then_inc(sems["x_new_layer"], 1)
                dve.wait_ge(sems["x_new_layer"], L.nxt("x_new_layer"))
            rms_norm(xT[:, :, :], hT[:, :, :], KT, D)
            Rtok = R[:].rearrange("p (t k) s -> p t (k s)", t=TT)
            for j in range(4):
                copy_out(BANK_AT["x_out"] + j, Rtok[:, j // 2, (j % 2) * 512:(j % 2 + 1) * 512])

        @block.scalar
        def _(act):
            L = Count()
            f = nc.scalar.activation

            def copy_out(n, dst, src=None):
                act.wait_ge(bank_full[n % BANKS], filled(n))
                f(dst, bk(n)[:, :] if src is None else src, ACT.Copy).then_inc(bank_read[n % BANKS], 1)

            def finish_norm(dst, K, gain, bias, layer=None):
                act.wait_ge(sems["norm_var"], L.nxt("norm_var"))
                f(stat[:, 1, :], stat[:, 1, :], ACT.Sqrt).then_inc(sems["norm_std"], 1)
                act.wait_ge(sems["norm_scaled"], L.nxt("norm_scaled"))
                src = R if layer else dst
                for k in range(K):
                    b = 0.0 if bias is None else bias[:, k:k + 1]
                    ins = f(dst[:, k, :], src[:, k, :], ACT.Identity, bias=b, scale=gain[:, k:k + 1])
                ins.then_inc(sems["norm_out"], 1)

            def layer_norm(dst, g, b):
                act.wait_ge(sems["norm_centered"], L.nxt("norm_centered"))
                f(flat(SQ[:, :, :]), flat(R[:, :, :]), ACT.Square).then_inc(sems["norm_sq"], 1)
                finish_norm(dst, KT, V_(g), V_(b), True)

            def rms_norm(src, dst, gain, bias, K=KT, k0=0):
                f(flat(SQ[:, k0:k0 + K, :]), flat(src), ACT.Square).then_inc(sems["norm_sq"], 1)
                finish_norm(dst, K, gain, bias)

            act.wait_ge(sems["lam_abs"], L.nxt("lam_abs"))
            lam = sm[:, LAM:LAM + 4]
            f(lam, lam, ACT.Exp).then_inc(sems["act_chain"], 1)
            act.wait_ge(sems["act_chain"], L.up())
            f(lam, lam, ACT.Ln, bias=1.0).then_inc(sems["lam_log"], 1)
            f(sm[:, CS:CS + 8], V_("c"), ACT.Sigmoid).then_inc(sems["c_sig"], 1)
            n0 = BANK_AT["hy_in"]
            for j in range(1, 8, 2):
                copy_out(n0 + j, flat(PR[:, 2 * j:2 * j + 2, :]))
            z = flat(R[:, 0:4, :])
            act.wait_ge(sems["gelu_in"], L.nxt("gelu_in"))
            f(z, z, ACT.Sigmoid, scale=2 * math.sqrt(2 / math.pi)).then_inc(sems["gelu_sig"], 1)
            g0 = BANK_AT["rg_gates"]
            for g, (dst, b) in enumerate(((RG, "ga_b"), (IG, "gx_b"))):
                for j in range(2):
                    n = g0 + 2 * g + j
                    act.wait_ge(bank_full[n % BANKS], filled(n))
                    for h in range(2):
                        ins = f(PR[:, dst + 2 * j + h, :], bk(n)[:, h * S:(h + 1) * S], ACT.Sigmoid,
                                bias=V_(b)[:, 2 * j + h:2 * j + h + 1])
                    ins.then_inc(bank_read[n % BANKS], 1)
            th = flat(PR[:, RG:RG + 4, :])
            act.wait_ge(sems["decay_in"], L.nxt("decay_in"))
            f(th, th, ACT.Tanh).then_inc(sems["decay_tanh"], 1)
            i0 = BANK_AT["idx"]
            for q in range(4):
                act.wait_ge(bank_full[(i0 + q) % BANKS], filled(i0 + q))
                f(flat(RELU[:, 2 * q:2 * q + 2, :]), bk(i0 + q)[:, :], ACT.Relu).then_inc(bank_read[(i0 + q) % BANKS], 1)
            act.wait_ge(sems["decay_den"], L.nxt("decay_den"))
            f(th, th, ACT.Sqrt).then_inc(sems["decay_sqrt"], 1)

            def attention(name, pairs, scale):
                order = attention_order(BANK_AT[name], pairs)
                for hp in range(pairs + 1):
                    if hp < pairs:
                        q = 4 * (hp % 2)
                        act.wait_ge(sems["dsa_max"], L.nxt("dsa_max"))
                        for j in range(4):
                            ins = f(LG[:, q + j, :], LG[:, q + j, :], ACT.Exp, bias=sm[:, NB + q + j:NB + q + j + 1],
                                    scale=scale, accum_out=sm[:, RS + q + j:RS + q + j + 1])
                        ins.then_inc(sems["dsa_exp"], 1)
                    if hp:
                        for h in range(2):
                            copy_out(order["t", hp - 1, h], flat(PTB[:, 2 * h:2 * h + 2, :]))

            def ffn_and_ple(l):
                layer_norm(hT, f"ln1_g{l}", f"ln1_b{l}")
                copy_out(BANK_AT[f"p_in{l}"], flat(pT[:, :, :]))
                n0 = BANK_AT[f"mlp{l}"]
                with nc.scalar.Fori(0, 4) as i:
                    for q in range(4):
                        n = n0 + q
                        tile_ = flat(FF[:, 2 * q:2 * q + 2, :])
                        act.wait_ge(bank_full[n % BANKS], filled(n, i))
                        f(tile_, bk(n)[:, :], ACT.Relu).then_inc(bank_read[n % BANKS], 1)
                        act.wait_ge(bank_read[n % BANKS], i + (n // BANKS + 1))
                        f(tile_, tile_, ACT.Square).then_inc(sems["ff_act"], 1)
                for j in range(4):
                    n = BANK_AT[f"ple_gate{l}"] + j
                    act.wait_ge(bank_full[n % BANKS], filled(n))
                    f(flat(SQ[:, 2 * j:2 * j + 2, :]), bk(n)[:, :], ACT.Sigmoid).then_inc(bank_read[n % BANKS], 1)
                layer_norm(xT, f"ln2_g{l}", f"ln2_b{l}")

            attention("dsa", 4, DSA_D ** -0.5)
            ffn_and_ple(0)

            n0 = BANK_AT["mla_down"]
            act.wait_ge(bank_read[n0 % BANKS], filled(n0))
            act.wait_ge(bank_read[(n0 + 1) % BANKS], filled(n0 + 1))
            rms_norm(CQ[:, 0:4, :], CQ[:, 0:4, :], V_("q_norm"), None, 4)
            act.wait_ge(bank_read[(n0 + 2) % BANKS], filled(n0 + 2))
            rms_norm(CQ[:, 4:6, :], CQ[:, 4:6, :], V_("kv_norm"), None, 2, 4)
            for j in range(1, 8, 2):
                n = BANK_AT["mla_uq"] + j
                act.wait_ge(bank_full[n % BANKS], filled(n))
                f(flat(QH[0:96, 2 * j:2 * j + 2, :]), bk(n)[0:96, :], ACT.Copy).then_inc(bank_read[n % BANKS], 1)
            act.wait_ge(sems["kr_rope"], L.nxt("kr_rope"))
            f(KH[64:96, :, :], KROT[64:96, :].unsqueeze(1).to_broadcast([32, MLA_H, S]), ACT.Copy).then_inc(sems["kr_spread"], 1)
            for j in range(8):
                n = BANK_AT["mla_k"] + j
                act.wait_ge(bank_full[n % BANKS], filled(n))
                f(flat(KH[0:64, 2 * j:2 * j + 2, :]), bk(n)[0:64, :], ACT.Copy).then_inc(bank_read[n % BANKS], 1)
            for q in range(4):
                copy_out(BANK_AT["mla_v"] + q, flat(VH)[:, q * 512:(q + 1) * 512])
            attention("mla", 8, (NOPE + ROPE) ** -0.5)
            ffn_and_ple(1)

            for t_ in (sinT, cosT):
                act.wait_ge(sems["rot_in"], L.nxt("rot_in"))
                f(t_[:, :], t_[:, :], ACT.Sin).then_inc(sems["rot_tables"], 1)
            for l in range(DEPTH):
                m0 = 48 * l
                act.wait_ge(sems["norm_out" if l == 0 else "x_new_layer"], L.nxt("norm_out" if l == 0 else "x_new_layer"))
                f(flat(SQ[:, :, :]), flat(xT[:, :, :]), ACT.Square).then_inc(sems["norm_sq"], 1)
                act.wait_ge(sems["mod_done"], L.nxt("mod_done"))
                finish_norm(hT, KT, sm[:, GA1:GA1 + 8], mod[:, m0:m0 + 8])
                n0 = BANK_AT[f"w_in{l}"]
                with nc.scalar.Fori(0, 5) as i:
                    for j in (1, 3):
                        act.wait_ge(bank_full[(n0 + j) % BANKS], filled(n0 + j, i))
                        f(PR[:, bass.ds(i * 8 + 2 * j, 2), :], two(bk(n0 + j)[:, :]), ACT.Copy).then_inc(bank_read[(n0 + j) % BANKS], 1)
                for m in range(n0 + 16, n0 + 20):
                    act.wait_ge(bank_read[m % BANKS], filled(m))
                f(flat(GT[:, 0:4, :]), flat(PR[:, 12:16, :]), ACT.Sigmoid).then_inc(sems["g_sig"], 1)
                n0 = BANK_AT[f"ret_t{l}"]
                VT = flat(GT[:, 4:8, :])
                for c in range(TT):
                    copy_out(n0 + c, VT[:, c * 512:(c + 1) * 512])

                def head_sqrt(H):
                    act.wait_ge(sems["head_var"], L.nxt("head_var"))
                    f(sm[:, HV:HV + H], sm[:, HV:HV + H], ACT.Sqrt).then_inc(sems["head_std"], 1)

                head_sqrt(RET_H)
                head_sqrt(RET_H)
                act.wait_ge(sems["mixed"], L.nxt("mixed"))
                f(PR[0:64, 28, :], PR[0:64, 28, :], ACT.Tanh).then_inc(sems["lora_in"], 1)
                f(PR[:, 29, :], PR[:, 29, :], ACT.Sigmoid).then_inc(sems["lora_in"], 1)
                l0 = BANK_AT[f"lora{l}"]
                for g, b in enumerate(("w0", "a0")):
                    for j in range(2):
                        n = l0 + 2 * g + j
                        act.wait_ge(bank_full[n % BANKS], filled(n))
                        for h in range(2):
                            m = 2 * j + h
                            ins = f(GT[:, 4 * g + m, :], bk(n)[:, h * S:(h + 1) * S], ACT.Sigmoid, bias=V_(f"{b}{l}")[:, m:m + 1])
                        ins.then_inc(bank_read[n % BANKS], 1)
                for j in range(2):
                    copy_out(l0 + 4 + j, flat(GG[:, 2 * j:2 * j + 2, :]))
                act.wait_ge(sems["decay_sum"], L.nxt("decay_sum"))
                f(flat(R[:, 0:4, :]), flat(CUM), ACT.Exp)
                f(flat(R[:, 4:8, :]), flat(CUM), ACT.Exp, scale=-1.0)
                f(sm[:, CEND:CEND + 4], sm[:, CEND:CEND + 4], ACT.Exp)
                f(flat(AT_), flat(AT_), ACT.Exp).then_inc(sems["decay_exp"], 1)
                h0 = BANK_AT[f"head_sum{l}"]
                act.wait_ge(bank_read[h0 % BANKS], filled(h0))
                act.wait_ge(bank_read[(h0 + 1) % BANKS], filled(h0 + 1))
                f(flat(HI[:, 0:4, :]), flat(HI[:, 0:4, :]), ACT.Sqrt).then_inc(sems["kk_sqrt"], 1)
                n0 = BANK_AT[f"rw_t{l}"]
                for q, dst in enumerate((VT2[:, 0:512], VT2[:, 512:1024], BT0, KT0)):
                    copy_out(n0 + q, dst)
                n = BANK_AT[f"rwkv{l}"]
                for c in range(TT):
                    for g in range(2):
                        copy_out(n + g, MTraw[:, g * 512:(g + 1) * 512])
                    n += 8
                    for lev in range(7):
                        for g in range(2):
                            copy_out(n + g, Tm[:, g * 512:(g + 1) * 512])
                        n += 6
                    copy_out(n, Zm)
                    copy_out(n + 1, Um)
                    head_sqrt(RW_H)
                    n += 5 if c == 0 else 4
                act.wait_ge(sems["branch_done"], L.nxt("branch_done"))
                n0 = BANK_AT[f"w_gate{l}"]
                o = VEC_AT[f"b_gate{l}"][0]
                with nc.scalar.Fori(0, 3) as i:
                    for j in range(4):
                        n = n0 + j
                        act.wait_ge(bank_full[n % BANKS], filled(n, i))
                        for h in range(2):
                            m = 2 * j + h
                            ins = f(GT[:, bass.ds(i * 8 + m, 1), :].rearrange("p o s -> p (o s)"), bk(n)[:, h * S:(h + 1) * S],
                                    ACT.Sigmoid, bias=vec[:, bass.ds(i * 8 + (o + m), 1)])
                        ins.then_inc(bank_read[n % BANKS], 1)
                n0 = BANK_AT[f"w_o{l}"]
                for m in range(n0, n0 + 4):
                    act.wait_ge(bank_read[m % BANKS], filled(m))
                f(flat(SQ[:, :, :]), flat(xT[:, :, :]), ACT.Square).then_inc(sems["norm_sq"], 1)
                finish_norm(hT, KT, sm[:, GA2:GA2 + 8], mod[:, m0 + 24:m0 + 32])
                act.wait_ge(sems["router_max"], L.nxt("router_max"))
                ex, dv = sm[:, RT + 10:RT + 18], sm[:, RT + 24:RT + 26]
                f(ex, ex, ACT.Exp)
                f(dv, dv, ACT.Exp).then_inc(sems["router_exp"], 1)
                e0, r0 = N_EXP * l, N_ROUND * l
                with nc.scalar.Fori(0, N_ROUND) as i:
                    for q in (1, 3):
                        act.wait_ge(sems["xs_full"], i * 4 + (4 * r0 + q + 1))
                        f(flat(XS[:, 2 * q:2 * q + 2, :]), bank[1][:, :], ACT.Copy).then_inc(sems["xs_read_a"], 1)
                    act.wait_ge(sems["swt_full"], i + (r0 + 1))
                    f(flat(SWT), bank[2][:, :], ACT.Copy).then_inc(sems["swt_read"], 1)

                    def gate_sigmoid(pr):
                        act.wait_ge(sems["gu_full"], i * GROUP + (e0 + 2 * pr + 2))
                        if pr:
                            act.wait_ge(sems["ht_full"], i * 2 + (2 * r0 + 1))
                        f(SG, bank[0][:, :], ACT.Sigmoid).then_inc(sems["moe_sig"], 1)

                    def hidden(pr):
                        act.wait_ge(sems["ht_full"], i * 2 + (2 * r0 + pr + 1))
                        f(HE, bank[2][:, :], ACT.Copy).then_inc(sems["ht_read"], 1)

                    def outputs(pr):
                        act.wait_ge(sems["y_full"], i * GROUP + (e0 + 2 * pr + 2))
                        f(YE[:, 512:1024], bank[3][:, :], ACT.Copy).then_inc(sems["y_read_a"], 1)

                    gate_sigmoid(0)
                    hidden(0)
                    outputs(0)
                    gate_sigmoid(1)
                    hidden(1)
                    outputs(1)
                act.wait_ge(sems["over_known"], L.nxt("over_known"))
                with nc.scalar.If(nc.scalar.value_load(flag[0:1, 0:1], min_val=0, max_val=2 * S) > 0):
                    F_ = spill[l]
                    with nc.scalar.Fori(0, N_EXP) as e:
                        for q in range(4):
                            act.wait_ge(F_[f"spill_full{q}"], e + 1)
                            f(SQ[:, q, :], bank[q][:, 0:S], ACT.Sigmoid).then_inc(F_["spill_sig"], 1)
            act.wait_ge(sems["x_new_layer"], L.nxt("x_new_layer"))
            rms_norm(xT[:, :, :], hT, V_("final_g"), None)

        @block.gpsimd
        def _(pool):
            L = Count()
            for l in range(DEPTH):
                n = BANK_AT[f"rwkv{l}"]
                masked = [None, None]
                for c in range(TT):
                    pool.wait_ge(bank_read[n % BANKS], filled(n))
                    pool.wait_ge(bank_read[(n + 1) % BANKS], filled(n + 1))
                    n += 8
                    for lev in range(7):
                        b = lev % 2
                        if masked[b] is not None:
                            pool.wait_ge(bank_full[(masked[b]) % BANKS], filled(masked[b]))
                        elif c == 0:
                            if lev == 0:
                                pool.wait_ge(sems["rw_ops"], L.nxt("rw_ops"))
                        mask = C("levels")[:, lev * P:(lev + 1) * P]
                        nc.gpsimd.tensor_tensor(h8(MMs[b]), h8(MTraw), bcast(mask, 8), ALU.mult).then_inc(sems["mm_mask"], 1)
                        masked[b] = n + 1
                        n += 6
                    n += 5 if c == 0 else 4
                pool.wait_ge(sems["over_known"], L.nxt("over_known"))
                pool.wait_ge(bank_read[(BANK_AT[f"route{l}"] + 3) % BANKS], filled(BANK_AT[f"route{l}"] + 3))
                with nc.gpsimd.If(nc.gpsimd.value_load(flag[0:1, 0:1], min_val=0, max_val=2 * S) > 0):
                    nc.gpsimd.dma_start(cw_dram[l], pT[0:N_EXP, 0, :]).then_inc(spill[l]["spill_stored"], 16)
                    pool.wait_ge(spill[l]["spill_stored"], 16)
                    pool.wait_ge(sems["scattered"], N_EXP * (l + 1) // 2)
                    nc.gpsimd.dma_start(PR[:, 0:N_EXP, :].rearrange("p e s -> p (e s)"),
                                        cw_dram[l:l + 1].rearrange("o e s -> o (e s)").to_broadcast([P, N_EXP * S])).then_inc(
                        spill[l]["spill_cw"], 16)


_RAW = ["x", "p", "mlp_w1", "mlp_w2", "ple_w_proj", "ple_w_gate", "hy_w_in", "hy_w_out", "mla_w_down", "mla_w_uq",
        "mla_w_ukv", "mla_w_out", "positions_2", "w_ada_2", "w_in_2", "w_gate_2", "rwkv_w_lora_2", "rwkv_a_lora_2",
        "rwkv_g_lora_2", "w_branch_2", "w_o_2", "w_router_group_2", "b_router_group_2", "w_router_expert_2",
        "b_router_expert_2", "w_exp_gate_2", "w_exp_up_2", "w_exp_down_2"]


def lay_out(inputs):
    arrays = {n: np.ascontiguousarray(inputs[n]) for n in _RAW}
    cols = []
    for _, tiles, name, at in VECTORS:
        v = inputs[name] if at is None else inputs[name][at]
        cols.append(np.asarray(v).reshape(tiles, P).T)
    arrays["vectors"] = np.ascontiguousarray(np.concatenate(cols, 1))
    blocks = np.zeros((P, 2, 4, P), np.float32)
    for g, name in enumerate(("hy_ga_w", "hy_gx_w")):
        w = np.asarray(inputs[name][0])
        for c in range(4):
            for h in range(2):
                blocks[64 * h:64 * h + 64, g, c, 64 * h:64 * h + 64] = w[2 * c + h]
    arrays["gate_blocks"] = blocks.reshape(P, 1024)
    arrays["const"] = CONST
    return arrays


def program(nc, shapes):
    a = {n: nc.dram_tensor(f"in_{n}", s, mybir.dt.from_np(d), kind="ExternalInput").ap() for n, (s, d) in shapes.items()}
    out = nc.dram_tensor("out_0", (1, S, D), F32, kind="ExternalOutput").ap()
    build(nc, a, out)


def kernel(**inputs):
    import concourse.bacc as bacc
    from concourse.bass_utils import run_bass_kernel_spmd
    arrays = lay_out(inputs)
    nc = bacc.Bacc("TRN2", target_bir_lowering=False, num_devices=1)
    program(nc, {n: (v.shape, v.dtype) for n, v in arrays.items()})
    r = run_bass_kernel_spmd(nc, [{f"in_{n}": v for n, v in arrays.items()}], core_ids=[0])
    return r.results[0]["out_0"]
```
